# Optimizing a Trainium2 kernel written in Bass

```python
import math
import jax, jax.numpy as jnp
from jax import lax
import numpy as np

D_MODEL = 1024
BATCH = 1
SEQ = 1024
DEPTH = 2

GRID_W = 64
N_META = 16
EPS = 1e-6
ATTN_HEADS = 8
ATTN_KV_HEADS = 2
HEAD_DIM = 128
KV_REP = ATTN_HEADS // ATTN_KV_HEADS
ROPE_AXIS_DIM = HEAD_DIM // 2
ROPE_THETA = 10000.0
Q_BLOCK = 128
ATTN_WIDTH = ATTN_HEADS * HEAD_DIM
KV_WIDTH = ATTN_KV_HEADS * HEAD_DIM
S5_WIDTH = D_MODEL
S5_GROUP = 16
S5_GROUPS = S5_WIDTH // S5_GROUP
S5_STATE = 64
EVEN_IN_WIDTH = 2 * ATTN_WIDTH + 2 * KV_WIDTH + 2 * S5_WIDTH
EVEN_SPLITS = (ATTN_WIDTH, ATTN_WIDTH + KV_WIDTH, ATTN_WIDTH + 2 * KV_WIDTH,
               2 * ATTN_WIDTH + 2 * KV_WIDTH, 2 * ATTN_WIDTH + 2 * KV_WIDTH + S5_WIDTH)
MLSTM_WIDTH = 2 * D_MODEL
MLSTM_HEADS = 8
MLSTM_HEAD_V = MLSTM_WIDTH // MLSTM_HEADS
MLSTM_HEAD_QK = MLSTM_HEAD_V // 2
CONV_W = 5
CHUNK = 64
PAD_FRONT = CHUNK - N_META
NEG_BIG = -1e9
N_EVEN = (DEPTH + 1) // 2
N_ODD = DEPTH // 2

kernel_name = 'hybrid_attn_s5_mlstm_encoder'

def rms_norm(x, g):
    xf = x.astype(jnp.float32)
    y = xf * lax.rsqrt(jnp.mean(xf * xf, axis=-1, keepdims=True) + EPS)
    return (y * g.astype(jnp.float32)).astype(x.dtype)

def axial_rope_tables(n_real):
    rows = n_real // GRID_W
    row = jnp.repeat(jnp.arange(rows, dtype=jnp.float32), GRID_W)
    col = jnp.tile(jnp.arange(GRID_W, dtype=jnp.float32), rows)
    meta = jnp.zeros((N_META,), jnp.float32)
    row = jnp.concatenate([meta, row])
    col = jnp.concatenate([meta, col])
    freqs = ROPE_THETA ** (-jnp.arange(0, ROPE_AXIS_DIM, 2, dtype=jnp.float32) / ROPE_AXIS_DIM)
    ang_r = row[:, None] * freqs[None]
    ang_c = col[:, None] * freqs[None]
    shp = lambda a: a[None, :, None, :]
    return shp(jnp.cos(ang_r)), shp(jnp.sin(ang_r)), shp(jnp.cos(ang_c)), shp(jnp.sin(ang_c))

def apply_axial_rope(x, tabs):
    cos_r, sin_r, cos_c, sin_c = tabs
    xf = x.astype(jnp.float32)

    def rot(xs, cos, sin):
        half = xs.shape[-1] // 2
        x1, x2 = xs[..., :half], xs[..., half:]
        return jnp.concatenate([x1 * cos - x2 * sin, x2 * cos + x1 * sin], axis=-1)

    out = jnp.concatenate([rot(xf[..., :ROPE_AXIS_DIM], cos_r, sin_r),
                           rot(xf[..., ROPE_AXIS_DIM:], cos_c, sin_c)], axis=-1)
    return out.astype(x.dtype)

def block_attention(q, k, v):
    b, l = q.shape[0], q.shape[1]
    n_blocks = -(-l // Q_BLOCK)
    pad = n_blocks * Q_BLOCK - l
    qp = jnp.pad(q, ((0, 0), (0, pad), (0, 0), (0, 0)))
    qb = qp.reshape(b, n_blocks, Q_BLOCK, ATTN_KV_HEADS, KV_REP, HEAD_DIM).transpose(1, 0, 3, 4, 2, 5)
    kt = k.transpose(0, 2, 1, 3)
    vt = v.transpose(0, 2, 1, 3)
    scale = HEAD_DIM ** -0.5

    def one_block(qblk):
        s = jnp.einsum('bgrqd,bgkd->bgrqk', qblk, kt).astype(jnp.float32) * scale
        p = jax.nn.softmax(s, axis=-1).astype(vt.dtype)
        return jnp.einsum('bgrqk,bgkd->bgrqd', p, vt)

    o = lax.map(one_block, qb)
    o = o.transpose(1, 0, 4, 2, 3, 5).reshape(b, n_blocks * Q_BLOCK, ATTN_WIDTH)
    return o[:, :l]

def _linear_combine(e1, e2):
    a1, b1 = e1
    a2, b2 = e2
    return a1 * a2, a2 * b1 + b2

def s5_bidirectional(u, a_re, a_im, log_dt, b_re, b_im, c_re, c_im, d_skip, w_glu, b_glu):
    bsz, l, _ = u.shape
    f32 = jnp.float32
    uf = u.astype(f32)
    ug = uf.reshape(bsz, l, S5_GROUPS, S5_GROUP)
    y = uf * d_skip.astype(f32)
    for direction, reverse in ((0, False), (1, True)):
        a = lax.complex(a_re[direction].astype(f32), a_im[direction].astype(f32))
        dt = jnp.exp(log_dt[direction].astype(f32))[:, None]
        a_bar = jnp.exp(a * dt)
        b_bar = ((a_bar - 1.0) / a)[..., None] * lax.complex(b_re[direction].astype(f32),
                                                           b_im[direction].astype(f32))
        bu = jnp.einsum('blgp,gnp->blgn', ug.astype(jnp.complex64), b_bar)
        a_seq = jnp.broadcast_to(a_bar, bu.shape)
        _, states = lax.associative_scan(_linear_combine, (a_seq, bu), axis=1, reverse=reverse)
        c = lax.complex(c_re[direction].astype(f32), c_im[direction].astype(f32))
        y = y + jnp.einsum('blgn,gpn->blgp', states, c).real.reshape(bsz, l, S5_WIDTH)
    y = jax.nn.gelu(y)
    y = y * jax.nn.sigmoid(y @ w_glu.astype(f32) + b_glu.astype(f32))
    return y.astype(u.dtype)

def mlstm_chunkwise(q, k, v, log_i, log_f):
    bsz, nh, t, dk = q.shape
    dv = v.shape[-1]
    nc = t // CHUNK
    q = q.reshape(bsz, nh, nc, CHUNK, dk) * (dk ** -0.5)
    k = k.reshape(bsz, nh, nc, CHUNK, dk)
    v = v.reshape(bsz, nh, nc, CHUNK, dv)
    li = log_i.reshape(bsz, nh, nc, CHUNK)
    lf = log_f.reshape(bsz, nh, nc, CHUNK)
    b = jnp.cumsum(lf, axis=-1)
    b_last = b[..., -1]
    g = b_last[..., None] - b + li
    g_max = jnp.max(g, axis=-1)

    def step(carry, xs):
        c_st, n_st, m_st = carry
        k_c, v_c, g_c, gmax_c, bl_c = xs
        m_new = jnp.maximum(bl_c + m_st, gmax_c)
        decay = jnp.exp(bl_c + m_st - m_new)
        w = jnp.exp(g_c - m_new[..., None])
        c_new = decay[..., None, None] * c_st + jnp.einsum('bhs,bhsv,bhsk->bhvk', w, v_c, k_c)
        n_new = decay[..., None] * n_st + jnp.einsum('bhs,bhsk->bhk', w, k_c)
        return (c_new, n_new, m_new), (c_st, n_st, m_st)

    init = (jnp.zeros((bsz, nh, dv, dk), jnp.float32), jnp.zeros((bsz, nh, dk), jnp.float32),
            jnp.zeros((bsz, nh), jnp.float32))
    xs = (jnp.moveaxis(k, 2, 0), jnp.moveaxis(v, 2, 0), jnp.moveaxis(g, 2, 0),
          jnp.moveaxis(g_max, 2, 0), jnp.moveaxis(b_last, 2, 0))
    _, (c_prev, n_prev, m_prev) = lax.scan(step, init, xs)
    m_prev = jnp.moveaxis(m_prev, 0, 2)

    d = b[..., :, None] - b[..., None, :] + li[..., None, :]
    causal_in_chunk = jnp.tril(jnp.ones((CHUNK, CHUNK), dtype=bool))
    d = jnp.where(causal_in_chunk, d, -jnp.inf)
    inter_log = b + m_prev[..., None]
    m_t = jnp.maximum(jnp.max(d, axis=-1), inter_log)
    sw = jnp.exp(d - m_t[..., None]) * jnp.einsum('bhntd,bhnsd->bhnts', q, k)
    inter_scale = jnp.exp(inter_log - m_t)
    num = jnp.einsum('bhnts,bhnsv->bhntv', sw, v) + \
        inter_scale[..., None] * jnp.einsum('nbhvk,bhntk->bhntv', c_prev, q)
    den = jnp.sum(sw, axis=-1) + inter_scale * jnp.einsum('nbhk,bhntk->bhnt', n_prev, q)
    h = num / jnp.maximum(jnp.abs(den), jnp.exp(-m_t))[..., None]
    return h.reshape(bsz, nh, t, dv)

def attn_s5_layer(h, tabs, w_in, q_norm, k_norm, a_re, a_im, log_dt, b_re, b_im, c_re, c_im,
                  d_skip, w_glu, b_glu, w_out):
    bsz, l, _ = h.shape
    proj = h @ w_in
    q, k, v, gate_a, u, gate_b = jnp.split(proj, EVEN_SPLITS, axis=-1)
    q = apply_axial_rope(rms_norm(q.reshape(bsz, l, ATTN_HEADS, HEAD_DIM), q_norm), tabs)
    k = apply_axial_rope(rms_norm(k.reshape(bsz, l, ATTN_KV_HEADS, HEAD_DIM), k_norm), tabs)
    v = v.reshape(bsz, l, ATTN_KV_HEADS, HEAD_DIM)
    y_a = block_attention(q, k, v) * jax.nn.silu(gate_a)
    y_b = s5_bidirectional(u, a_re, a_im, log_dt, b_re, b_im, c_re, c_im, d_skip, w_glu, b_glu) \
        * jax.nn.silu(gate_b)
    return jnp.concatenate([y_a, y_b], axis=-1) @ w_out

def mlstm_layer(h, w_in, conv_w, conv_b, w_q, w_k, w_v, w_igate, b_igate, w_fgate, b_fgate,
                w_ogate, b_ogate, head_norm, skip, w_out):
    bsz, l, _ = h.shape
    f32 = jnp.float32
    proj = h @ w_in
    xm, z = jnp.split(proj, [MLSTM_WIDTH], axis=-1)
    conv = lax.conv_general_dilated(xm, conv_w[:, None, :].astype(xm.dtype), window_strides=(1,),
                                    padding=[(CONV_W // 2, CONV_W // 2)],
                                    dimension_numbers=('NWC', 'WIO', 'NWC'),
                                    feature_group_count=MLSTM_WIDTH)
    xc = jax.nn.silu(conv + conv_b)
    xch = xc.reshape(bsz, l, MLSTM_HEADS, MLSTM_HEAD_V)
    q = jnp.einsum('blhc,hcd->bhld', xch, w_q).astype(f32)
    k = jnp.einsum('blhc,hcd->bhld', xch, w_k).astype(f32)
    v = jnp.einsum('blhc,hcd->bhld', xm.reshape(bsz, l, MLSTM_HEADS, MLSTM_HEAD_V), w_v).astype(f32)
    li = (jnp.einsum('blc,dch->dbhl', xc, w_igate) + b_igate[:, None, :, None]).astype(f32)
    lf = jax.nn.log_sigmoid((jnp.einsum('blc,dch->dbhl', xc, w_fgate)
                             + b_fgate[:, None, :, None]).astype(f32))
    pad4 = ((0, 0), (0, 0), (PAD_FRONT, 0), (0, 0))
    pad3 = ((0, 0), (0, 0), (PAD_FRONT, 0))
    q, k, v = jnp.pad(q, pad4), jnp.pad(k, pad4), jnp.pad(v, pad4)
    li_f, li_b = jnp.pad(li[0], pad3, constant_values=NEG_BIG), jnp.pad(li[1], pad3, constant_values=NEG_BIG)
    lf_f, lf_b = jnp.pad(lf[0], pad3), jnp.pad(lf[1], pad3)
    flip = lambda a: jnp.flip(a, axis=2)
    h_f = mlstm_chunkwise(q, k, v, li_f, lf_f)
    h_b = flip(mlstm_chunkwise(flip(q), flip(k), flip(v), flip(li_b), flip(lf_b)))
    cell = (h_f + h_b)[:, :, PAD_FRONT:].transpose(0, 2, 1, 3)
    cell = rms_norm(cell, head_norm.reshape(MLSTM_HEADS, MLSTM_HEAD_V)).reshape(bsz, l, MLSTM_WIDTH)
    o = jax.nn.sigmoid(xc @ w_ogate + b_ogate)
    hh = o * cell.astype(xc.dtype) + skip * xc
    return (hh * jax.nn.silu(z)) @ w_out

def setup_inputs(seed: int = 0) -> dict:
    key = jax.random.key(seed)
    ks = iter(jax.random.split(key, 48))
    nrm = lambda shape, scale: jax.random.normal(next(ks), shape, jnp.float32) * scale
    gain = lambda shape: 1.0 + nrm(shape, 0.05)
    a_im0 = jnp.pi * jnp.arange(S5_STATE, dtype=jnp.float32)
    return {
        'x': nrm((BATCH, SEQ, D_MODEL), 1.0),
        'meta_tokens': nrm((N_META, D_MODEL), 1.0),
        'norm_pre': gain((DEPTH, D_MODEL)),
        'norm_post': gain((DEPTH, D_MODEL)),
        'w_in_even': nrm((N_EVEN, D_MODEL, EVEN_IN_WIDTH), D_MODEL ** -0.5),
        'q_norm': gain((N_EVEN, HEAD_DIM)),
        'k_norm': gain((N_EVEN, HEAD_DIM)),
        'ssm_a_re': -0.5 + nrm((N_EVEN, 2, S5_GROUPS, S5_STATE), 0.01),
        'ssm_a_im': a_im0 + nrm((N_EVEN, 2, S5_GROUPS, S5_STATE), 0.01),
        'ssm_log_dt': jax.random.uniform(next(ks), (N_EVEN, 2, S5_GROUPS), jnp.float32,
                                         math.log(1e-3), math.log(1e-1)),
        'ssm_b_re': nrm((N_EVEN, 2, S5_GROUPS, S5_STATE, S5_GROUP), (2 * S5_GROUP) ** -0.5),
        'ssm_b_im': nrm((N_EVEN, 2, S5_GROUPS, S5_STATE, S5_GROUP), (2 * S5_GROUP) ** -0.5),
        'ssm_c_re': nrm((N_EVEN, 2, S5_GROUPS, S5_GROUP, S5_STATE), S5_STATE ** -0.5),
        'ssm_c_im': nrm((N_EVEN, 2, S5_GROUPS, S5_GROUP, S5_STATE), S5_STATE ** -0.5),
        'ssm_d': nrm((N_EVEN, S5_WIDTH), 1.0),
        'w_glu': nrm((N_EVEN, S5_WIDTH, S5_WIDTH), S5_WIDTH ** -0.5),
        'b_glu': nrm((N_EVEN, S5_WIDTH), 0.02),
        'w_out_even': nrm((N_EVEN, ATTN_WIDTH + S5_WIDTH, D_MODEL), (ATTN_WIDTH + S5_WIDTH) ** -0.5),
        'w_in_odd': nrm((N_ODD, D_MODEL, 2 * MLSTM_WIDTH), D_MODEL ** -0.5),
        'conv_w': nrm((N_ODD, CONV_W, MLSTM_WIDTH), CONV_W ** -0.5),
        'conv_b': nrm((N_ODD, MLSTM_WIDTH), 0.02),
        'w_q': nrm((N_ODD, MLSTM_HEADS, MLSTM_HEAD_V, MLSTM_HEAD_QK), MLSTM_HEAD_V ** -0.5),
        'w_k': nrm((N_ODD, MLSTM_HEADS, MLSTM_HEAD_V, MLSTM_HEAD_QK), MLSTM_HEAD_V ** -0.5),
        'w_v': nrm((N_ODD, MLSTM_HEADS, MLSTM_HEAD_V, MLSTM_HEAD_V), MLSTM_HEAD_V ** -0.5),
        'w_igate': nrm((N_ODD, 2, MLSTM_WIDTH, MLSTM_HEADS), MLSTM_WIDTH ** -0.5),
        'b_igate': nrm((N_ODD, 2, MLSTM_HEADS), 0.1),
        'w_fgate': nrm((N_ODD, 2, MLSTM_WIDTH, MLSTM_HEADS), MLSTM_WIDTH ** -0.5),
        'b_fgate': jnp.linspace(3.0, 6.0, MLSTM_HEADS, dtype=jnp.float32) + nrm((N_ODD, 2, MLSTM_HEADS), 0.1),
        'w_ogate': nrm((N_ODD, MLSTM_WIDTH, MLSTM_WIDTH), MLSTM_WIDTH ** -0.5),
        'b_ogate': nrm((N_ODD, MLSTM_WIDTH), 0.02),
        'head_norm': gain((N_ODD, MLSTM_WIDTH)),
        'mlstm_skip': gain((N_ODD, MLSTM_WIDTH)),
        'w_out_odd': nrm((N_ODD, MLSTM_WIDTH, D_MODEL), MLSTM_WIDTH ** -0.5),
    }

def reference(x, meta_tokens, norm_pre, norm_post, w_in_even, q_norm, k_norm, ssm_a_re, ssm_a_im,
              ssm_log_dt, ssm_b_re, ssm_b_im, ssm_c_re, ssm_c_im, ssm_d, w_glu, b_glu, w_out_even,
              w_in_odd, conv_w, conv_b, w_q, w_k, w_v, w_igate, b_igate, w_fgate, b_fgate,
              w_ogate, b_ogate, head_norm, mlstm_skip, w_out_odd):
    bsz, n_real, _ = x.shape
    meta = jnp.broadcast_to(meta_tokens[None].astype(x.dtype), (bsz, N_META, D_MODEL))
    h_res = jnp.concatenate([meta, x], axis=1)
    tabs = axial_rope_tables(n_real)
    for layer in range(DEPTH):
        i = layer // 2
        h = rms_norm(h_res, norm_pre[layer])
        if layer % 2 == 0:
            y = attn_s5_layer(h, tabs, w_in_even[i], q_norm[i], k_norm[i], ssm_a_re[i], ssm_a_im[i],
                              ssm_log_dt[i], ssm_b_re[i], ssm_b_im[i], ssm_c_re[i], ssm_c_im[i],
                              ssm_d[i], w_glu[i], b_glu[i], w_out_even[i])
        else:
            y = mlstm_layer(h, w_in_odd[i], conv_w[i], conv_b[i], w_q[i], w_k[i], w_v[i],
                            w_igate[i], b_igate[i], w_fgate[i], b_fgate[i], w_ogate[i], b_ogate[i],
                            head_norm[i], mlstm_skip[i], w_out_odd[i])
        h_res = h_res + rms_norm(y, norm_post[layer])
    return h_res[:, N_META:]


_drawn_inputs = setup_inputs


def setup_inputs(seed=0):
    import zlib

    import numpy as np

    out = dict(_drawn_inputs(seed))
    spreads = {}
    factors = {'q_norm': 5.74,
     'k_norm': 6.252,
     'ssm_a_re': 200.0,
     'b_glu': 18.381,
     'b_igate': 5.106,
     'b_ogate': 8.0,
     'head_norm': 22.935,
     'mlstm_skip': 21.194,
     'ssm_a_im': 27.976,
     'ssm_log_dt': 29.504,
     'ssm_b_re': 39.248,
     'ssm_b_im': 38.752,
     'ssm_c_re': 39.48,
     'ssm_c_im': 39.48}
    for name, (base, spread) in spreads.items():
        noise = np.random.default_rng([zlib.crc32(name.encode()), seed]).standard_normal(out[name].shape)
        drawn = base * np.exp(spread * noise) if base else spread * noise
        out[name] = __import__('jax').numpy.asarray(drawn.astype(out[name].dtype))
    for name, factor in factors.items():
        out[name] = (out[name] * factor).astype(out[name].dtype)
    return out
```

```python
from contextlib import ExitStack, contextmanager
import math

import numpy as np

import concourse.bass as bass
from concourse import mybir

D = 1024
L = 1040
META = 16
P = 128
KC = D // P
HEADS, KV, HD = 8, 2, 128
G, GP, NS = 64, 16, 64
T = P // GP
CH = L // T
GB = 8
W2 = 2048
MH, MV, MK = 8, 256, 128
CONV = 5
GRID_W = 64
EPS = 1e-6
E_IN = 2 * HEADS * HD + 2 * KV * HD + 2 * D
Q0, K0, V0, GA0, U0, GB0 = 0, 1024, 1280, 1536, 2560, 3584
TILES = [(i * P, min(P, L - i * P)) for i in range(-(-L // P))]
NT = len(TILES)
PO = 248
PIECES = [(0, 264), (264, 512), (776, 264)]
QT = [(0, 120), (120, 120), (240, 112), (352, 120), (472, 112), (584, 112),
      (696, 120), (816, 112), (928, 112)]

F32 = mybir.dt.float32
I32 = mybir.dt.int32
ACT = mybir.ActivationFunctionType
ALU = mybir.AluOpType
AX = mybir.AxisListType.X


class Signal:

    def __init__(self, sem, per=1, credit=0):
        self.sem, self.per, self.credit = sem, per, credit

    def start(self, eng):
        eng.sem_inc(self.sem, self.credit)

    def wait(self, eng, i, k):
        eng.wait_ge(self.sem, i * self.per + (k + self.credit))


class Steps:

    def __init__(self, eng, sem):
        self.eng, self.sem, self.n, self.base = eng, sem, 0, 0

    def __call__(self, instruction):
        instruction.then_inc(self.sem, 1)
        self.n += 1
        self.eng.wait_ge(self.sem, self.base + self.n)
        return instruction

    def free(self, instruction):
        instruction.then_inc(self.sem, 1)
        self.n += 1
        return instruction

    @contextmanager
    def loop(self, count, per):
        before = self.n
        with self.eng.Fori(0, count) as i:
            self.n, self.base = 0, i * per + before
            yield i
            assert self.n == per, (self.n, per)
        self.n, self.base = before + count * per, 0


def trunk(nc, a, out):
    outer = ExitStack()
    Stage.finished = []
    with outer:
        top = Stage(nc, outer)
        c = {}
        d = dict(
            res=nc.dram_tensor("res_d", (P, KC, L), F32).ap(),
            u=nc.dram_tensor("u_d", (G, GP, T, CH), F32).ap(),
            y=nc.dram_tensor("y_d", (G, GP, T, CH), F32).ap(),
            cat=nc.dram_tensor("cat_d", (2 * KC, P, L), F32).ap(),
            v=nc.dram_tensor("v_d", (MH, P, NT, MV), F32).ap(),
            bm=nc.dram_tensor("bm_d", (2, MH, L), F32).ap(),
            ends=nc.dram_tensor("ends_d", (2, MH, 2, NT), F32).ap(),
            hh=nc.dram_tensor("hh_d", (2 * KC, P, L), F32).ap(),
        )
        constants(nc, top, a, c)
        h = top.sb("h", [P, KC, L])
        enter(nc, a, c, d, h)
        with ExitStack() as s5:
            s = s5_tensors(Stage(nc, s5))
            s5_inputs(nc, a, c, d, h, s)
            s5_states(nc, c, d, s)
            s5_scan(nc, s)
            s5_outputs(nc, c, d, s)
        s5_gates(nc, a, c, d, h)
        attention(nc, a, c, d, h)
        project_out(nc, a["w_out_even"], d["cat"], c, d, h, layer=0, out=None)
        with ExitStack() as ml:
            st = Stage(nc, ml)
            xc = st.sb("xc", [P, 2 * KC, L])
            conv_and_values(nc, a, c, d, h, xc)
            cols = st.sb("cols", [P, NT, 3, 40])
            gate_rows(nc, a, c, d, xc, cols)
            mlstm(nc, a, c, d, h, xc, cols)
        project_out(nc, a["w_out_odd"], d["hh"], c, d, h, layer=1, out=out)


class Stage:

    count = 0
    finished = []

    def __init__(self, nc, stack):
        self.nc, self.stack, self.sems = nc, stack, []

    def sb(self, name, shape, dtype=F32):
        Stage.count += 1
        return self.stack.enter_context(self.nc.sbuf_tensor(f"{name}_{Stage.count}", shape, dtype))

    def ps(self, name, columns):
        Stage.count += 1
        return self.stack.enter_context(self.nc.psum_tensor(f"{name}_{Stage.count}", [P, columns], F32))

    def sem(self, name):
        Stage.count += 1
        self.sems.append(self.nc.alloc_semaphore(f"{name}_{Stage.count}"))
        return self.sems[-1]

    def flag(self, name, per=1, credit=0):
        return Signal(self.sem(name), per, credit)


@contextmanager
def stage(nc):
    with ExitStack() as stack:
        s = Stage(nc, stack)
        yield s
        Stage.finished += s.sems
        if len(Stage.finished) > 50:
            nc.clear_and_free_semaphores(Stage.finished)
            nc.all_engine_barrier()
            Stage.finished = []


def rows_of(region):
    return region[:, PO:PO + L]


COLS_A = [("norm_pre", 16), ("norm_post", 16), ("q_norm", 1), ("k_norm", 1), ("b_glu", 8),
          ("conv_b", 16), ("b_ogate", 16), ("head_norm", 16), ("mlstm_skip", 16)]


def constants(nc, top, a, c):
    c["ident"] = top.sb("ident", [P, P])
    c["ones"] = top.sb("ones", [P, P])
    c["cols_a"] = top.sb("cols_a", [P, 112])
    c["conv_w"] = top.sb("conv_w", [P, CONV * 2 * KC])
    c["eps"] = top.sb("eps", [P, 1])
    with stage(nc) as s:
        ra, rb = s.sb("ra", [P, P]), s.sb("rb", [P, P])
        pt = s.ps("pt", 512)
        loaded, made, turned = s.sem("params_loaded"), s.sem("ones_made"), s.sem("turned")
        with nc.Block() as block:
            @block.sync
            def _(sp):
                sp.dma_start(c["ident"][:, :], a["ident"]).then_inc(loaded, 16)
                at = 0
                for name, n in COLS_A:
                    c[name] = at
                    sp.dma_start(ra[at:at + n, :], a[name].rearrange("(r p) -> r p", p=P)).then_inc(loaded, 16)
                    at += n
                sp.dma_start(rb[0:CONV * 16, :], a["conv_w"].rearrange("w (r p) -> (w r) p", p=P)).then_inc(loaded, 16)

            @block.vector
            def _(dve):
                nc.vector.memset(c["ones"][:, :], 1.0)
                nc.vector.memset(c["eps"][:, :], EPS)
                dve.wait_ge(turned, 1)
                nc.vector.tensor_copy(c["cols_a"][:, 0:106], pt[:, 0:106])
                nc.vector.tensor_copy(c["conv_w"][:, :], pt[:, 128:128 + CONV * 16])

            @block.tensor
            def _(pe):
                pe.wait_ge(loaded, 16 * (len(COLS_A) + 2))
                nc.tensor.transpose(pt[:, 0:106], ra[0:106, :], c["ident"][0:106, 0:106])
                nc.tensor.transpose(pt[:, 128:128 + CONV * 16], rb[0:CONV * 16, :],
                                    c["ident"][0:CONV * 16, 0:CONV * 16]).then_inc(turned, 1)
    a_cols = c["cols_a"]
    c["col"] = lambda name, i: a_cols[:, c[name] + i:c[name] + i + 1]


def sum_of_squares(nc, pe, ones, squares, region, ready, used, signal_done):
    for k in range(KC):
        ready.wait(pe, 0, k + 1)
        for off, n in PIECES:
            last = nc.tensor.matmul(region[:, PO + off:PO + off + n], ones[:, :], squares[:, k % 2, off:off + n],
                                    start=(k == 0), stop=(k == KC - 1))
        last.then_inc(used.sem, 1)
    last = None


def norm_block(nc, c, src, dst, gain, resid=None, save=None):
    with stage(nc) as s:
        sq = s.sb("sq", [P, 2, L])
        rstd = s.sb("rstd", [P, L])
        rt = s.sb("resid", [P, KC, L]) if resid is not None else None
        tmp = s.sb("tmp", [P, 2, L])
        region = s.ps("sumsq", 1536)
        squared = s.flag("squared")
        used = s.flag("squares_used", credit=2)
        root = s.sem("root_done")
        loaded = s.sem("resid_loaded")
        scaled, saved = s.sem("scaled"), s.sem("saved")
        steps = s.sem("dve_steps")
        with nc.Block() as block:
            @block.sync
            def _(sp):
                if resid is not None:
                    sp.dma_start(rt[:, :, :], resid).then_inc(loaded, 16)
                if save is not None:
                    for k in range(KC):
                        sp.wait_ge(scaled, k + 1)
                        sp.dma_start(save[:, k, :], dst[:, k, :]).then_inc(saved, 16)
                    sp.wait_ge(saved, 16 * KC)

            @block.scalar
            def _(act):
                for k in range(KC):
                    used.wait(act, 0, k - 1)
                    nc.scalar.activation(sq[:, k % 2, :], src[:, k, :], ACT.Square).then_inc(squared.sem, 1)
                used.wait(act, 0, KC)
                nc.scalar.activation(rstd[:, :], rows_of(region), ACT.Sqrt, bias=c["eps"][:, :],
                                     scale=1.0 / D).then_inc(root, 1)

            @block.tensor
            def _(pe):
                used.start(pe)
                sum_of_squares(nc, pe, c["ones"], sq, region, squared, used, None)

            @block.vector
            def _(dve):
                do = Steps(dve, steps)
                dve.wait_ge(root, 1)
                do(nc.vector.reciprocal(rstd[:, :], rstd[:, :]))
                if resid is not None:
                    dve.wait_ge(loaded, 16)
                for k in range(KC):
                    if resid is None:
                        nc.vector.scalar_tensor_tensor(dst[:, k, :], src[:, k, :], gain(k), rstd[:, :],
                                                       ALU.mult, ALU.mult).then_inc(scaled, 1)
                    else:
                        do(nc.vector.scalar_tensor_tensor(tmp[:, k % 2, :], src[:, k, :], gain(k), rstd[:, :],
                                                          ALU.mult, ALU.mult))
                        nc.vector.tensor_tensor(dst[:, k, :], tmp[:, k % 2, :], rt[:, k, :],
                                                ALU.add).then_inc(scaled, 1)


def enter(nc, a, c, d, h):
    with stage(nc) as s0:
        res = s0.sb("res", [P, KC, L])
        with stage(nc) as s:
            xt = s.sb("xt", [P, 2, D])
            mt = s.sb("mt", [META, D])
            pt = [s.ps(f"pt{i}", 512) for i in range(4)]
            xl = [s.sem("x_loaded0"), s.sem("x_loaded1")]
            ml = s.sem("meta_loaded")
            turned = s.flag("turned", per=4, credit=4)
            evac = s.flag("evac", per=4, credit=4)
            meta_turned = s.sem("meta_turned")
            saved = s.sem("saved")
            x_tiles = a["x"].rearrange("(i p) f -> i p f", p=P)
            with nc.Block() as block:
                @block.sync
                def _(sp):
                    sp.dma_start(mt[:, :], a["meta_tokens"]).then_inc(ml, 16)
                    with sp.Fori(0, 4) as i:
                        for b in range(2):
                            turned.wait(sp, i, 2 * b - 2)
                            sp.dma_start(xt[:, b, :], x_tiles[i * 2 + b]).then_inc(xl[b], 16)

                @block.tensor
                def _(pe):
                    turned.start(pe)
                    with pe.Fori(0, 4) as i:
                        for b in range(2):
                            pe.wait_ge(xl[b], i * 16 + 16)
                            for half in range(2):
                                evac.wait(pe, i, 2 * b + half - 3)
                                for k in range(4):
                                    last = nc.tensor.transpose(pt[2 * b + half][:, k * P:(k + 1) * P],
                                                               xt[:, b, (4 * half + k) * P:(4 * half + k + 1) * P],
                                                               c["ident"][:, :])
                                last.then_inc(turned.sem, 1)
                    pe.wait_ge(ml, 16)
                    evac.wait(pe, 3, 4)
                    for k in range(KC):
                        last = nc.tensor.transpose(pt[0][:, k * META:(k + 1) * META], mt[:, k * P:(k + 1) * P],
                                                   c["ident"][0:META, 0:META])
                    last.then_inc(meta_turned, 1)

                @block.vector
                def _(dve):
                    evac.start(dve)
                    with dve.Fori(0, 4) as i:
                        for b in range(2):
                            for half in range(2):
                                turned.wait(dve, i, 2 * b + half + 1)
                                nc.vector.tensor_copy(
                                    res[:, 4 * half:4 * half + 4, bass.ds(i * 256 + (b * P + META), P)],
                                    pt[2 * b + half][:, :].rearrange("p (k t) -> p k t", k=4)).then_inc(evac.sem, 1)
                    dve.wait_ge(meta_turned, 1)
                    nc.vector.tensor_copy(res[:, :, 0:META], pt[0][:, 0:P].rearrange("p (k t) -> p k t", k=KC))
        with stage(nc) as s:
            saved = s.sem("saved")
            with nc.Block() as block:
                @block.sync
                def _(sp):
                    sp.dma_start(d["res"], res[:, :, :]).then_inc(saved, 16)
                    sp.wait_ge(saved, 16)
        norm_block(nc, c, res, h, lambda k: c["col"]("norm_pre", k))


def s5_tensors(s):
    t = {}
    t["B"] = s.sb("B", [P, 2, G, GP])
    t["C"] = s.sb("C", [P, 3, G, GP])
    t["pw_in"] = s.sb("pw_in", [P, T, 2, G])
    t["pw_out"] = s.sb("pw_out", [P, T, 2, G])
    t["step_re"] = s.sb("step_re", [P, 2, G])
    t["step_im"] = s.sb("step_im", [P, 2, G])
    t["skip"] = s.sb("skip", [P, G])
    t["Z"] = s.sb("Z", [P, CH + 1, 2, G])
    return t


ROUND = 1.5 * 2.0 ** 23
LN2_HI, LN2_LO = 0.693359375, -2.12194440e-4
PI2_A, PI2_B = 6.28125, 0.0019350051879882812
PI2_C = 2 * math.pi - PI2_A - PI2_B


def s5_inputs(nc, a, c, d, h, t):
    with stage(nc) as s:
        w = s.sb("w", [P, 2, KC, P])
        st = s.sb("staged", [P, 2, T, CH])
        raw = s.sb("raw", [G, 2, P])
        dr = s.sb("d_rows", [G, T, GP])
        a0 = s.sb("a", [P, 2, G])
        logdt = s.sb("log_dt", [P, G])
        b_in = s.sb("b_in", [P, 2, G, GP])
        c_in = s.sb("c_in", [P, 2, KC, P])
        x = s.sb("x", [P, 24, G])
        xi = s.sb("xi", [P, G], I32)
        pw = s.sb("pw", [P, T + 1, 2, G])
        pt = s.sb("pt", [P, 2, 4, G])
        bt = s.sb("bt", [P, 2, G, GP])
        reg = [s.ps(f"u{b}", 1536) for b in range(2)]
        pa, pc = s.ps("pa", 512), s.ps("pc", 512)
        wl = [s.sem("w_loaded0"), s.sem("w_loaded1")]
        params, skip_loaded = s.sem("params_loaded"), s.sem("skip_loaded")
        bl, cl = s.sem("b_loaded"), s.sem("c_loaded")
        mm = s.flag("u_projected", per=2, credit=2)
        evac = s.flag("u_copied", per=2, credit=2)
        st_sem = [s.flag(f"u_stored{b}", per=16, credit=16) for b in range(2)]
        at, ac, acc = s.sem("a_turned"), s.sem("c_turned"), s.sem("c_copied")
        steps = s.sem("dve_steps")
        asked, answered = s.sem("function_asked"), s.sem("function_done")
        wv = a["w_in_even"].rearrange("(k p) n -> p k n", p=P)
        uv = d["u"].rearrange("(j g) p s c -> j (g p) (s c)", j=KC)
        with nc.Block() as block:
            @block.sync
            def _(sp):
                for q, name in enumerate(("ssm_a_re", "ssm_a_im")):
                    for r in range(2):
                        sp.dma_start(raw[:, q, r * NS:(r + 1) * NS], a[name][r]).then_inc(params, 16)
                for r in range(2):
                    rows = slice(r * NS, (r + 1) * NS)
                    sp.dma_start(logdt[rows, :], a["ssm_log_dt"][r:r + 1, :].broadcast_to([NS, G])).then_inc(params, 16)
                    for q, name in enumerate(("ssm_b_re", "ssm_b_im")):
                        sp.dma_start(b_in[rows, q, :, :], a[name][r].rearrange("g n p -> n g p")).then_inc(bl, 16)
                    for q, name in enumerate(("ssm_c_re", "ssm_c_im")):
                        sp.dma_start(c_in[:, q, :, rows],
                                     a[name][r].rearrange("(k g) q n -> (g q) k n", k=KC)).then_inc(cl, 16)
                with sp.Fori(0, KC // 2) as i:
                    for b in range(2):
                        mm.wait(sp, i, b - 1)
                        sp.dma_start(w[:, b, :, :], wv[:, :, bass.ds(i * 256 + (U0 + b * P), P)]).then_inc(wl[b], 16)

            @block.gpsimd
            def _(gp):
                for j in range(T):
                    gp.dma_start(dr[:, j, :], a["ssm_d"].rearrange("(g p) -> g p", p=GP)).then_inc(skip_loaded, 16)

            @block.tensor
            def _(pe):
                mm.start(pe)
                pe.wait_ge(params, 16 * 6)
                pe.wait_ge(skip_loaded, 16 * T)
                for q in range(2):
                    nc.tensor.transpose(pa[:, q * G:(q + 1) * G], raw[:, q, :], c["ident"][0:G, 0:G])
                last = nc.tensor.transpose(pa[:, 2 * G:3 * G], dr[:, :, :].rearrange("g s p -> g (s p)"),
                                           c["ident"][0:G, 0:G])
                last.then_inc(at, 1)
                pe.wait_ge(cl, 16 * 4)
                for q in range(2):
                    for k in range(0, KC, 4):
                        if q or k:
                            pe.wait_ge(acc, 2 * q + k // 4)
                        for kk in range(4):
                            last = nc.tensor.transpose(pc[:, kk * P:(kk + 1) * P], c_in[:, q, k + kk, :],
                                                       c["ident"][:, :])
                        last.then_inc(ac, 1)
                with pe.Fori(0, KC // 2) as i:
                    for b in range(2):
                        pe.wait_ge(wl[b], i * 16 + 16)
                        evac.wait(pe, i, b - 1)
                        for k in range(KC):
                            for off, n in PIECES:
                                last = nc.tensor.matmul(reg[b][:, PO + off:PO + off + n], w[:, b, k, :],
                                                        h[:, k, off:off + n], start=(k == 0), stop=(k == KC - 1))
                        last.then_inc(mm.sem, 1)

            calls = [(ACT.Tanh, 3, 4, 0.5), (ACT.Sin, 8, 9, 1.0), (ACT.Sin, 8, 10, 0.5), (ACT.Tanh, 6, 11, 0.5)]

            @block.scalar
            def _(act):
                evac.start(act)
                for b in range(2):
                    st_sem[b].start(act)
                for n, (f, src, dst, scale) in enumerate(calls):
                    act.wait_ge(asked, 1 if n == 0 else 2)
                    nc.scalar.activation(x[:, dst, :], x[:, src, :], f, scale=scale).then_inc(answered, 1)
                with act.Fori(0, KC // 2) as i:
                    for b in range(2):
                        mm.wait(act, i, b + 1)
                        st_sem[b].wait(act, i, 0)
                        nc.scalar.activation(st[:, b, :, :].rearrange("p s c -> p c s"),
                                             rows_of(reg[b]).rearrange("p (c s) -> p c s", s=T),
                                             ACT.Copy).then_inc(evac.sem, 1)
                        evac.wait(act, i, b + 1)
                        act.dma_start(uv[i * 2 + b], st[:, b, :, :]).then_inc(st_sem[b].sem, 16)
                for b in range(2):
                    st_sem[b].wait(act, KC // 2, 0)

            @block.vector
            def _(dve):
                v = nc.vector
                do = Steps(dve, steps)

                def two(o, i0, s1, op0, s2=None, op1=None):
                    do(v.tensor_scalar(o, i0, s1, s2, op0, op1) if op1 is not None else
                       v.tensor_scalar(o, i0, s1, None, op0))

                def tt(o, i0, i1, op):
                    do(v.tensor_tensor(o, i0, i1, op))

                def X(n):
                    return x[:, n, :]

                dve.wait_ge(params, 16 * 6)
                two(X(0), logdt[:, :], -87.0, ALU.max)
                two(X(1), X(0), 1 / math.log(2), ALU.mult)
                two(X(1), X(1), ROUND, ALU.add)
                two(X(1), X(1), ROUND, ALU.subtract)
                do(v.scalar_tensor_tensor(X(2), X(1), -LN2_HI, X(0), ALU.mult, ALU.add))
                do(v.scalar_tensor_tensor(X(3), X(1), -LN2_LO, X(2), ALU.mult, ALU.add))
                two(xi[:, :], X(1), 127.0, ALU.add)
                do(v.tensor_single_scalar(xi[:, :], xi[:, :], 23, ALU.logical_shift_left))
                dve.sem_inc(asked, 1)
                dve.wait_ge(answered, 1)
                two(X(5), X(4), -1.0, ALU.mult, 1.0, ALU.add)
                do(v.reciprocal(X(5), X(5)))
                do(v.scalar_tensor_tensor(X(4), X(4), 1.0, X(5), ALU.add, ALU.mult))
                tt(X(12), X(4), xi[:, :].bitcast(F32), ALU.mult)
                dve.wait_ge(at, 1)
                do(v.tensor_copy(a0[:, :, :], pa[:, 0:2 * G].rearrange("p (q g) -> p q g", q=2)))
                do(v.tensor_copy(t["skip"][:, :], pa[:, 2 * G:3 * G]))
                tt(X(6), a0[:, 0, :], X(12), ALU.mult)
                tt(X(7), a0[:, 1, :], X(12), ALU.mult)
                two(X(13), X(7), 1 / (2 * math.pi), ALU.mult)
                two(X(13), X(13), ROUND, ALU.add)
                two(X(13), X(13), ROUND, ALU.subtract)
                for part in (PI2_A, PI2_B, PI2_C):
                    do(v.scalar_tensor_tensor(X(7), X(13), -part, X(7), ALU.mult, ALU.add))
                two(X(8), X(7), 3.1415925, ALU.min, -3.1415925, ALU.max)
                dve.sem_inc(asked, 1)
                dve.wait_ge(answered, 4)
                two(X(14), X(11), -1.0, ALU.mult, 1.0, ALU.add)
                do(v.reciprocal(X(14), X(14)))
                do(v.scalar_tensor_tensor(X(14), X(11), 2.0, X(14), ALU.mult, ALU.mult))
                do(v.scalar_tensor_tensor(X(15), X(10), -2.0, X(10), ALU.mult, ALU.mult))
                do(v.scalar_tensor_tensor(X(16), X(15), 1.0, X(14), ALU.add, ALU.mult))
                tt(X(16), X(16), X(15), ALU.add)
                do(v.scalar_tensor_tensor(X(17), X(14), 1.0, X(9), ALU.add, ALU.mult))
                tt(X(18), a0[:, 0, :], a0[:, 0, :], ALU.mult)
                tt(X(19), a0[:, 1, :], a0[:, 1, :], ALU.mult)
                tt(X(18), X(18), X(19), ALU.add)
                do(v.reciprocal(X(18), X(18)))
                tt(X(19), X(16), a0[:, 0, :], ALU.mult)
                tt(X(20), X(17), a0[:, 1, :], ALU.mult)
                tt(X(19), X(19), X(20), ALU.add)
                tt(X(21), X(19), X(18), ALU.mult)
                tt(X(19), X(17), a0[:, 0, :], ALU.mult)
                tt(X(20), X(16), a0[:, 1, :], ALU.mult)
                tt(X(19), X(19), X(20), ALU.subtract)
                tt(X(22), X(19), X(18), ALU.mult)
                do(v.memset(pw[:, 0, 0, :], 1.0))
                do(v.memset(pw[:, 0, 1, :], 0.0))
                two(pw[:, 1, 0, :], X(16), 1.0, ALU.add)
                do(v.tensor_copy(pw[:, 1, 1, :], X(17)))
                n = 1
                while n < T:
                    lo = pw[:, 1:n + 1, :, :]

                    def last(q, n=n):
                        return pw[:, n:n + 1, q, :].broadcast_to([P, n, G])
                    tt(pt[:, 0, 0:n, :], lo[:, :, 0, :], last(0), ALU.mult)
                    tt(pt[:, 1, 0:n, :], lo[:, :, 1, :], last(1), ALU.mult)
                    tt(pw[:, n + 1:2 * n + 1, 0, :], pt[:, 0, 0:n, :], pt[:, 1, 0:n, :], ALU.subtract)
                    tt(pt[:, 0, 0:n, :], lo[:, :, 0, :], last(1), ALU.mult)
                    tt(pt[:, 1, 0:n, :], lo[:, :, 1, :], last(0), ALU.mult)
                    tt(pw[:, n + 1:2 * n + 1, 1, :], pt[:, 0, 0:n, :], pt[:, 1, 0:n, :], ALU.add)
                    n *= 2
                f, r = slice(0, NS), slice(NS, P)
                for e in range(T):
                    do.free(v.tensor_copy(t["pw_in"][f, e, :, :], pw[f, T - 1 - e, :, :]))
                    do.free(v.tensor_copy(t["pw_in"][r, e, :, :], pw[r, e, :, :]))
                    do.free(v.tensor_copy(t["pw_out"][f, e, :, :], pw[f, e + 1, :, :]))
                    do.free(v.tensor_copy(t["pw_out"][r, e, :, :], pw[r, T - e, :, :]))
                do.free(v.tensor_copy(t["step_re"][:, 0, :], pw[:, T, 0, :]))
                do.free(v.tensor_copy(t["step_re"][:, 1, :], pw[:, T, 0, :]))
                two(t["step_im"][:, 1, :], pw[:, T, 1, :], -1.0, ALU.mult)
                do.free(v.tensor_copy(t["step_im"][:, 0, :], pw[:, T, 1, :]))
                do.free(v.memset(t["Z"][:, 0, :, :], 0.0))
                dve.wait_ge(bl, 16 * 4)
                g = [X(21 + q).unsqueeze(2).broadcast_to([P, G, GP]) for q in range(2)]
                tt(bt[:, 0], b_in[:, 0], g[0], ALU.mult)
                tt(bt[:, 1], b_in[:, 1], g[1], ALU.mult)
                tt(t["B"][:, 0], bt[:, 0], bt[:, 1], ALU.subtract)
                tt(bt[:, 0], b_in[:, 0], g[1], ALU.mult)
                tt(bt[:, 1], b_in[:, 1], g[0], ALU.mult)
                tt(t["B"][:, 1], bt[:, 0], bt[:, 1], ALU.add)
                for q in range(2):
                    for k in range(2):
                        dve.wait_ge(ac, 2 * q + k + 1)
                        v.tensor_copy(t["C"][:, q, 32 * k:32 * k + 32, :],
                                      pc[:, :].rearrange("p (g q) -> p g q", q=GP)).then_inc(acc, 1)
                dve.wait_ge(acc, 4)
                do(v.tensor_scalar(t["C"][:, 2], t["C"][:, 1], -1.0, None, ALU.mult))


def complex_table(nc, do, out, tmp, pw, x, sign):
    v, tt = nc.vector, nc.vector.tensor_tensor

    def p(q):
        return pw[:, q].rearrange("p s g -> p g s").unsqueeze(3).broadcast_to([P, GB, T, GP])

    def y(q):
        return x[:, q].unsqueeze(2).broadcast_to([P, GB, T, GP])
    do.free(tt(tmp[:, 0], p(0), y(0), ALU.mult))
    do(tt(tmp[:, 1], p(1), y(1), ALU.mult))
    do.free(tt(out[:, 0], tmp[:, 0], tmp[:, 1], ALU.subtract))
    do.free(tt(tmp[:, 2], p(0), y(1), ALU.mult))
    do(tt(tmp[:, 3], p(1), y(0), ALU.mult))
    if sign > 0:
        return tt(out[:, 1], tmp[:, 2], tmp[:, 3], ALU.add)
    flat = [z.rearrange("p g s q -> p (g s q)") for z in (out[:, 1], tmp[:, 2], tmp[:, 3])]
    return v.scalar_tensor_tensor(flat[0], flat[1], -1.0, flat[2], ALU.mult, ALU.subtract)


def s5_states(nc, c, d, t):
    with stage(nc) as s:
        us = s.sb("us", [P, G, CH])
        blk = s.sb("blk", [P, 2, GB, T * GP + 2 * T])
        tab = s.sb("tab", [P, 2, GB, T, GP])
        tmp = s.sb("tmp", [P, 4, GB, T, GP])
        wl = s.sb("w_in", [P, GB, 2, P])
        tp = [s.ps(f"tp{b}", 512) for b in range(2)]
        zp = [s.ps(f"zp{b}", 512) for b in range(4)]
        loaded = s.sem("u_loaded")
        built = s.flag("table_built")
        turned = s.flag("turned", per=4, credit=4)
        copied = s.flag("weights_copied", per=4, credit=4)
        summed = s.flag("summed", per=GB, credit=GB)
        stored = s.flag("stored", per=GB, credit=GB)
        steps = s.sem("dve_steps")
        uv = d["u"].rearrange("g p s c -> s p g c")
        with nc.Block() as block:
            @block.sync
            def _(sp):
                for j in range(T):
                    sp.dma_start(us[j * GP:(j + 1) * GP, :, :], uv[j]).then_inc(loaded, 16)

            @block.vector
            def _(dve):
                do = Steps(dve, steps)
                with do.loop(G // GB, 5) as i:
                    turned.wait(dve, i, 0)
                    g = bass.ds(i * GB, GB)
                    complex_table(nc, do, tab, tmp,
                                  t["pw_in"][:, :, :, g].rearrange("p s q g -> p q s g"),
                                  t["B"][:, :, g, :], 1).then_inc(built.sem, 1)

            @block.tensor
            def _(pe):
                turned.start(pe)
                summed.start(pe)
                pe.wait_ge(loaded, 16 * T)
                with pe.Fori(0, G // GB) as i:
                    built.wait(pe, i, 1)
                    for m in range(4):
                        copied.wait(pe, i, m - 1)
                        for n in range(4):
                            g, q = 2 * m + n // 2, n % 2
                            last = nc.tensor.transpose(tp[m % 2][:, n * P:(n + 1) * P],
                                                       tab[:, q, g].rearrange("p s q -> p (s q)"), c["ident"][:, :])
                        last.then_inc(turned.sem, 1)
                    for g in range(GB):
                        if g % 2 == 0:
                            copied.wait(pe, i, g // 2 + 1)
                        stored.wait(pe, i, g - 3)
                        for q in range(2):
                            last = nc.tensor.matmul(zp[g % 4][:, q * CH:(q + 1) * CH], wl[:, g, q, :],
                                                    us[:, bass.ds(i * GB + g, 1), :].rearrange("p g c -> p (g c)"),
                                                    start=True, stop=True)
                        last.then_inc(summed.sem, 1)

            @block.scalar
            def _(act):
                copied.start(act)
                stored.start(act)
                with act.Fori(0, G // GB) as i:
                    for m in range(4):
                        turned.wait(act, i, m + 1)
                        summed.wait(act, i, 2 * m + 2 - GB)
                        nc.scalar.activation(wl[:, 2 * m:2 * m + 2, :, :].rearrange("p g q m -> p (g q m)"),
                                             tp[m % 2][:, :], ACT.Copy).then_inc(copied.sem, 1)
                    for g in range(GB):
                        summed.wait(act, i, g + 1)
                        gg = bass.ds(i * GB + g, 1)
                        f, r = slice(0, NS), slice(NS, P)
                        src = zp[g % 4][:, 0:2 * CH].rearrange("p (q c) -> p q c", q=2)
                        nc.scalar.activation(
                            t["Z"][f, 1:CH + 1, :, gg].rearrange("p c q g -> p q (c g)"), src[f], ACT.Copy)
                        nc.scalar.activation(
                            t["Z"][r, 1:CH + 1, :, gg].rearrange("p c q g -> p q (c g)"),
                            src[r, :, ::-1], ACT.Copy).then_inc(stored.sem, 1)


def s5_scan(nc, t):
    with stage(nc) as s:
        tmp = s.sb("tmp", [P, 2, 2, G])
        steps = s.sem("dve_steps")
        with nc.Block() as block:
            @block.vector
            def _(dve):
                do = Steps(dve, steps)
                tt = nc.vector.tensor_tensor
                with do.loop(CH // 2, 8) as i:
                    for b in range(2):
                        now = t["Z"][:, bass.ds(i * 2 + b, 1), :, :].rearrange("p k q g -> p (k q) g")
                        nxt = t["Z"][:, bass.ds(i * 2 + (b + 1), 1), :, :].rearrange("p k q g -> p (k q) g")
                        do.free(tt(tmp[:, 0], now, t["step_re"][:, :, :], ALU.mult))
                        do(tt(tmp[:, 1], now, t["step_im"][:, :, :], ALU.mult))
                        do(tt(tmp[:, 0], tmp[:, 0], tmp[:, 1, ::-1, :], ALU.add))
                        do(tt(nxt, nxt, tmp[:, 0], ALU.add))


def s5_outputs(nc, c, d, t):
    K = 2 * (T - 1) * GP + GP
    with stage(nc) as s:
        us = s.sb("us", [P, GB, CH])
        bb = s.sb("bb", [P, 2, GB, GP])
        cb = s.sb("cb", [P, 3, GB, GP])
        tab = s.sb("tab", [P, 2, GB, T, GP])
        tmp = s.sb("tmp", [P, 4, GB, T, GP])
        kt = s.sb("kt", [GP, GB, K])
        toe = s.sb("toe", [P, GB, P])
        diag = s.sb("diag", [P, GB, P])
        rhs = s.sb("rhs", [P, GB, 2, CH])
        ys = s.sb("ys", [P, GB, CH])
        kb = [s.ps(f"kb{b}", 512) for b in range(2)]
        kf = [s.ps(f"kf{b}", 512) for b in range(2)]
        yp = [s.ps(f"yp{b}", 512) for b in range(3)]
        u_loaded = s.sem("u_loaded")
        built = s.flag("table_built", per=1)
        gathered = s.flag("states_gathered", per=2)
        lag = s.flag("lags_done", per=GB, credit=GB)
        lagc = s.flag("lags_copied", per=GB, credit=GB)
        windowed = s.flag("windows_loaded", per=16 * T, credit=16)
        toe_ready = s.flag("toeplitz_ready", per=1)
        done = s.flag("outputs_done", per=GB, credit=GB)
        ycop = s.flag("outputs_copied", per=GB, credit=GB)
        ysto = s.flag("outputs_stored", per=16 * T, credit=16)
        steps = s.sem("dve_steps")
        uv = d["u"].rearrange("g p s c -> s p g c")
        yv = d["y"].rearrange("g p s c -> s p g c")
        NB = G // GB
        with nc.Block() as block:
            @block.sync
            def _(sp):
                with sp.Fori(0, NB) as i:
                    g = bass.ds(i * GB, GB)
                    done.wait(sp, i, 0)
                    for j in range(T):
                        sp.dma_start(us[j * GP:(j + 1) * GP, :, :], uv[j][:, g, :]).then_inc(u_loaded, 16)
                    lagc.wait(sp, i, GB)
                    for j in range(T):
                        off = (T - 1 - j) * GP
                        sp.dma_start(toe[j * GP:(j + 1) * GP, :, :], kt[:, :, off:off + P]).then_inc(windowed.sem, 16)

            @block.vector
            def _(dve):
                do = Steps(dve, steps)
                lagc.start(dve)
                windowed.start(dve)
                with do.loop(NB, 9) as i:
                    g = bass.ds(i * GB, GB)
                    done.wait(dve, i, 0)
                    do.free(nc.vector.tensor_copy(bb[:, :, :, :], t["B"][:, :, g, :]))
                    do.free(nc.vector.tensor_copy(cb[:, :, :, :], t["C"][:, :, g, :]))
                    complex_table(nc, do, tab, tmp,
                                  t["pw_out"][:, :, :, g].rearrange("p s q g -> p q s g"),
                                  t["C"][:, :, g, :], -1).then_inc(built.sem, 1)
                    for n in range(GB):
                        lag.wait(dve, i, n + 1)
                        if n == 0:
                            windowed.wait(dve, i, 0)
                        nc.vector.tensor_copy(kt[:, n, 0:(T - 1) * GP], kb[n % 2][0:GP, 0:(T - 1) * GP])
                        nc.vector.tensor_copy(kt[:, n, (T - 1) * GP:K], kf[n % 2][0:GP, 0:T * GP])\
                            .then_inc(lagc.sem, 1)
                    do(nc.vector.tensor_tensor(
                        diag[:, :, :], c["ident"][:, :].unsqueeze(1).broadcast_to([P, GB, P]),
                        t["skip"][:, g].unsqueeze(2).broadcast_to([P, GB, P]), ALU.mult))
                    windowed.wait(dve, i, 16 * T)
                    do(nc.vector.tensor_tensor(toe[:, :, :], toe[:, :, :], diag[:, :, :], ALU.add))
                    dve.sem_inc(toe_ready.sem, 1)

            @block.tensor
            def _(pe):
                lag.start(pe)
                done.start(pe)
                with pe.Fori(0, NB) as i:
                    built.wait(pe, i, 1)
                    f, r = slice(0, NS), slice(NS, P)
                    flat = "p t q -> p (t q)"
                    for n in range(GB):
                        lagc.wait(pe, i, n - 1)
                        ob, o = kb[n % 2][0:GP, :], kf[n % 2][0:GP, :]
                        for q in range(2):
                            nc.tensor.matmul(o[:, 0:GP], bb[:, q, n, :],
                                                    cb[:, 2 * q, n, :], start=(q == 0), stop=(q == 1))
                        for q in range(2):
                            nc.tensor.matmul(ob[:, 0:(T - 1) * GP], bb[r, q, n, :],
                                             tab[r, q, n, 1:T, :].rearrange(flat), start=(q == 0), stop=(q == 1))
                        for q in range(2):
                            last = nc.tensor.matmul(o[:, GP:T * GP], bb[f, q, n, :],
                                                    tab[f, q, n, 0:T - 1, :].rearrange(flat), start=(q == 0), stop=(q == 1))
                        last.then_inc(lag.sem, 1)
                    pe.wait_ge(u_loaded, (i + 1) * (16 * T))
                    gathered.wait(pe, i, 2)
                    toe_ready.wait(pe, i, 1)
                    for n in range(GB):
                        ycop.wait(pe, i, n - 2)
                        o = yp[n % 3][:, 0:CH]
                        nc.tensor.matmul(o, toe[:, n, :], us[:, n, :], start=True, stop=False)
                        nc.tensor.matmul(o, tab[:, 0, n].rearrange(flat), rhs[:, n, 0, :], start=False, stop=False)
                        nc.tensor.matmul(o, tab[:, 1, n].rearrange(flat), rhs[:, n, 1, :],
                                         start=False, stop=True).then_inc(done.sem, 1)

            @block.scalar
            def _(act):
                ycop.start(act)
                ysto.start(act)
                with act.Fori(0, NB) as i:
                    g = bass.ds(i * GB, GB)
                    done.wait(act, i, 0)
                    for rows, order in ((slice(0, NS), slice(None)), (slice(NS, P), slice(None, None, -1))):
                        for q in range(2):
                            ins = nc.scalar.activation(
                                rhs[rows, :, q, order], t["Z"][rows, 0:CH, q, g].rearrange("p c g -> p g c"), ACT.Copy)
                        ins.then_inc(gathered.sem, 1)
                    ysto.wait(act, i, 0)
                    for n in range(GB):
                        done.wait(act, i, n + 1)
                        nc.scalar.activation(ys[:, n, :], yp[n % 3][:, 0:CH], ACT.Copy).then_inc(ycop.sem, 1)
                    ycop.wait(act, i, GB)
                    for j in range(T):
                        act.dma_start(yv[j][:, bass.ds(i * GB, GB), :],
                                      ys[j * GP:(j + 1) * GP, :, :]).then_inc(ysto.sem, 16)
                ysto.wait(act, NB, 0)


def weight_loads(sp, i, used, slots, loaded, sources):
    for b, source in enumerate(sources):
        used.wait(sp, i, b + 1 - len(sources))
        sp.dma_start(slots[b], source).then_inc(loaded[b], 16)


def product(nc, region, w, x, kc):
    for k in range(kc):
        for off, n in PIECES:
            last = nc.tensor.matmul(region[:, PO + off:PO + off + n], w[:, k, :], x(k, off, n),
                                    start=(k == 0), stop=(k == kc - 1))
    return last


def s5_gates(nc, a, c, d, h):
    with stage(nc) as s:
        y = s.sb("y", [P, KC, L])
        yin = s.sb("y_in", [P, 2, T, CH])
        w = s.sb("w", [P, 2, KC, P])
        sg = s.sb("sigmoids", [P, 2, L])
        t = s.sb("gated", [P, 2, L])
        reg = [s.ps(f"r{b}", 1536) for b in range(2)]
        yl = [s.sem(f"y_loaded{b}") for b in range(2)]
        gelu = s.sem("gelu_done")
        bias = s.sb("bias", [P, 1])
        col = s.flag("bias_ready")
        wl = [s.sem("glu_loaded"), s.sem("gate_loaded")]
        mm = s.flag("projected", per=2, credit=2)
        sig = s.flag("sigmoids_done", per=2, credit=2)
        gated = s.flag("gated", per=2, credit=2)
        stored = s.flag("stored", per=16, credit=16)
        steps = s.sem("dve_steps")
        yv = d["y"].rearrange("(j g) p s c -> j (g p) (s c)", j=KC)
        glu = a["w_glu"].rearrange("(k p) n -> p k n", p=P)
        win = a["w_in_even"].rearrange("(k p) n -> p k n", p=P)
        with nc.Block() as block:
            @block.sync
            def _(sp):
                for j in range(KC):
                    if j >= 2:
                        sp.wait_ge(gelu, j - 1)
                    sp.dma_start(yin[:, j % 2, :, :], yv[j]).then_inc(yl[j % 2], 16)
                with sp.Fori(0, KC) as i:
                    weight_loads(sp, i, mm, [w[:, 0, :, :], w[:, 1, :, :]], wl,
                                 [glu[:, :, bass.ds(i * P, P)], win[:, :, bass.ds(i * P + GB0, P)]])

            @block.tensor
            def _(pe):
                mm.start(pe)
                pe.wait_ge(gelu, KC)
                with pe.Fori(0, KC) as i:
                    for b, x in enumerate((y, h)):
                        pe.wait_ge(wl[b], i * 16 + 16)
                        gated.wait(pe, i, b - 1)
                        product(nc, reg[b], w[:, b], lambda k, o, n: x[:, k, o:o + n], KC).then_inc(mm.sem, 1)

            @block.scalar
            def _(act):
                sig.start(act)
                stored.start(act)
                for j in range(KC):
                    act.wait_ge(yl[j % 2], 16 * (j // 2 + 1))
                    nc.scalar.activation(y[:, j, :].rearrange("p (c s) -> p s c", s=T), yin[:, j % 2, :, :],
                                         ACT.Gelu_apprx_tanh).then_inc(gelu, 1)
                with act.Fori(0, KC) as i:
                    for b in range(2):
                        mm.wait(act, i, b + 1)
                        gated.wait(act, i, b - 1)
                        if b == 0:
                            col.wait(act, i, 1)
                        nc.scalar.activation(sg[:, b, :], rows_of(reg[b]), ACT.Sigmoid,
                                             **({"bias": bias[:, :]} if b == 0 else {})).then_inc(sig.sem, 1)
                    gated.wait(act, i, 2)
                    act.dma_start(d["cat"][i + KC], t[:, 1, :]).then_inc(stored.sem, 16)
                stored.wait(act, KC, 0)

            @block.vector
            def _(dve):
                gated.start(dve)
                do = Steps(dve, steps)
                with do.loop(KC, 2) as i:
                    sig.wait(dve, i, -1)
                    nc.vector.tensor_copy(bias[:, :], c["cols_a"][:, bass.ds(i + c["b_glu"], 1)]).then_inc(col.sem, 1)
                    sig.wait(dve, i, 1)
                    do(nc.vector.tensor_tensor(t[:, 0, :], sg[:, 0, :],
                                               y[:, bass.ds(i, 1), :].rearrange("p k t -> p (k t)"), ALU.mult))
                    dve.sem_inc(gated.sem, 1)
                    sig.wait(dve, i, 2)
                    do(nc.vector.tensor_tensor(t[:, 0, :], t[:, 0, :], sg[:, 1, :], ALU.mult))
                    stored.wait(dve, i, 0)
                    nc.vector.tensor_tensor(t[:, 1, :], t[:, 0, :], rows_of(reg[1]), ALU.mult).then_inc(gated.sem, 1)


SCALE = HD ** -0.5


def attention(nc, a, c, d, h):
    with stage(nc) as outer:
        kt = outer.sb("k", [P, KV, L])
        vt = outer.sb("v", [P, NT, KV * HD])
        rope = outer.sb("rope", [P, 2, L])
        swap = outer.sb("swap", [P, P])
        qk_side(nc, a, c, h, kt, vt, rope, swap)
        heads(nc, a, c, d, h, kt, vt, rope, swap)


def qk_side(nc, a, c, h, kt, vt, rope, swap):
    with stage(nc) as s:
        w = s.sb("w", [P, KV, KC, P])
        wv = s.sb("w_v", [P, KC, KV * HD])
        kg, sq = s.sb("kg", [P, L]), s.sb("sq", [P, L])
        rs, tm = s.sb("rs", [P, L]), s.sb("tm", [P, L])
        reg = [s.ps("k_raw", 1536), s.ps("k_side", 1536)]
        vp = [s.ps(f"v{b}", 512) for b in range(2)]
        load = s.sem("loaded")
        mm, qg_ready, ss, sw = s.sem("projected"), s.sem("gained"), s.sem("squares_summed"), s.sem("swapped")
        root, side_free, k_done = s.sem("root"), s.sem("side_free"), s.sem("k_done")
        vmm, vcop = s.sem("v_projected"), s.sem("v_copied")
        steps = s.sem("dve_steps")
        win = a["w_in_even"].rearrange("(k p) n -> p k n", p=P)
        with nc.Block() as block:
            @block.sync
            def _(sp):
                for n in range(KV):
                    sp.dma_start(w[:, n, :, :], win[:, :, K0 + n * P:K0 + (n + 1) * P]).then_inc(load, 16)
                sp.dma_start(wv[:, :, :], win[:, :, V0:V0 + KV * HD]).then_inc(load, 16)
                sp.dma_start(rope[:, :, :], a["rope"]).then_inc(load, 16)
                sp.dma_start(swap[:, :], a["swap"]).then_inc(load, 16)

            @block.tensor
            def _(pe):
                pe.wait_ge(load, 16 * 5)
                for n in range(KV):
                    if n:
                        pe.wait_ge(qg_ready, 2 * n)
                    product(nc, reg[0], w[:, n], lambda k, o, m: h[:, k, o:o + m], KC).then_inc(mm, 1)
                    pe.wait_ge(qg_ready, 2 * n + 2)
                    if n:
                        pe.wait_ge(side_free, 2 * n)
                    for off, m in PIECES:
                        last = nc.tensor.matmul(reg[1][:, PO + off:PO + off + m], c["ones"][:, :],
                                                sq[:, off:off + m], start=True, stop=True)
                    last.then_inc(ss, 1)
                    pe.wait_ge(side_free, 2 * n + 1)
                    for off, m in PIECES:
                        last = nc.tensor.matmul(reg[1][:, PO + off:PO + off + m], swap[:, :],
                                                kg[:, off:off + m], start=True, stop=True)
                    last.then_inc(sw, 1)
                for n, (off, m) in enumerate(TILES):
                    if n >= 2:
                        pe.wait_ge(vcop, n - 1)
                    for k in range(KC):
                        last = nc.tensor.matmul(vp[n % 2][0:m, 0:KV * HD], h[:, k, off:off + m], wv[:, k, :],
                                                start=(k == 0), stop=(k == KC - 1))
                    last.then_inc(vmm, 1)

            @block.scalar
            def _(act):
                for n in range(KV):
                    act.wait_ge(mm, n + 1)
                    if n:
                        act.wait_ge(k_done, n)
                    nc.scalar.activation(kg[:, :], rows_of(reg[0]), ACT.Copy,
                                         scale=c["col"]("k_norm", 0)).then_inc(qg_ready, 1)
                    nc.scalar.activation(sq[:, :], rows_of(reg[0]), ACT.Square).then_inc(qg_ready, 1)
                    act.wait_ge(ss, n + 1)
                    nc.scalar.activation(rs[:, :], rows_of(reg[1]), ACT.Sqrt, bias=c["eps"][:, :],
                                         scale=1.0 / HD).then_inc(side_free, 1)
                for n, (off, m) in enumerate(TILES):
                    act.wait_ge(vmm, n + 1)
                    nc.scalar.activation(vt[0:m, n, :], vp[n % 2][0:m, 0:KV * HD], ACT.Copy).then_inc(vcop, 1)

            @block.vector
            def _(dve):
                do = Steps(dve, steps)
                for n in range(KV):
                    dve.wait_ge(side_free, 2 * n + 1)
                    do(nc.vector.reciprocal(rs[:, :], rs[:, :]))
                    do(nc.vector.tensor_tensor(kt[:, n, :], kg[:, :], rope[:, 0, :], ALU.mult))
                    dve.wait_ge(sw, n + 1)
                    do(nc.vector.tensor_tensor(tm[:, :], rows_of(reg[1]), rope[:, 1, :], ALU.mult))
                    dve.sem_inc(side_free, 1)
                    do(nc.vector.tensor_tensor(kt[:, n, :], kt[:, n, :], tm[:, :], ALU.add))
                    do(nc.vector.tensor_tensor(kt[:, n, :], kt[:, n, :], rs[:, :], ALU.mult))
                    dve.sem_inc(k_done, 1)


def heads(nc, a, c, d, h, kt, vt, rope, swap):
    REP = HEADS // KV
    NQ = len(QT)
    with stage(nc) as s:
        w = s.sb("w", [P, 2, KC, P])
        qg, sq, rs, tm = (s.sb(n, [P, L]) for n in ("qg", "sq", "rs", "tm"))
        q = s.sb("q", [P, L])
        gate = s.sb("gate", [P, L])
        prob = s.sb("prob", [P, 2, L])
        pt = s.sb("prob_t", [P, 2, NT, P])
        y = s.sb("y", [P, L])
        mx, sm = s.sb("mx", [P, 2, 2]), s.sb("sm", [P, 2, 2])
        sreg, treg = s.ps("scores", 1536), s.ps("turned", 1536)
        op = [s.ps(f"o{b}", 512) for b in range(2)]
        wl = [s.sem("wq_loaded"), s.sem("wg_loaded")]
        mmq = s.flag("q_projected", per=2, credit=2)
        mmg = s.flag("gate_projected", per=2, credit=2)
        gained = s.flag("q_gained", per=4)
        ss = s.flag("squares_summed", per=2)
        root = s.flag("root_done", per=2)
        sw = s.flag("swapped", per=2)
        q_done = s.flag("q_ready", per=2)
        sig = s.flag("sigmoid_done", per=2)
        gate_done = s.flag("gate_ready", per=2, credit=2)
        sc = s.flag("scores_done", per=2 * NQ)
        mxd = s.flag("max_done", per=2 * NQ)
        ex = s.flag("exp_done", per=2 * NQ)
        nd = s.flag("normalised", per=2 * NQ)
        tu = s.flag("prob_turned", per=2 * NQ)
        tc = s.flag("turned_copied", per=2 * NQ * 2, credit=4)
        pv = s.flag("mixed", per=2 * NQ, credit=4)
        yd = s.flag("y_ready", per=2 * NQ, credit=2)
        stored = s.flag("stored", per=32, credit=16)
        steps = s.sem("dve_steps")
        win = a["w_in_even"].rearrange("(k p) n -> p k n", p=P)
        tview = treg[:, :].rearrange("p (b n) -> p b n", b=3)[:, :, 0:3 * P].rearrange("p b (k q) -> p b k q", k=3)
        with nc.Block() as block:
            @block.sync
            def _(sp):
                with sp.Fori(0, REP) as i:
                    for g in range(KV):
                        mmq.wait(sp, i, g)
                        sp.dma_start(w[:, 0, :, :], win[:, :, bass.ds(i * P + (Q0 + g * REP * HD), P)]).then_inc(wl[0], 16)
                        mmg.wait(sp, i, g)
                        sp.dma_start(w[:, 1, :, :], win[:, :, bass.ds(i * P + (GA0 + g * REP * HD), P)]).then_inc(wl[1], 16)

            @block.tensor
            def _(pe):
                mmg.start(pe)
                mmq.start(pe)
                pv.start(pe)
                with pe.Fori(0, REP) as i:
                    for g in range(KV):
                        hx = lambda k, o, n: h[:, k, o:o + n]
                        pe.wait_ge(wl[0], i * 32 + (g * 16 + 16))
                        tc.wait(pe, i, 2 * NQ * g)
                        product(nc, sreg, w[:, 0], hx, KC).then_inc(mmq.sem, 1)
                        gained.wait(pe, i, 2 * g + 2)
                        for off, n in PIECES:
                            last = nc.tensor.matmul(treg[:, PO + off:PO + off + n], c["ones"][:, :],
                                                    sq[:, off:off + n], start=True, stop=True)
                        last.then_inc(ss.sem, 1)
                        for off, n in PIECES:
                            last = nc.tensor.matmul(sreg[:, PO + off:PO + off + n], swap[:, :],
                                                    qg[:, off:off + n], start=True, stop=True)
                        last.then_inc(sw.sem, 1)
                        pe.wait_ge(wl[1], i * 32 + (g * 16 + 16))
                        root.wait(pe, i, g + 1)
                        product(nc, treg, w[:, 1], hx, KC).then_inc(mmg.sem, 1)

                        def scores(t):
                            off, m = QT[t]
                            for o, n in PIECES:
                                last = nc.tensor.matmul(sreg[0:m, PO + o:PO + o + n], q[:, off:off + m],
                                                        kt[:, g, o:o + n], start=True, stop=True)
                            last.then_inc(sc.sem, 1)

                        def turn(t):
                            off, m = QT[t]
                            for k, (ko, kn) in enumerate(TILES):
                                last = nc.tensor.transpose(tview[0:kn, k // 3, k % 3, 0:m],
                                                           prob[0:m, (g * NQ + t) % 2, ko:ko + kn], c["ident"][0:m, 0:m])
                            last.then_inc(tu.sem, 1)

                        def mix(t):
                            off, m = QT[t]
                            for k, (ko, kn) in enumerate(TILES):
                                last = nc.tensor.matmul(op[(g * NQ + t) % 2][:, 0:m], vt[0:kn, k, g * HD:(g + 1) * HD],
                                                        pt[0:kn, (g * NQ + t) % 2, k, 0:m], start=(k == 0), stop=(k == NT - 1))
                            last.then_inc(pv.sem, 1)

                        q_done.wait(pe, i, g + 1)
                        scores(0)
                        gate_done.wait(pe, i, g + 1)
                        for t in range(NQ):
                            n = g * NQ + t
                            if t + 1 < NQ:
                                ex.wait(pe, i, n + 1)
                                scores(t + 1)
                            if t:
                                tc.wait(pe, i, 2 * n)
                                yd.wait(pe, i, n - 2)
                                mix(t - 1)
                            nd.wait(pe, i, n + 1)
                            turn(t)
                        tc.wait(pe, i, 2 * (g + 1) * NQ)
                        yd.wait(pe, i, (g + 1) * NQ - 2)
                        mix(NQ - 1)

            @block.scalar
            def _(act):
                stored.start(act)
                with act.Fori(0, REP) as i:
                    for g in range(KV):
                        mmq.wait(act, i, g + 1)
                        nc.scalar.activation(qg[:, :], rows_of(sreg), ACT.Copy,
                                             scale=c["col"]("q_norm", 0)).then_inc(gained.sem, 1)
                        nc.scalar.activation(sq[:, :], rows_of(sreg), ACT.Square).then_inc(gained.sem, 1)
                        ss.wait(act, i, g + 1)
                        nc.scalar.activation(rs[:, :], rows_of(treg), ACT.Sqrt, bias=c["eps"][:, :],
                                             scale=1.0 / HD).then_inc(root.sem, 1)
                        mmg.wait(act, i, g + 1)
                        nc.scalar.activation(gate[:, :], rows_of(treg), ACT.Sigmoid).then_inc(sig.sem, 1)

                        def copied(t):
                            off, m = QT[t]
                            nc.scalar.activation(pt[:, (g * NQ + t) % 2, 0:3, 0:m], tview[:, 0, :, 0:m], ACT.Copy)
                            return nc.scalar.activation(pt[:, (g * NQ + t) % 2, 3:6, 0:m], tview[:, 1, :, 0:m], ACT.Copy)

                        for t in range(NQ + 1):
                            n = g * NQ + t
                            if t < NQ:
                                off, m = QT[t]
                                mxd.wait(act, i, n + 1)
                                if t >= 2:
                                    tu.wait(act, i, n - 1)
                                nc.scalar.activation(prob[0:m, (g * NQ + t) % 2, :], rows_of(sreg)[0:m], ACT.Exp,
                                                     bias=mx[0:m, (g * NQ + t) % 2, 1:2], scale=SCALE,
                                                     accum_out=sm[0:m, (g * NQ + t) % 2, 0:1]).then_inc(ex.sem, 1)
                            if t:
                                tu.wait(act, i, n)
                                pv.wait(act, i, n - 2)
                                copied(t - 1).then_inc(tc.sem, 1)
                        yd.wait(act, i, (g + 1) * NQ)
                        act.dma_start(d["cat"][i + g * REP], y[:, :]).then_inc(stored.sem, 16)
                stored.wait(act, REP, 0)

            @block.vector
            def _(dve):
                v = nc.vector
                for x in (gate_done, yd, tc):
                    x.start(dve)
                do = Steps(dve, steps)
                with do.loop(REP, 2 * (5 + 1 + 2 * NQ)) as i:
                    for g in range(KV):
                        root.wait(dve, i, g + 1)
                        do(v.reciprocal(rs[:, :], rs[:, :]))
                        do(v.tensor_tensor(q[:, :], qg[:, :], rope[:, 0, :], ALU.mult))
                        sw.wait(dve, i, g + 1)
                        do(v.tensor_tensor(tm[:, :], rows_of(sreg), rope[:, 1, :], ALU.mult))
                        do(v.tensor_tensor(q[:, :], q[:, :], tm[:, :], ALU.add))
                        do(v.tensor_tensor(q[:, :], q[:, :], rs[:, :], ALU.mult))
                        dve.sem_inc(q_done.sem, 1)
                        sig.wait(dve, i, g + 1)
                        do(v.tensor_tensor(gate[:, :], gate[:, :], rows_of(treg), ALU.mult))
                        dve.sem_inc(gate_done.sem, 1)
                        stored.wait(dve, i, 16 * g)
                        for t in range(NQ + 1):
                            n = g * NQ + t
                            if t < NQ:
                                off, m = QT[t]
                                sc.wait(dve, i, n + 1)
                                do(v.tensor_reduce(mx[0:m, (g * NQ + t) % 2, 0:1], rows_of(sreg)[0:m], AX, ALU.max))
                                v.tensor_scalar(mx[0:m, (g * NQ + t) % 2, 1:2], mx[0:m, (g * NQ + t) % 2, 0:1], -SCALE, None,
                                                ALU.mult).then_inc(mxd.sem, 1)
                            if t:
                                off, m = QT[t - 1]
                                tu.wait(dve, i, n)
                                pv.wait(dve, i, n - 2)
                                v.tensor_copy(pt[:, (g * NQ + t - 1) % 2, 6:8, 0:m], tview[:, 2, 0:2, 0:m])
                                v.tensor_copy(pt[0:TILES[-1][1], (g * NQ + t - 1) % 2, 8, 0:m],
                                              tview[0:TILES[-1][1], 2, 2, 0:m]).then_inc(tc.sem, 1)
                            if t < NQ:
                                off, m = QT[t]
                                ex.wait(dve, i, n + 1)
                                do(v.reciprocal(sm[0:m, (g * NQ + t) % 2, 1:2], sm[0:m, (g * NQ + t) % 2, 0:1]))
                                v.tensor_scalar(prob[0:m, (g * NQ + t) % 2, :], prob[0:m, (g * NQ + t) % 2, :], sm[0:m, (g * NQ + t) % 2, 1:2], None,
                                                ALU.mult).then_inc(nd.sem, 1)
                            if t:
                                off, m = QT[t - 1]
                                pv.wait(dve, i, n)
                                v.tensor_tensor(y[:, off:off + m], op[(g * NQ + t - 1) % 2][:, 0:m], gate[:, off:off + m],
                                                ALU.mult).then_inc(yd.sem, 1)


def project_out(nc, w_out, cat, c, d, h, layer, out):
    with stage(nc) as s0:
        y = s0.sb("y", [P, KC, L])
        with stage(nc) as s:
            x = s.sb("x", [P, 2 * KC, L])
            w = s.sb("w", [P, 2, 2 * KC, P])
            reg = [s.ps(f"r{b}", 1536) for b in range(2)]
            xl = s.sem("x_loaded")
            wl = [s.sem(f"w_loaded{b}") for b in range(2)]
            mm = s.flag("projected", per=2, credit=2)
            cop = s.flag("copied", per=2, credit=2)
            wv = w_out.rearrange("(k p) n -> p k n", p=P)
            with nc.Block() as block:
                @block.sync
                def _(sp):
                    mm.start(sp)
                    with sp.Fori(0, KC // 2) as i:
                        weight_loads(sp, i, mm, [w[:, b, :, :] for b in range(2)], wl,
                                     [wv[:, :, bass.ds(i * 256 + b * P, P)] for b in range(2)])

                @block.tensor
                def _(pe):
                    pe.wait_ge(xl, 16 * 2 * KC)
                    with pe.Fori(0, KC // 2) as i:
                        for b in range(2):
                            pe.wait_ge(wl[b], i * 16 + 16)
                            cop.wait(pe, i, b - 1)
                            product(nc, reg[b], w[:, b], lambda k, o, n: x[:, k, o:o + n],
                                    2 * KC).then_inc(mm.sem, 1)

                @block.scalar
                def _(act):
                    cop.start(act)
                    for k in range(2 * KC):
                        act.dma_start(x[:, k, :], cat[k]).then_inc(xl, 16)
                    with act.Fori(0, KC // 2) as i:
                        for b in range(2):
                            mm.wait(act, i, b + 1)
                            nc.scalar.activation(y[:, bass.ds(i * 2 + b, 1), :].rearrange("p k t -> p (k t)"),
                                                 rows_of(reg[b]), ACT.Copy).then_inc(cop.sem, 1)
        res = s0.sb("res", [P, KC, L])
        norm_block(nc, c, y, res, lambda k: c["col"]("norm_post", KC * layer + k), resid=d["res"],
                   save=d["res"] if out is None else None)
        if out is None:
            norm_block(nc, c, res, h, lambda k: c["col"]("norm_pre", KC * (layer + 1) + k))
        else:
            leave(nc, c, res, out)


def leave(nc, c, res, out):
    with stage(nc) as s:
        ot = s.sb("ot", [P, 2, D])
        pt = [s.ps(f"pt{b}", 512) for b in range(4)]
        turned, copied, stored = s.sem("turned"), s.sem("copied"), [s.sem("stored0"), s.sem("stored1")]
        n_tiles = (L - META) // P
        with nc.Block() as block:
            @block.tensor
            def _(pe):
                for i in range(n_tiles):
                    for half in range(2):
                        n = 2 * i + half
                        if n >= 4:
                            pe.wait_ge(copied, n - 3)
                        for k in range(4):
                            last = nc.tensor.transpose(pt[n % 4][:, k * P:(k + 1) * P],
                                                       res[:, 4 * half + k, META + i * P:META + (i + 1) * P],
                                                       c["ident"][:, :])
                        last.then_inc(turned, 1)

            @block.vector
            def _(dve):
                for n in range(2 * n_tiles):
                    i = n // 2
                    dve.wait_ge(turned, n + 1)
                    if i >= 2 and n % 2 == 0:
                        dve.wait_ge(stored[i % 2], 16 * (i // 2))
                    nc.vector.tensor_copy(ot[:, i % 2, 512 * (n % 2):512 * (n % 2) + 512],
                                          pt[n % 4][:, :]).then_inc(copied, 1)

            @block.sync
            def _(sp):
                for i in range(n_tiles):
                    sp.wait_ge(copied, 2 * i + 2)
                    sp.dma_start(out[i * P:(i + 1) * P, :], ot[:, i % 2, :]).then_inc(stored[i % 2], 16)
                for b in range(2):
                    sp.wait_ge(stored[b], 16 * n_tiles // 2)


def conv_and_values(nc, a, c, d, h, xc):
    EDGE = CONV // 2
    with stage(nc) as s:
        w = s.sb("w", [P, 2, KC, P])
        wv = s.sb("w_v", [P, 2, MV])
        xm = s.sb("xm", [P, 2, L + 2 * EDGE])
        acc, sg = s.sb("acc", [P, 2, L]), s.sb("sg", [P, 2, L])
        vs = s.sb("vs", [P, NT, MV])
        reg = [s.ps(f"r{b}", 1536) for b in range(2)]
        vp = [s.ps(f"v{b}", 512) for b in range(2)]
        wl = [s.sem(f"w_loaded{b}") for b in range(2)]
        wvl = s.sem("wv_loaded")
        mm = s.flag("projected", per=2, credit=2)
        cop = s.flag("xm_copied", per=2, credit=2)
        vmm = s.flag("v_projected", per=NT, credit=NT)
        vcop = s.flag("v_copied", per=NT, credit=NT)
        conv = s.flag("convolved", per=2, credit=2)
        sig = s.flag("sigmoid_done", per=2)
        act_done = s.flag("xc_done", per=2, credit=2)
        stored = s.flag("v_stored", per=16, credit=16)
        steps = s.sem("dve_steps")
        win = a["w_in_odd"].rearrange("(k p) n -> p k n", p=P)
        wvv = a["w_v"].rearrange("h (c p) n -> h p c n", p=P)
        with nc.Block() as block:
            @block.sync
            def _(sp):
                with sp.Fori(0, MH) as i:
                    weight_loads(sp, i, mm, [w[:, b, :, :] for b in range(2)], wl,
                                 [win[:, :, bass.ds(i * 256 + b * P, P)] for b in range(2)])
                    vmm.wait(sp, i, 0)
                    sp.dma_start(wv[:, :, :], wvv[i]).then_inc(wvl, 16)

            @block.tensor
            def _(pe):
                mm.start(pe)
                vmm.start(pe)
                with pe.Fori(0, MH) as i:
                    for b in range(2):
                        pe.wait_ge(wl[b], i * 16 + 16)
                        cop.wait(pe, i, b - 1)
                        product(nc, reg[b], w[:, b], lambda k, o, n: h[:, k, o:o + n], KC).then_inc(mm.sem, 1)
                    pe.wait_ge(wvl, i * 16 + 16)
                    cop.wait(pe, i, 2)
                    for t, (off, m) in enumerate(TILES):
                        vcop.wait(pe, i, t - 1)
                        for b in range(2):
                            last = nc.tensor.matmul(vp[t % 2][0:m, 0:MV], xm[:, b, EDGE + off:EDGE + off + m],
                                                    wv[:, b, :], start=(b == 0), stop=(b == 1))
                        last.then_inc(vmm.sem, 1)
                    vcop.wait(pe, i, NT)

            @block.scalar
            def _(act):
                cop.start(act)
                vcop.start(act)
                stored.start(act)
                with act.Fori(0, MH) as i:
                    for b in range(2):
                        mm.wait(act, i, b + 1)
                        conv.wait(act, i, b - 1)
                        vmm.wait(act, i, 0)
                        nc.scalar.activation(xm[:, b, EDGE:EDGE + L], rows_of(reg[b]), ACT.Copy).then_inc(cop.sem, 1)
                    stored.wait(act, i, 0)
                    for t, (off, m) in enumerate(TILES):
                        vmm.wait(act, i, t + 1)
                        nc.scalar.activation(vs[0:m, t, :], vp[t % 2][0:m, 0:MV], ACT.Copy).then_inc(vcop.sem, 1)
                    vcop.wait(act, i, NT)
                    act.dma_start(d["v"][i], vs[:, :, :]).then_inc(stored.sem, 16)
                    for b in range(2):
                        conv.wait(act, i, b + 1)
                        act_done.wait(act, i, b - 1)
                        nc.scalar.activation(sg[:, b, :], acc[:, b, :], ACT.Sigmoid).then_inc(sig.sem, 1)
                stored.wait(act, MH, 0)

            @block.vector
            def _(dve):
                do = Steps(dve, steps)
                do.free(nc.vector.memset(vs[:, NT - 1, :], 0.0))
                for b in range(2):
                    do.free(nc.vector.memset(xm[:, b, 0:EDGE], 0.0))
                    do(nc.vector.memset(xm[:, b, EDGE + L:], 0.0))
                conv.start(dve)
                act_done.start(dve)
                with do.loop(MH, 2 * (CONV - 1)) as i:
                    for b in range(2):
                        cop.wait(dve, i, b + 1)

                        def tap(n, b=b):
                            return c["conv_w"][:, bass.ds(i * 2 + (n * 2 * KC + b), 1)]
                        act_done.wait(dve, i, b - 1)
                        do(nc.vector.tensor_scalar(acc[:, b, :], xm[:, b, 0:L], tap(0),
                                                   c["cols_a"][:, bass.ds(i * 2 + (c["conv_b"] + b), 1)],
                                                   ALU.mult, ALU.add))
                        for n in range(1, CONV):
                            ins = nc.vector.scalar_tensor_tensor(acc[:, b, :], xm[:, b, n:n + L], tap(n),
                                                                 acc[:, b, :], ALU.mult, ALU.add)
                            if n < CONV - 1:
                                do(ins)
                        ins.then_inc(conv.sem, 1)
                    for b in range(2):
                        sig.wait(dve, i, b + 1)
                        nc.vector.tensor_tensor(xc[:, bass.ds(i * 2 + b, 1), :].rearrange("p k t -> p (k t)"),
                                                acc[:, b, :], sg[:, b, :], ALU.mult).then_inc(act_done.sem, 1)


def gate_rows(nc, a, c, d, xc, cols):
    R = 40
    F, B = slice(0, MH), slice(32, 40)
    with stage(nc) as s:
        wg = s.sb("wg", [P, 2 * KC, 104])
        bias = s.sb("bias", [P, 1])
        keep = s.sb("keep", [R, L])
        li, lf, fx, e1, mn = (s.sb(n, [R, L]) for n in ("li", "lf", "fx", "e1", "mn"))
        b_, m_ = s.sb("b", [R, L]), s.sb("m", [R, L])
        bn, m_n, ln = s.sb("bn", [R, L]), s.sb("mn2", [R, L]), s.sb("ln", [R, L])
        row = s.sb("row", [R, 3, L])
        bm = s.sb("bm", [R, L])
        end = s.sb("end", [R, 6, NT])
        ends = s.sb("ends", [R, 2, NT])
        reg = s.ps("gates", 1536)
        tp = [s.ps(f"tp{q}", 512) for q in range(3)]
        load, cleared = s.sem("loaded"), s.sem("cleared")
        wld = s.sem("weights_loaded")
        mm, raw = s.sem("projected"), s.sem("raw_copied")
        asked, answered = s.sem("function_asked"), s.sem("function_done")
        rows, turned, stored = s.sem("rows_ready"), s.sem("turned"), s.sem("stored")
        steps, asteps = s.sem("dve_steps"), s.sem("act_steps")
        with nc.Block() as block:
            @block.sync
            def _(sp):
                sp.dma_start(keep[:, :], a["starts"]).then_inc(load, 16)
                sp.wait_ge(cleared, 2)
                for n, name in enumerate(("igate", "fgate")):
                    for r in range(2):
                        at = 64 * n + 32 * r
                        sp.dma_start(wg[:, :, at:at + MH],
                                     a["w_" + name][r].rearrange("(k p) h -> p k h", p=P)).then_inc(wld, 16)
                        sp.dma_start(bias[at:at + MH, :], a["b_" + name][r].unsqueeze(1)).then_inc(wld, 16)
                sp.wait_ge(rows, 1)
                for r, part in enumerate((F, B)):
                    sp.dma_start(d["bm"][r], bm[part, :]).then_inc(stored, 16)
                    sp.dma_start(d["ends"][r], ends[part, :, :]).then_inc(stored, 16)
                sp.wait_ge(stored, 64)

            @block.tensor
            def _(pe):
                pe.wait_ge(wld, 16 * 8)
                for k in range(2 * KC):
                    for off, n in PIECES:
                        last = nc.tensor.matmul(reg[0:104, PO + off:PO + off + n], wg[:, k, :], xc[:, k, off:off + n],
                                                start=(k == 0), stop=(k == 2 * KC - 1))
                last.then_inc(mm, 1)
                pe.wait_ge(rows, 1)
                for q in range(3):
                    for t, (off, m) in enumerate(TILES):
                        last = nc.tensor.transpose(tp[q][0:m, R * t:R * t + R], row[:, q, off:off + m],
                                                   c["ident"][0:R, 0:R])
                    last.then_inc(turned, 1)

            @block.scalar
            def _(act):
                act.wait_ge(mm, 1)
                act.wait_ge(cleared, 2)
                g = rows_of(reg)
                n = 0
                for dst, at in ((li, 0), (fx, 64)):
                    nc.scalar.activation(dst[F, :], g[at:at + MH], ACT.Identity, bias=bias[at:at + MH, :])
                    nc.scalar.activation(dst[B, :], g[at + 32:at + 32 + MH, ::-1], ACT.Identity,
                                         bias=bias[at + 32:at + 32 + MH, :]).then_inc(raw, 1)
                act.wait_ge(raw, 2)
                do = Steps(act, asteps)
                do(nc.scalar.activation(e1[:, :], fx[:, :], ACT.Abs))
                do(nc.scalar.activation(e1[:, :], e1[:, :], ACT.Exp, scale=-1.0))
                nc.scalar.activation(lf[:, :], e1[:, :], ACT.Ln, bias=1.0).then_inc(raw, 1)
                act.wait_ge(asked, 1)
                nc.scalar.activation(row[:, 1, :], row[:, 1, :], ACT.Exp)
                nc.scalar.activation(row[:, 2, :], m_n[:, :], ACT.Exp, scale=-1.0)
                nc.scalar.activation(ends[:, 1, :], end[:, 4, :], ACT.Exp).then_inc(answered, 1)

            @block.vector
            def _(dve):
                v = nc.vector
                do = Steps(dve, steps)
                v.memset(wg[:, :, :], 0.0).then_inc(cleared, 1)
                for x in (li, fx, bn, m_n, ln):
                    do.free(v.memset(x[:, :], 0.0))
                do.free(v.memset(end[:, :, :], 0.0))
                do(v.memset(cols[:, NT - 1, :, :], 0.0))
                dve.sem_inc(cleared, 1)
                dve.wait_ge(load, 16)
                dve.wait_ge(raw, 3)
                do(v.tensor_scalar(mn[:, :], fx[:, :], 0.0, None, ALU.min))
                do(v.tensor_tensor(lf[:, :], mn[:, :], lf[:, :], ALU.subtract))
                do.free(v.tensor_tensor_scan(b_[:, :], keep[:, :], lf[:, :], 0.0, ALU.mult, ALU.add))
                do(v.tensor_tensor_scan(m_[:, :], lf[:, :], li[:, :], 0.0, ALU.add, ALU.max))
                for dst, src in ((bn, b_), (m_n, m_), (ln, li)):
                    do.free(v.tensor_copy(dst[F, :], src[F, :]))
                    do(v.tensor_copy(dst[B, :], src[B, ::-1]))
                N = NT - 1
                for q, src in ((0, bn), (1, m_n)):
                    do.free(v.tensor_copy(end[F, q, 0:N], src[F, P - 1:N * P:P]))
                    do.free(v.tensor_copy(end[F, q, N:NT], src[F, L - 1:L]))
                    do(v.tensor_copy(end[B, q, 0:NT], src[B, 0:L:P]))
                do.free(v.tensor_copy(end[F, 2, 1:NT], end[F, 1, 0:N]))
                do(v.tensor_copy(end[B, 2, 0:N], end[B, 1, 1:NT]))
                do(v.tensor_copy(ends[:, 0, :], end[:, 2, :]))
                do(v.tensor_tensor(end[:, 3, :], end[:, 0, :], end[:, 1, :], ALU.subtract))
                do(v.tensor_tensor(end[:, 4, :], end[:, 3, :], end[:, 2, :], ALU.add))
                do(v.tensor_tensor(row[:, 0, :], ln[:, :], bn[:, :], ALU.subtract))
                do(v.tensor_tensor(bm[:, :], bn[:, :], m_n[:, :], ALU.subtract))
                for t, (off, m) in enumerate(TILES):
                    do(v.tensor_scalar(row[:, 1, off:off + m], row[:, 0, off:off + m], end[:, 3, t:t + 1], None, ALU.add))
                dve.sem_inc(asked, 1)
                dve.wait_ge(answered, 1)
                dve.sem_inc(rows, 1)
                for q in range(3):
                    dve.wait_ge(turned, q + 1)
                    view = tp[q][:, 0:R * NT].rearrange("p (t r) -> p t r", r=R)
                    v.tensor_copy(cols[:, 0:N, q, :], view[:, 0:N, :])
                    v.tensor_copy(cols[0:TILES[N][1], N, q, :], view[0:TILES[N][1], N, :])


def mlstm(nc, a, c, d, h, xc, cols):
    LS, WS, FLOOR = 0, 1, 2
    N = NT - 1
    VW = MV + 1
    FILL = {0: (0, 0, 4), 1: (0, 4, 7), 2: (0, 7, 10), 3: (0, 10, 13), 4: (0, 13, 16),
            6: (1, 0, 4), 7: (1, 4, 7), 8: (1, 7, 10), 9: (1, 10, 13), 10: (1, 13, 16),
            12: (2, 0, 4), 13: (2, 4, 8), 15: (3, 0, 4), 16: (3, 4, 8)}
    with stage(nc) as s:
        wqk = s.sb("w_qk", [P, 2, 2, MK])
        wo = s.sb("w_o", [P, 2, 2 * KC, P])
        wz = s.sb("w_z", [P, 2, KC, P])
        masks = s.sb("masks", [P, 2, P])
        v1 = s.sb("v1", [P, NT, VW])
        bmb = s.sb("bm_b", [P, 2, L])
        endb = s.sb("ends_b", [P, 2, MH, 2, NT])
        qT, kT = s.sb("qT", [P, L]), s.sb("kT", [P, L])
        kt = s.sb("kt", [P, NT, MK])
        kw = s.sb("kw", [P, 2, MK])
        cb, cf = s.sb("state_b", [P, N, VW]), s.sb("state_f", [P, 2, VW])
        D_, qe = s.sb("D", [P, 2, P]), s.sb("qe", [P, 2, P])
        sw, qs = s.sb("sw", [P, 2, P]), s.sb("qs", [P, 2, P])
        dn, rd = s.sb("dn", [P, 2]), s.sb("rd", [P, 2])
        hf, hs = s.sb("hf", [P, MV]), s.sb("hs", [P, NT, MV])
        sq, ssq, rstd = s.sb("sq", [P, MV]), s.sb("ssq", [P, NT]), s.sb("rstd", [P, NT])
        og, zs = s.sb("og", [P, 2, L]), s.sb("zs", [P, 2, L])
        psum = s.ps("psum", 4096)
        A, B = psum[:, 0:1536], psum[:, 1536:3072]
        kq = [psum[:, 0:512], psum[:, 3584:4096]]
        ub, hfb, hbb = psum[:, 512:1024], psum[:, 1024:1536], psum[:, 3072:3584]
        once, ones_set = s.sem("once_loaded"), s.sem("ones_set")
        wql, wol, wzl, vl, bl = (s.sem(n) for n in ("wqk_loaded", "wo_loaded", "wz_loaded", "v_loaded", "bm_loaded"))
        wol2, wzl2 = s.sem("wo2_loaded"), s.sem("wz2_loaded")
        qk = s.flag("qk_projected", per=2, credit=2)
        qkc = s.flag("qk_copied", per=2)
        ktt = s.flag("k_turned")
        ktc = s.flag("kt_copied")
        fill = s.flag("filled", per=4, credit=4)
        sig = s.flag("sigmoids_done", per=4)
        zdone = s.flag("z_done", per=2, credit=2)
        kwd = s.flag("kw_ready", per=2 * N)
        um = s.flag("update_made", per=2 * N, credit=2)
        us = s.flag("update_added", per=2 * N)
        dd = s.flag("D_ready", per=NT)
        de = s.flag("D_exp_done", per=NT)
        qed = s.flag("qe_done", per=NT)
        kqd = s.flag("kq_done", per=NT)
        swd = s.flag("sw_ready", per=NT)
        qsd = s.flag("qs_ready", per=NT, credit=1)
        hd = s.flag("h_made", per=NT, credit=1)
        rdd = s.flag("den_ready", per=NT)
        hfd = s.flag("hf_done", per=NT)
        hsd = s.flag("hs_done", per=NT, credit=1)
        sqd = s.flag("squares_done", per=NT)
        root = s.flag("root_done")
        hscaled = s.flag("h_scaled")
        turned = s.flag("h_turned", per=2, credit=2)
        gated = s.flag("gated", per=2, credit=2)
        stored = s.flag("stored", per=16, credit=16)
        steps, asteps = s.sem("dve_steps"), s.sem("act_steps")
        win = a["w_in_odd"].rearrange("(k p) n -> p k n", p=P)
        wog = a["w_ogate"].rearrange("(k p) n -> p k n", p=P)
        wqv = [a[n].rearrange("h (c p) n -> h p c n", p=P) for n in ("w_q", "w_k")]
        with nc.Block() as block:
            @block.sync
            def _(sp):
                sp.dma_start(masks[:, :, :], a["masks"]).then_inc(once, 16)
                for r in range(2):
                    sp.dma_start(endb[:, r, :, :, :].rearrange("p h e t -> p (h e t)"),
                                 d["ends"][r].rearrange("h e t -> (h e t)").unsqueeze(0)
                                 .broadcast_to([P, MH * 2 * NT])).then_inc(once, 16)
                sp.wait_ge(ones_set, 1)
                with sp.Fori(0, MH) as i:
                    qk.wait(sp, i, 0)
                    for n in range(2):
                        sp.dma_start(wqk[:, n, :, :], wqv[n][i]).then_inc(wql, 16)
                    hd.wait(sp, i, 0)
                    sp.dma_start(v1[:, :, 0:MV], d["v"][i]).then_inc(vl, 16)
                    qsd.wait(sp, i, 0)
                    sp.dma_start(bmb[:, :, :], d["bm"][:, bass.ds(i, 1), :].rearrange("r h t -> h r t")
                                 .broadcast_to([P, 2, L])).then_inc(bl, 16)
                    for b, sem in enumerate((wol, wol2)):
                        fill.wait(sp, i, b + 1 - 4)
                        sp.dma_start(wo[:, b, :, :], wog[:, :, bass.ds(i * 256 + b * P, P)]).then_inc(sem, 16)
                    for b, sem in enumerate((wzl, wzl2)):
                        fill.wait(sp, i, b + 3 - 4)
                        sp.dma_start(wz[:, b, :, :], win[:, :, bass.ds(i * 256 + (W2 + b * P), P)]).then_inc(sem, 16)

            @block.tensor
            def _(pe):
                for x in (qk, fill, hd, turned, um):
                    x.start(pe)
                pe.wait_ge(ones_set, 1)
                pe.wait_ge(once, 48)
                with pe.Fori(0, MH) as i:
                    def filler(slot):
                        if slot not in FILL:
                            return
                        p, k0, k1 = FILL[slot]
                        w, x, kc = ((wo[:, p], lambda k, o, n: xc[:, k, o:o + n], 2 * KC) if p < 2 else
                                    (wz[:, p - 2], lambda k, o, n: h[:, k, o:o + n], KC))
                        if k0 == 0:
                            pe.wait_ge((wol, wol2, wzl, wzl2)[p], i * 16 + 16)
                            if p == 0:
                                gated.wait(pe, i, 0)
                            elif p < 3:
                                sig.wait(pe, i, p)
                            else:
                                zdone.wait(pe, i, 1)
                        for k in range(k0, k1):
                            for off, n in PIECES:
                                last = nc.tensor.matmul(B[:, PO + off:PO + off + n], w[:, k, :], x(k, off, n),
                                                        start=(k == 0), stop=(k == kc - 1))
                        if k1 == kc:
                            last.then_inc(fill.sem, 1)

                    pe.wait_ge(wql, i * 32 + 32)
                    gated.wait(pe, i, 0)
                    for n, reg in enumerate((A, B)):
                        product(nc, reg, wqk[:, n],
                                lambda k, o, m: xc[:, bass.ds(i * 2 + k, 1), o:o + m].rearrange("p k t -> p (k t)"),
                                2).then_inc(qk.sem, 1)
                    qkc.wait(pe, i, 2)
                    for t, (off, m) in enumerate(TILES):
                        last = nc.tensor.transpose(A[0:m, t * P:(t + 1) * P], kT[:, off:off + m], c["ident"][:, :])
                    last.then_inc(ktt.sem, 1)
                    pe.wait_ge(vl, i * 16 + 16)

                    def update(n, t, b):
                        off, m = TILES[t]
                        kwd.wait(pe, i, n + 1)
                        if n:
                            us.wait(pe, i, n)
                        nc.tensor.matmul(ub[:, 0:VW], kw[0:m, b, :], v1[0:m, t, :],
                                         start=True, stop=True).then_inc(um.sem, 1)

                    def scores(t):
                        off, m = TILES[t]
                        if t >= 2:
                            swd.wait(pe, i, t - 1)
                        nc.tensor.matmul(kq[t % 2][0:m, 0:m], kT[:, off:off + m], qT[:, off:off + m],
                                         start=True, stop=True).then_inc(kqd.sem, 1)

                    ktc.wait(pe, i, 1)
                    for n, t in enumerate(range(N, 0, -1)):
                        update(n, t, n % 2)
                        filler(n)
                    scores(0)
                    for t, (off, m) in enumerate(TILES):
                        if t < N:
                            scores(t + 1)
                            update(N + t, t, (N + t) % 2)
                        filler(N + t)
                        swd.wait(pe, i, t + 1)
                        qsd.wait(pe, i, t + 1)
                        hsd.wait(pe, i, t)
                        if t:
                            us.wait(pe, i, N + t)
                        for r, bank in enumerate((hfb, hbb)):
                            state = cf[:, t % 2, :] if r == 0 else cb[:, min(t, N - 1), :]
                            has = t > 0 if r == 0 else t < N
                            if has:
                                nc.tensor.matmul(bank[0:m, 0:VW], qs[:, r, 0:m], state, start=True, stop=False)
                            last = nc.tensor.matmul(bank[0:m, 0:VW], sw[0:m, r, 0:m], v1[0:m, t, :],
                                                    start=not has, stop=True)
                        last.then_inc(hd.sem, 1)
                    hscaled.wait(pe, i, 1)
                    zdone.wait(pe, i, 2)
                    for b, reg in enumerate((A, B)):
                        for t, (off, m) in enumerate(TILES):
                            last = nc.tensor.transpose(reg[:, off:off + m], hs[0:m, t, b * P:(b + 1) * P],
                                                       c["ident"][0:m, 0:m])
                        last.then_inc(turned.sem, 1)

            @block.scalar
            def _(act):
                stored.start(act)
                act.wait_ge(once, 48)
                with act.Fori(0, MH) as i:
                    qk.wait(act, i, 1)
                    hd.wait(act, i, 0)
                    nc.scalar.activation(qT[:, :], A[:, PO:PO + L], ACT.Copy, scale=MK ** -0.5).then_inc(qkc.sem, 1)
                    qk.wait(act, i, 2)
                    nc.scalar.activation(kT[:, :], B[:, PO:PO + L], ACT.Copy).then_inc(qkc.sem, 1)

                    def sigmoid(p):
                        fill.wait(act, i, p + 1)
                        if p < 2:
                            if p == 0:
                                stored.wait(act, i, 0)
                            nc.scalar.activation(og[:, p, :], B[:, PO:PO + L], ACT.Sigmoid,
                                                 bias=c["cols_a"][:, bass.ds(i * 2 + (c["b_ogate"] + p), 1)]
                                                 ).then_inc(sig.sem, 1)
                        else:
                            if p == 2:
                                gated.wait(act, i, 0)
                            nc.scalar.activation(zs[:, p - 2, :], B[:, PO:PO + L], ACT.Sigmoid).then_inc(sig.sem, 1)

                    sigmoid(0)
                    act.wait_ge(bl, i * 16 + 16)
                    for t in range(NT + 1):
                        if t < NT:
                            off, m = TILES[t]
                            if N + t == 11:
                                sigmoid(1)
                            if N + t == 14:
                                sigmoid(2)
                            if t:
                                qsd.wait(act, i, t)
                            for r in range(2):
                                last = nc.scalar.activation(
                                    qe[:, r, 0:m], bmb[:, r, off:off + m], ACT.Exp,
                                    bias=endb[:, r, bass.ds(i, 1), 0, t:t + 1].rearrange("p h t -> p (h t)"))
                            last.then_inc(qed.sem, 1)
                            dd.wait(act, i, t + 1)
                            nc.scalar.activation(D_[0:m, :, 0:m], D_[0:m, :, 0:m], ACT.Exp).then_inc(de.sem, 1)
                        if t:
                            m = TILES[t - 1][1]
                            rdd.wait(act, i, t)
                            nc.scalar.activation(hf[0:m, :], hfb[0:m, 0:MV], ACT.Copy,
                                                 scale=rd[0:m, 0:1]).then_inc(hfd.sem, 1)
                            hsd.wait(act, i, t)
                            nc.scalar.activation(sq[0:m, :], hs[0:m, t - 1, :], ACT.Square,
                                                 accum_out=ssq[0:m, t - 1:t]).then_inc(sqd.sem, 1)
                    sigmoid(3)
                    sqd.wait(act, i, NT)
                    nc.scalar.activation(rstd[:, :], ssq[:, :], ACT.Sqrt, bias=c["eps"][:, :],
                                         scale=1.0 / MV).then_inc(root.sem, 1)
                    gated.wait(act, i, 2)
                    act.dma_start(d["hh"][bass.ds(i * 2, 2), :, :].rearrange("b p t -> p b t"), og[:, :, :])\
                        .then_inc(stored.sem, 16)
                stored.wait(act, MH, 0)

            @block.vector
            def _(dve):
                v = nc.vector
                do = Steps(dve, steps)
                for x in (zdone, gated, hsd, qsd):
                    x.start(dve)
                v.memset(ssq[:, :], 0.0)
                v.memset(v1[:, :, MV:VW], 1.0).then_inc(ones_set, 1)
                dve.wait_ge(once, 48)
                with do.loop(MH, MLSTM_STEPS) as i:
                    def col(t, q, r, m):
                        return cols[0:m, t, q, bass.ds(i + 32 * r, 1)]

                    def decay(t, r):
                        return endb[:, r, bass.ds(i, 1), 1, t:t + 1].rearrange("p h t -> p (h t)")

                    def weigh(n, t, r):
                        m = TILES[t][1]
                        if n >= 2:
                            um.wait(dve, i, n - 1)
                        v.tensor_scalar(kw[0:m, n % 2, :], kt[0:m, t, :], col(t, WS, r, m), None,
                                        ALU.mult).then_inc(kwd.sem, 1)

                    ktt.wait(dve, i, 1)
                    do.free(v.tensor_copy(kt[:, 0:N, :], A[:, 0:N * MK].rearrange("p (t k) -> p t k", k=MK)))
                    do(v.tensor_copy(kt[0:TILES[N][1], N, :], A[0:TILES[N][1], N * MK:NT * MK]))
                    dve.sem_inc(ktc.sem, 1)
                    weigh(0, N, 1)
                    for n, t in enumerate(range(N, 0, -1)):
                        if n + 1 < N:
                            weigh(n + 1, t - 1, 1)
                        um.wait(dve, i, n + 1)
                        if t == N:
                            do(v.tensor_copy(cb[:, t - 1, :], ub[:, 0:VW]))
                        else:
                            do(v.scalar_tensor_tensor(cb[:, t - 1, :], cb[:, t, :], decay(t, 1), ub[:, 0:VW],
                                                      ALU.mult, ALU.add))
                        dve.sem_inc(us.sem, 1)
                    dve.wait_ge(bl, i * 16 + 16)
                    for t in range(NT + 1):
                        if N + t == 15:
                            sig.wait(dve, i, 3)
                            do(v.tensor_tensor(zs[:, 0, :], zs[:, 0, :], B[:, PO:PO + L], ALU.mult))
                            dve.sem_inc(zdone.sem, 1)
                        if t < NT:
                            off, m = TILES[t]
                            for r in range(2):
                                last = v.scalar_tensor_tensor(D_[0:m, r, 0:m], bmb[0:m, r, off:off + m],
                                                              col(t, LS, r, m), masks[0:m, r, 0:m], ALU.add, ALU.add)
                            last.then_inc(dd.sem, 1)
                            if t < N:
                                weigh(N + t, t, 0)
                        if t:
                            p, m = t - 1, TILES[t - 1][1]
                            hd.wait(dve, i, t)
                            for r, bank in enumerate((hfb, hbb)):
                                ins = v.tensor_scalar(dn[0:m, r:r + 1], bank[0:m, MV:VW], -1.0,
                                                      col(p, FLOOR, r, m), ALU.mult, ALU.max)
                                do(ins) if r else do.free(ins)
                            for r, bank in enumerate((hfb, hbb)):
                                ins = v.tensor_tensor(dn[0:m, r:r + 1], bank[0:m, MV:VW], dn[0:m, r:r + 1], ALU.max)
                                do(ins) if r else do.free(ins)
                            do(v.reciprocal(rd[0:m, :], dn[0:m, :]))
                            dve.sem_inc(rdd.sem, 1)
                            hfd.wait(dve, i, t)
                            do(v.scalar_tensor_tensor(hs[0:m, p, :], hbb[0:m, 0:MV], rd[0:m, 1:2], hf[0:m, :],
                                                      ALU.mult, ALU.add))
                            dve.sem_inc(hsd.sem, 1)
                        if t < NT:
                            de.wait(dve, i, t + 1)
                            kqd.wait(dve, i, t + 1)
                            v.tensor_tensor(sw[0:m2(t), :, 0:m2(t)], D_[0:m2(t), :, 0:m2(t)],
                                            kq[t % 2][0:m2(t), 0:m2(t)].unsqueeze(1)
                                            .broadcast_to([m2(t), 2, m2(t)]), ALU.mult).then_inc(swd.sem, 1)
                            qed.wait(dve, i, t + 1)
                            off, m = TILES[t]
                            do(v.tensor_tensor(qs[:, :, 0:m], qe[:, :, 0:m],
                                               qT[:, off:off + m].unsqueeze(1).broadcast_to([P, 2, m]), ALU.mult))
                            dve.sem_inc(qsd.sem, 1)
                            if t < N:
                                um.wait(dve, i, N + t + 1)
                                if t == 0:
                                    do(v.tensor_copy(cf[:, 1, :], ub[:, 0:VW]))
                                else:
                                    do(v.scalar_tensor_tensor(cf[:, (t + 1) % 2, :], cf[:, t % 2, :], decay(t, 0),
                                                              ub[:, 0:VW], ALU.mult, ALU.add))
                                dve.sem_inc(us.sem, 1)
                    sig.wait(dve, i, 4)
                    do(v.tensor_tensor(zs[:, 1, :], zs[:, 1, :], B[:, PO:PO + L], ALU.mult))
                    dve.sem_inc(zdone.sem, 1)
                    root.wait(dve, i, 1)
                    do(v.reciprocal(rstd[:, :], rstd[:, :]))
                    for t, (off, m) in enumerate(TILES):
                        ins = v.tensor_scalar(hs[0:m, t, :], hs[0:m, t, :], rstd[0:m, t:t + 1], None, ALU.mult)
                        do(ins) if t == N else do.free(ins)
                    dve.sem_inc(hscaled.sem, 1)
                    for b, reg in enumerate((A, B)):
                        turned.wait(dve, i, b + 1)
                        do(v.scalar_tensor_tensor(og[:, b, :], reg[:, 0:L],
                                                  c["cols_a"][:, bass.ds(i * 2 + (c["head_norm"] + b), 1)],
                                                  og[:, b, :], ALU.mult, ALU.mult))
                        do(v.scalar_tensor_tensor(og[:, b, :],
                                                  xc[:, bass.ds(i * 2 + b, 1), :].rearrange("p k t -> p (k t)"),
                                                  c["cols_a"][:, bass.ds(i * 2 + (c["mlstm_skip"] + b), 1)],
                                                  og[:, b, :], ALU.mult, ALU.add))
                        v.tensor_tensor(og[:, b, :], og[:, b, :], zs[:, b, :], ALU.mult).then_inc(gated.sem, 1)


def m2(t):
    return TILES[t][1]


MLSTM_STEPS = 2 + (NT - 1) + 2 + 6 * NT + NT + (NT - 1) + 1 + NT + 4


def rope_tables():
    n = L - META
    pos = np.zeros((2, L), np.float32)
    pos[0, META:] = np.repeat(np.arange(n // GRID_W, dtype=np.float32), GRID_W)
    pos[1, META:] = np.tile(np.arange(GRID_W, dtype=np.float32), n // GRID_W)
    axis = HD // 2
    freqs = (np.float32(10000.0) ** (-np.arange(0, axis, 2, dtype=np.float32) / np.float32(axis))).astype(np.float32)
    angle = np.stack([pos[f // axis] * freqs[f % (axis // 2)] for f in range(HD)])
    return np.stack([np.cos(angle), np.sin(angle)], axis=1).astype(np.float32)


def rope_swap():
    swap = np.zeros((HD, HD), np.float32)
    half = HD // 4
    for f in range(HD):
        first = f % (2 * half) < half
        swap[f + half if first else f - half, f] = -1.0 if first else 1.0
    return swap


def before_masks():
    s, t = np.arange(P)[:, None], np.arange(P)[None, :]
    return np.stack([np.where(s <= t, 0.0, -1e30), np.where(s >= t, 0.0, -1e30)], axis=1).astype(np.float32)


def scan_starts():
    keep = np.ones((40, L), np.float32)
    keep[0:32, [o for o, _ in TILES]] = 0.0
    keep[32:40, [L - o - n for o, n in TILES]] = 0.0
    return keep


_INS = ["x", "meta_tokens", "norm_pre", "norm_post", "w_in_even", "q_norm", "k_norm", "ssm_a_re", "ssm_a_im",
        "ssm_log_dt", "ssm_b_re", "ssm_b_im", "ssm_c_re", "ssm_c_im", "ssm_d", "w_glu", "b_glu", "w_out_even",
        "w_in_odd", "conv_w", "conv_b", "w_q", "w_k", "w_v", "w_igate", "b_igate", "w_fgate", "b_fgate",
        "w_ogate", "b_ogate", "head_norm", "mlstm_skip", "w_out_odd"]
_FLAT = ("norm_pre", "norm_post")


def kernel(**inputs):
    import concourse.bacc as bacc
    from concourse.bass_utils import run_bass_kernel_spmd
    nc = bacc.Bacc("TRN2", target_bir_lowering=False, num_devices=1)
    arrays = {}
    for name in _INS:
        v = np.asarray(inputs[name])
        if name in _FLAT:
            v = v.reshape(-1)
        elif name != "meta_tokens":
            v = v[0]
        arrays[name] = np.ascontiguousarray(v)
    arrays["ident"] = np.eye(P, dtype=np.float32)
    arrays["rope"] = rope_tables()
    arrays["swap"] = rope_swap()
    arrays["masks"] = before_masks()
    arrays["starts"] = scan_starts()
    a = {n: nc.dram_tensor(f"in_{n}", v.shape, mybir.dt.from_np(v.dtype), kind="ExternalInput").ap()
         for n, v in arrays.items()}
    out = nc.dram_tensor("out", (L - META, D), F32, kind="ExternalOutput").ap()
    trunk(nc, a, out)
    result = run_bass_kernel_spmd(nc, [{f"in_{n}": v for n, v in arrays.items()}], core_ids=[0])
    return result.results[0]["out"][None]
```

```python
from contextlib import ExitStack, contextmanager
import math

import numpy as np

import concourse.bass as bass
from concourse import mybir

D = 1024
L = 1040
META = 16
P = 128
KC = D // P
HEADS, KV, HD = 8, 2, 128
G, GP, NS = 64, 16, 64
T = P // GP
CH = L // T
GB = 8
W2 = 2048
MH, MV, MK = 8, 256, 128
CONV = 5
GRID_W = 64
EPS = 1e-6
E_IN = 2 * HEADS * HD + 2 * KV * HD + 2 * D
Q0, K0, V0, GA0, U0, GB0 = 0, 1024, 1280, 1536, 2560, 3584
TILES = [(i * P, min(P, L - i * P)) for i in range(-(-L // P))]
NT = len(TILES)
PO = 248
PIECES = [(0, 264), (264, 512), (776, 264)]
QT = [(0, 120), (120, 120), (240, 112), (352, 120), (472, 112), (584, 112),
      (696, 120), (816, 112), (928, 112)]

F32 = mybir.dt.float32
F32R = mybir.dt.float32r
I32 = mybir.dt.int32
ACT = mybir.ActivationFunctionType
ALU = mybir.AluOpType
AX = mybir.AxisListType.X


class Signal:

    def __init__(self, sem, per=1, credit=0):
        self.sem, self.per, self.credit = sem, per, credit

    def start(self, eng):
        eng.sem_inc(self.sem, self.credit)

    def wait(self, eng, i, k):
        eng.wait_ge(self.sem, i * self.per + (k + self.credit))


class Steps:

    def __init__(self, eng, sem):
        self.eng, self.sem, self.n, self.base = eng, sem, 0, 0

    def __call__(self, instruction):
        instruction.then_inc(self.sem, 1)
        self.n += 1
        self.eng.wait_ge(self.sem, self.base + self.n)
        return instruction

    def free(self, instruction):
        instruction.then_inc(self.sem, 1)
        self.n += 1
        return instruction

    @contextmanager
    def loop(self, count, per):
        before = self.n
        with self.eng.Fori(0, count) as i:
            self.n, self.base = 0, i * per + before
            yield i
            assert self.n == per, (self.n, per)
        self.n, self.base = before + count * per, 0


def trunk(nc, a, out):
    outer = ExitStack()
    Stage.finished = []
    with outer:
        top = Stage(nc, outer)
        c = {}

        def dram(name, *shape, dtype=F32):
            return nc.dram_tensor(f"{name}_d", shape, dtype).ap()
        d = dict(
            res=dram("res", P, KC, L), u=dram("u", G, GP, T, CH), y=dram("y", G, GP, T, CH),
            q=dram("q", HEADS, P, L), ga=dram("ga", HEADS, P, L), gb=dram("gb", KC, P, L),
            cat=dram("cat", 2 * KC, P, L), v=dram("v", MH, P, NT, MV), xc=dram("xc", 2 * KC, P, L),
            z=dram("z", 2 * KC, P, L), o=dram("o", 2 * KC, P, L), qk=dram("qk", MH, 2, P, L),
            kt=dram("kt", MH, P, NT, MK),
            bm=dram("bm", 2, MH, L), ends=dram("ends", 2, MH, 2, NT), hh=dram("hh", 2 * KC, P, L),
        )
        constants(nc, top, a, c)
        with ExitStack() as even:
            se = Stage(nc, even)
            t = s5_tensors(se)
            kr = se.sb("k_hi", [P, KV, L], F32R), se.sb("k_lo", [P, KV, L], F32R)
            vt = se.sb("v", [P, NT, KV * HD])
            with ExitStack() as with_h:
                sh = Stage(nc, with_h)
                h = [sh.sb(n, [P, KC, L], F32R) for n in ("h_hi", "h_lo")]
                enter(nc, a, c, d, h)
                s5_inputs(nc, a, c, d, h, t)
                keys_values(nc, a, c, h, kr, vt)
                queries_gates(nc, a, c, d, h)
            t["Z"] = se.sb("Z", [P, CH + 1, 2, G])
            s5_states(nc, c, d, t)
            heads(nc, c, d, kr, vt, t)
            s5_outputs(nc, c, d, t)
        s5_glu(nc, a, c, d)
        with ExitStack() as with_h:
            sh = Stage(nc, with_h)
            hi = sh.sb("h_hi", [P, KC, L], F32R)
            y = hi[:, :, :].bitcast(F32)
            project(nc, a["w_out_even"], d["cat"], None, c, y)
            h = [hi, sh.sb("h_lo", [P, KC, L], F32R)]
            with stage(nc) as s:
                res = s.sb("res", [P, KC, L])
                norm_block(nc, c, y, lambda k: c["col"]("norm_post", k), dst=res, resid=d["res"], save=d["res"])
                norm_block(nc, c, res, lambda k: c["col"]("norm_pre", KC + k), split=h)
            conv_values_z(nc, a, c, d, h)
        with ExitStack() as gates:
            cols = Stage(nc, gates).sb("cols", [P, NT, 3, 40])
            rows = Stage(nc, gates)
            raw = rows.sb("li", [40, L]), rows.sb("fx", [40, L])
            odd_gates(nc, a, c, d, raw)
            gate_rows(nc, a, c, d, raw, cols)
            mlstm(nc, a, c, d, cols)
        with stage(nc) as s:
            y = s.sb("y", [P, KC, L])
            project(nc, a["w_out_odd"], d["hh"], d["z"], c, y[:, :, :])
            res = s.sb("res", [P, KC, L])
            norm_block(nc, c, y, lambda k: c["col"]("norm_post", KC + k), dst=res, resid=d["res"])
            leave(nc, c, res, out)


class Stage:

    count = 0
    finished = []

    def __init__(self, nc, stack):
        self.nc, self.stack, self.sems = nc, stack, []

    def sb(self, name, shape, dtype=F32):
        Stage.count += 1
        return self.stack.enter_context(self.nc.sbuf_tensor(f"{name}_{Stage.count}", shape, dtype))

    def ps(self, name, columns):
        Stage.count += 1
        return self.stack.enter_context(self.nc.psum_tensor(f"{name}_{Stage.count}", [P, columns], F32))

    def sem(self, name):
        Stage.count += 1
        self.sems.append(self.nc.alloc_semaphore(f"{name}_{Stage.count}"))
        return self.sems[-1]

    def flag(self, name, per=1, credit=0):
        return Signal(self.sem(name), per, credit)


@contextmanager
def stage(nc):
    with ExitStack() as stack:
        s = Stage(nc, stack)
        yield s
        Stage.finished += s.sems
        if len(Stage.finished) > 50:
            nc.clear_and_free_semaphores(Stage.finished)
            nc.all_engine_barrier()
            Stage.finished = []


def rows_of(region):
    return region[:, PO:PO + L]


COLS_A = [("norm_pre", 16), ("norm_post", 16), ("q_norm", 1), ("k_norm", 1), ("b_glu", 8),
          ("conv_b", 16), ("b_ogate", 16), ("head_norm", 16), ("mlstm_skip", 16)]


def constants(nc, top, a, c):
    c["ident"] = top.sb("ident", [P, P])
    c["ones"] = top.sb("ones", [P, P])
    c["cols_a"] = top.sb("cols_a", [P, 112])
    c["conv_w"] = top.sb("conv_w", [P, CONV * 2 * KC])
    c["eps"] = top.sb("eps", [P, 1])
    with stage(nc) as s:
        ra, rb = s.sb("ra", [P, P]), s.sb("rb", [P, P])
        pt = s.ps("pt", 512)
        loaded, made, turned = s.sem("params_loaded"), s.sem("ones_made"), s.sem("turned")
        with nc.Block() as block:
            @block.sync
            def _(sp):
                sp.dma_start(c["ident"][:, :], a["ident"]).then_inc(loaded, 16)
                at = 0
                for name, n in COLS_A:
                    c[name] = at
                    sp.dma_start(ra[at:at + n, :], a[name].rearrange("(r p) -> r p", p=P)).then_inc(loaded, 16)
                    at += n
                sp.dma_start(rb[0:CONV * 16, :], a["conv_w"].rearrange("w (r p) -> (w r) p", p=P)).then_inc(loaded, 16)

            @block.vector
            def _(dve):
                nc.vector.memset(c["ones"][:, :], 1.0)
                nc.vector.memset(c["eps"][:, :], EPS)
                dve.wait_ge(turned, 1)
                nc.vector.tensor_copy(c["cols_a"][:, 0:106], pt[:, 0:106])
                nc.vector.tensor_copy(c["conv_w"][:, :], pt[:, 128:128 + CONV * 16])

            @block.tensor
            def _(pe):
                pe.wait_ge(loaded, 16 * (len(COLS_A) + 2))
                nc.tensor.transpose(pt[:, 0:106], ra[0:106, :], c["ident"][0:106, 0:106])
                nc.tensor.transpose(pt[:, 128:128 + CONV * 16], rb[0:CONV * 16, :],
                                    c["ident"][0:CONV * 16, 0:CONV * 16]).then_inc(turned, 1)
    a_cols = c["cols_a"]
    c["col"] = lambda name, i: a_cols[:, c[name] + i:c[name] + i + 1]


class Weights:

    def __init__(self, nc, s, units, tiles=None):
        assert units % 2 == 0
        self.nc, self.units = nc, units
        self.tiles = tiles or (KC,) * units
        self.raw = s.sb("w_raw", [P, 2, KC, P])
        self.hi, self.lo = s.sb("w_hi", [P, 2, KC, P], F32R), s.sb("w_lo", [P, 2, KC, P], F32R)
        self.loaded = [s.sem(f"w_loaded{b}") for b in range(2)]
        self.split = s.flag("w_split", per=units, credit=2)
        self.used = s.flag("w_used", per=units, credit=2)
        self.steps = s.sem("split_steps")

    def load(self, sp, i, u, source):
        self.split.wait(sp, i, u - 1)
        sp.dma_start(self.raw[:, u % 2, 0:self.tiles[u], :], source).then_inc(self.loaded[u % 2], 16)

    def split_all(self, gp, turns, ones):
        self.split.start(gp)
        do = Steps(gp, self.steps)
        with do.loop(turns, self.units) as i:
            for u in range(self.units):
                b = u % 2
                gp.wait_ge(self.loaded[b], i * (8 * self.units) + 16 * (u // 2 + 1))
                self.used.wait(gp, i, u - 1)
                n = self.tiles[u]
                one = ones[:, 0:1].unsqueeze(2).broadcast_to([P, n, P])
                do(self.nc.gpsimd.tensor_tensor(self.hi[:, b, 0:n], self.raw[:, b, 0:n], one, ALU.mult))
                self.nc.gpsimd.tensor_tensor(self.lo[:, b, 0:n], self.raw[:, b, 0:n], self.hi[:, b, 0:n].bitcast(F32),
                                             ALU.subtract).then_inc(self.split.sem, 1)

    def product(self, pe, i, u, region, x, first=True, last=True, between=None):
        b, kc = u % 2, self.tiles[u]
        self.split.wait(pe, i, u + 1)
        for k in range(kc):
            hi, lo = x(k)
            for w, z in ((self.hi, lo), (self.hi, hi), (self.lo, hi)):
                for off, n in PIECES:
                    ins = self.nc.tensor.matmul(region[:, PO + off:PO + off + n], w[:, b, k, :], z[:, off:off + n],
                                                start=(first and k == 0 and w is self.hi and z is lo),
                                                stop=(last and k == kc - 1 and w is self.lo))
            if between is not None and k < kc - 1:
                between(k)
        ins.then_inc(self.used.sem, 1)
        return ins


def pair(x):
    return lambda k: (x[0][:, k, :], x[1][:, k, :])


def norm_block(nc, c, src, gain, dst=None, split=None, resid=None, save=None):
    with stage(nc) as s:
        sq = s.sb("sq", [P, 2, L])
        rstd = s.sb("rstd", [P, L])
        rt = s.sb("resid", [P, KC, L]) if resid is not None else None
        tmp = s.sb("tmp", [P, 2, L])
        region = s.ps("sumsq", 1536)
        squared = s.flag("squared")
        used = s.flag("squares_used", credit=2)
        root = s.sem("root_done")
        loaded = s.sem("resid_loaded")
        scaled, saved, leading = s.sem("scaled"), s.sem("saved"), s.sem("hi_done")
        steps = s.sem("dve_steps")
        with nc.Block() as block:
            @block.sync
            def _(sp):
                if resid is not None:
                    sp.dma_start(rt[:, :, :], resid).then_inc(loaded, 16)
                if save is not None:
                    for k in range(KC):
                        sp.wait_ge(scaled, k + 1)
                        sp.dma_start(save[:, k, :], dst[:, k, :]).then_inc(saved, 16)
                    sp.wait_ge(saved, 16 * KC)

            @block.scalar
            def _(act):
                for k in range(KC):
                    used.wait(act, 0, k - 1)
                    nc.scalar.activation(sq[:, k % 2, :], src[:, k, :], ACT.Square).then_inc(squared.sem, 1)
                used.wait(act, 0, KC)
                nc.scalar.activation(rstd[:, :], rows_of(region), ACT.Sqrt, bias=c["eps"][:, :],
                                     scale=1.0 / D).then_inc(root, 1)
                if split is not None:
                    for k in range(KC):
                        act.wait_ge(scaled, k + 1)
                        nc.scalar.activation(split[0][:, k, :], tmp[:, k % 2, :], ACT.Copy).then_inc(leading, 1)

            @block.tensor
            def _(pe):
                used.start(pe)
                for k in range(KC):
                    squared.wait(pe, 0, k + 1)
                    for off, n in PIECES:
                        last = nc.tensor.matmul(region[:, PO + off:PO + off + n], c["ones"][:, :],
                                                sq[:, k % 2, off:off + n], start=(k == 0), stop=(k == KC - 1))
                    last.then_inc(used.sem, 1)

            @block.vector
            def _(dve):
                do = Steps(dve, steps)
                dve.wait_ge(root, 1)
                do(nc.vector.reciprocal(rstd[:, :], rstd[:, :]))
                if resid is not None:
                    dve.wait_ge(loaded, 16)
                for k in range(KC + 1):
                    if k < KC and split is not None:
                        if k >= 2:
                            dve.wait_ge(leading, k - 1)
                        nc.vector.scalar_tensor_tensor(tmp[:, k % 2, :], src[:, k, :], gain(k), rstd[:, :],
                                                       ALU.mult, ALU.mult).then_inc(scaled, 1)
                    if k and split is not None:
                        dve.wait_ge(leading, k)
                        do(nc.vector.tensor_tensor(split[1][:, k - 1, :], tmp[:, (k - 1) % 2, :],
                                                   split[0][:, k - 1, :].bitcast(F32), ALU.subtract))
                    if k < KC and split is None:
                        do(nc.vector.scalar_tensor_tensor(tmp[:, k % 2, :], src[:, k, :], gain(k), rstd[:, :],
                                                          ALU.mult, ALU.mult))
                        nc.vector.tensor_tensor(dst[:, k, :], tmp[:, k % 2, :], rt[:, k, :],
                                                ALU.add).then_inc(scaled, 1)


def enter(nc, a, c, d, h):
    with stage(nc) as s0:
        res = s0.sb("res", [P, KC, L])
        with stage(nc) as s:
            xt = s.sb("xt", [P, 2, D])
            mt = s.sb("mt", [META, D])
            pt = [s.ps(f"pt{i}", 512) for i in range(4)]
            xl = [s.sem("x_loaded0"), s.sem("x_loaded1")]
            ml = s.sem("meta_loaded")
            turned = s.flag("turned", per=4, credit=4)
            evac = s.flag("evac", per=4, credit=4)
            meta_turned = s.sem("meta_turned")
            saved = s.sem("saved")
            x_tiles = a["x"].rearrange("(i p) f -> i p f", p=P)
            with nc.Block() as block:
                @block.sync
                def _(sp):
                    sp.dma_start(mt[:, :], a["meta_tokens"]).then_inc(ml, 16)
                    with sp.Fori(0, 4) as i:
                        for b in range(2):
                            turned.wait(sp, i, 2 * b - 2)
                            sp.dma_start(xt[:, b, :], x_tiles[i * 2 + b]).then_inc(xl[b], 16)

                @block.tensor
                def _(pe):
                    turned.start(pe)
                    with pe.Fori(0, 4) as i:
                        for b in range(2):
                            pe.wait_ge(xl[b], i * 16 + 16)
                            for half in range(2):
                                evac.wait(pe, i, 2 * b + half - 3)
                                for k in range(4):
                                    last = nc.tensor.transpose(pt[2 * b + half][:, k * P:(k + 1) * P],
                                                               xt[:, b, (4 * half + k) * P:(4 * half + k + 1) * P],
                                                               c["ident"][:, :])
                                last.then_inc(turned.sem, 1)
                    pe.wait_ge(ml, 16)
                    evac.wait(pe, 3, 4)
                    for k in range(KC):
                        last = nc.tensor.transpose(pt[0][:, k * META:(k + 1) * META], mt[:, k * P:(k + 1) * P],
                                                   c["ident"][0:META, 0:META])
                    last.then_inc(meta_turned, 1)

                @block.vector
                def _(dve):
                    evac.start(dve)
                    with dve.Fori(0, 4) as i:
                        for b in range(2):
                            for half in range(2):
                                turned.wait(dve, i, 2 * b + half + 1)
                                nc.vector.tensor_copy(
                                    res[:, 4 * half:4 * half + 4, bass.ds(i * 256 + (b * P + META), P)],
                                    pt[2 * b + half][:, :].rearrange("p (k t) -> p k t", k=4)).then_inc(evac.sem, 1)
                    dve.wait_ge(meta_turned, 1)
                    nc.vector.tensor_copy(res[:, :, 0:META], pt[0][:, 0:P].rearrange("p (k t) -> p k t", k=KC))
        with stage(nc) as s:
            saved = s.sem("saved")
            with nc.Block() as block:
                @block.sync
                def _(sp):
                    sp.dma_start(d["res"], res[:, :, :]).then_inc(saved, 16)
                    sp.wait_ge(saved, 16)
        norm_block(nc, c, res, lambda k: c["col"]("norm_pre", k), split=h)


def s5_tensors(s):
    t = {}
    t["B"] = s.sb("B", [P, 2, G, GP])
    t["C"] = s.sb("C", [P, 3, G, GP])
    t["pw_in"] = s.sb("pw_in", [P, T, 2, G])
    t["pw_out"] = s.sb("pw_out", [P, T, 2, G])
    t["step_re"] = s.sb("step_re", [P, 2, G])
    t["step_im"] = s.sb("step_im", [P, 2, G])
    t["skip"] = s.sb("skip", [P, G])
    return t


ROUND = 1.5 * 2.0 ** 23
LN2_HI, LN2_LO = 0.693359375, -2.12194440e-4
PI2_A, PI2_B = 6.28125, 0.0019350051879882812
PI2_C = 2 * math.pi - PI2_A - PI2_B


def s5_inputs(nc, a, c, d, h, t):
    with stage(nc) as s:
        weights = Weights(nc, s, 2)
        st = s.sb("staged", [P, 2, T, CH])
        raw = s.sb("raw", [G, 2, P])
        dr = s.sb("d_rows", [G, T, GP])
        a0 = s.sb("a", [P, 2, G])
        logdt = s.sb("log_dt", [P, G])
        b_in = s.sb("b_in", [P, 2, G, GP])
        c_in = s.sb("c_in", [P, 2, KC, P])
        x = s.sb("x", [P, 24, G])
        xi = s.sb("xi", [P, G], I32)
        pw = s.sb("pw", [P, T + 1, 2, G])
        pt = s.sb("pt", [P, 2, 4, G])
        bt = s.sb("bt", [P, 2, G, GP])
        reg = [s.ps(f"u{b}", 1536) for b in range(2)]
        pa, pc = s.ps("pa", 512), s.ps("pc", 512)
        params, skip_loaded = s.sem("params_loaded"), s.sem("skip_loaded")
        bl, cl = s.sem("b_loaded"), s.sem("c_loaded")
        mm = weights.used
        evac = s.flag("u_copied", per=2, credit=2)
        st_sem = [s.flag(f"u_stored{b}", per=16, credit=16) for b in range(2)]
        at, ac, acc = s.sem("a_turned"), s.sem("c_turned"), s.sem("c_copied")
        steps = s.sem("dve_steps")
        asked, answered = s.sem("function_asked"), s.sem("function_done")
        wv = a["w_in_even"].rearrange("(k p) n -> p k n", p=P)
        uv = d["u"].rearrange("(j g) p s c -> j (g p) (s c)", j=KC)
        with nc.Block() as block:
            @block.sync
            def _(sp):
                for q, name in enumerate(("ssm_a_re", "ssm_a_im")):
                    for r in range(2):
                        sp.dma_start(raw[:, q, r * NS:(r + 1) * NS], a[name][r]).then_inc(params, 16)
                for r in range(2):
                    rows = slice(r * NS, (r + 1) * NS)
                    sp.dma_start(logdt[rows, :], a["ssm_log_dt"][r:r + 1, :].broadcast_to([NS, G])).then_inc(params, 16)
                    for q, name in enumerate(("ssm_b_re", "ssm_b_im")):
                        sp.dma_start(b_in[rows, q, :, :], a[name][r].rearrange("g n p -> n g p")).then_inc(bl, 16)
                    for q, name in enumerate(("ssm_c_re", "ssm_c_im")):
                        sp.dma_start(c_in[:, q, :, rows],
                                     a[name][r].rearrange("(k g) q n -> (g q) k n", k=KC)).then_inc(cl, 16)
                with sp.Fori(0, KC // 2) as i:
                    for b in range(2):
                        weights.load(sp, i, b, wv[:, :, bass.ds(i * 256 + (U0 + b * P), P)])

            @block.gpsimd
            def _(gp):
                for j in range(T):
                    gp.dma_start(dr[:, j, :], a["ssm_d"].rearrange("(g p) -> g p", p=GP)).then_inc(skip_loaded, 16)
                weights.split_all(gp, KC // 2, c["ones"])

            @block.tensor
            def _(pe):
                weights.used.start(pe)
                pe.wait_ge(params, 16 * 6)
                pe.wait_ge(skip_loaded, 16 * T)
                for q in range(2):
                    nc.tensor.transpose(pa[:, q * G:(q + 1) * G], raw[:, q, :], c["ident"][0:G, 0:G])
                last = nc.tensor.transpose(pa[:, 2 * G:3 * G], dr[:, :, :].rearrange("g s p -> g (s p)"),
                                           c["ident"][0:G, 0:G])
                last.then_inc(at, 1)
                pe.wait_ge(cl, 16 * 4)
                for q in range(2):
                    for k in range(0, KC, 4):
                        if q or k:
                            pe.wait_ge(acc, 2 * q + k // 4)
                        for kk in range(4):
                            last = nc.tensor.transpose(pc[:, kk * P:(kk + 1) * P], c_in[:, q, k + kk, :],
                                                       c["ident"][:, :])
                        last.then_inc(ac, 1)
                with pe.Fori(0, KC // 2) as i:
                    for b in range(2):
                        evac.wait(pe, i, b - 1)
                        weights.product(pe, i, b, reg[b], pair(h))

            calls = [(ACT.Tanh, 3, 4, 0.5), (ACT.Sin, 8, 9, 1.0), (ACT.Sin, 8, 10, 0.5), (ACT.Tanh, 6, 11, 0.5)]

            @block.scalar
            def _(act):
                evac.start(act)
                for b in range(2):
                    st_sem[b].start(act)
                for n, (f, src, dst, scale) in enumerate(calls):
                    act.wait_ge(asked, 1 if n == 0 else 2)
                    nc.scalar.activation(x[:, dst, :], x[:, src, :], f, scale=scale).then_inc(answered, 1)
                with act.Fori(0, KC // 2) as i:
                    for b in range(2):
                        mm.wait(act, i, b + 1)
                        st_sem[b].wait(act, i, 0)
                        nc.scalar.activation(st[:, b, :, :].rearrange("p s c -> p c s"),
                                             rows_of(reg[b]).rearrange("p (c s) -> p c s", s=T),
                                             ACT.Copy).then_inc(evac.sem, 1)
                        evac.wait(act, i, b + 1)
                        act.dma_start(uv[i * 2 + b], st[:, b, :, :]).then_inc(st_sem[b].sem, 16)
                for b in range(2):
                    st_sem[b].wait(act, KC // 2, 0)

            @block.vector
            def _(dve):
                v = nc.vector
                do = Steps(dve, steps)

                def two(o, i0, s1, op0, s2=None, op1=None):
                    do(v.tensor_scalar(o, i0, s1, s2, op0, op1) if op1 is not None else
                       v.tensor_scalar(o, i0, s1, None, op0))

                def tt(o, i0, i1, op):
                    do(v.tensor_tensor(o, i0, i1, op))

                def X(n):
                    return x[:, n, :]

                dve.wait_ge(params, 16 * 6)
                two(X(0), logdt[:, :], -87.0, ALU.max)
                two(X(1), X(0), 1 / math.log(2), ALU.mult)
                two(X(1), X(1), ROUND, ALU.add)
                two(X(1), X(1), ROUND, ALU.subtract)
                do(v.scalar_tensor_tensor(X(2), X(1), -LN2_HI, X(0), ALU.mult, ALU.add))
                do(v.scalar_tensor_tensor(X(3), X(1), -LN2_LO, X(2), ALU.mult, ALU.add))
                two(xi[:, :], X(1), 127.0, ALU.add)
                do(v.tensor_single_scalar(xi[:, :], xi[:, :], 23, ALU.logical_shift_left))
                dve.sem_inc(asked, 1)
                dve.wait_ge(answered, 1)
                two(X(5), X(4), -1.0, ALU.mult, 1.0, ALU.add)
                do(v.reciprocal(X(5), X(5)))
                do(v.scalar_tensor_tensor(X(4), X(4), 1.0, X(5), ALU.add, ALU.mult))
                tt(X(12), X(4), xi[:, :].bitcast(F32), ALU.mult)
                dve.wait_ge(at, 1)
                do(v.tensor_copy(a0[:, :, :], pa[:, 0:2 * G].rearrange("p (q g) -> p q g", q=2)))
                do(v.tensor_copy(t["skip"][:, :], pa[:, 2 * G:3 * G]))
                tt(X(6), a0[:, 0, :], X(12), ALU.mult)
                tt(X(7), a0[:, 1, :], X(12), ALU.mult)
                two(X(13), X(7), 1 / (2 * math.pi), ALU.mult)
                two(X(13), X(13), ROUND, ALU.add)
                two(X(13), X(13), ROUND, ALU.subtract)
                for part in (PI2_A, PI2_B, PI2_C):
                    do(v.scalar_tensor_tensor(X(7), X(13), -part, X(7), ALU.mult, ALU.add))
                two(X(8), X(7), 3.1415925, ALU.min, -3.1415925, ALU.max)
                dve.sem_inc(asked, 1)
                dve.wait_ge(answered, 4)
                two(X(14), X(11), -1.0, ALU.mult, 1.0, ALU.add)
                do(v.reciprocal(X(14), X(14)))
                do(v.scalar_tensor_tensor(X(14), X(11), 2.0, X(14), ALU.mult, ALU.mult))
                do(v.scalar_tensor_tensor(X(15), X(10), -2.0, X(10), ALU.mult, ALU.mult))
                do(v.scalar_tensor_tensor(X(16), X(15), 1.0, X(14), ALU.add, ALU.mult))
                tt(X(16), X(16), X(15), ALU.add)
                do(v.scalar_tensor_tensor(X(17), X(14), 1.0, X(9), ALU.add, ALU.mult))
                tt(X(18), a0[:, 0, :], a0[:, 0, :], ALU.mult)
                tt(X(19), a0[:, 1, :], a0[:, 1, :], ALU.mult)
                tt(X(18), X(18), X(19), ALU.add)
                do(v.reciprocal(X(18), X(18)))
                tt(X(19), X(16), a0[:, 0, :], ALU.mult)
                tt(X(20), X(17), a0[:, 1, :], ALU.mult)
                tt(X(19), X(19), X(20), ALU.add)
                tt(X(21), X(19), X(18), ALU.mult)
                tt(X(19), X(17), a0[:, 0, :], ALU.mult)
                tt(X(20), X(16), a0[:, 1, :], ALU.mult)
                tt(X(19), X(19), X(20), ALU.subtract)
                tt(X(22), X(19), X(18), ALU.mult)
                do(v.memset(pw[:, 0, 0, :], 1.0))
                do(v.memset(pw[:, 0, 1, :], 0.0))
                two(pw[:, 1, 0, :], X(16), 1.0, ALU.add)
                do(v.tensor_copy(pw[:, 1, 1, :], X(17)))
                n = 1
                while n < T:
                    lo = pw[:, 1:n + 1, :, :]

                    def last(q, n=n):
                        return pw[:, n:n + 1, q, :].broadcast_to([P, n, G])
                    tt(pt[:, 0, 0:n, :], lo[:, :, 0, :], last(0), ALU.mult)
                    tt(pt[:, 1, 0:n, :], lo[:, :, 1, :], last(1), ALU.mult)
                    tt(pw[:, n + 1:2 * n + 1, 0, :], pt[:, 0, 0:n, :], pt[:, 1, 0:n, :], ALU.subtract)
                    tt(pt[:, 0, 0:n, :], lo[:, :, 0, :], last(1), ALU.mult)
                    tt(pt[:, 1, 0:n, :], lo[:, :, 1, :], last(0), ALU.mult)
                    tt(pw[:, n + 1:2 * n + 1, 1, :], pt[:, 0, 0:n, :], pt[:, 1, 0:n, :], ALU.add)
                    n *= 2
                f, r = slice(0, NS), slice(NS, P)
                for e in range(T):
                    do.free(v.tensor_copy(t["pw_in"][f, e, :, :], pw[f, T - 1 - e, :, :]))
                    do.free(v.tensor_copy(t["pw_in"][r, e, :, :], pw[r, e, :, :]))
                    do.free(v.tensor_copy(t["pw_out"][f, e, :, :], pw[f, e + 1, :, :]))
                    do.free(v.tensor_copy(t["pw_out"][r, e, :, :], pw[r, T - e, :, :]))
                do.free(v.tensor_copy(t["step_re"][:, 0, :], pw[:, T, 0, :]))
                do.free(v.tensor_copy(t["step_re"][:, 1, :], pw[:, T, 0, :]))
                two(t["step_im"][:, 1, :], pw[:, T, 1, :], -1.0, ALU.mult)
                do.free(v.tensor_copy(t["step_im"][:, 0, :], pw[:, T, 1, :]))
                dve.wait_ge(bl, 16 * 4)
                g = [X(21 + q).unsqueeze(2).broadcast_to([P, G, GP]) for q in range(2)]
                tt(bt[:, 0], b_in[:, 0], g[0], ALU.mult)
                tt(bt[:, 1], b_in[:, 1], g[1], ALU.mult)
                tt(t["B"][:, 0], bt[:, 0], bt[:, 1], ALU.subtract)
                tt(bt[:, 0], b_in[:, 0], g[1], ALU.mult)
                tt(bt[:, 1], b_in[:, 1], g[0], ALU.mult)
                tt(t["B"][:, 1], bt[:, 0], bt[:, 1], ALU.add)
                for q in range(2):
                    for k in range(2):
                        dve.wait_ge(ac, 2 * q + k + 1)
                        v.tensor_copy(t["C"][:, q, 32 * k:32 * k + 32, :],
                                      pc[:, :].rearrange("p (g q) -> p g q", q=GP)).then_inc(acc, 1)
                dve.wait_ge(acc, 4)
                do(v.tensor_scalar(t["C"][:, 2], t["C"][:, 1], -1.0, None, ALU.mult))


def complex_table(nc, do, out, tmp, pw, x, sign):
    v, tt = nc.vector, nc.vector.tensor_tensor

    def p(q):
        return pw[:, q].rearrange("p s g -> p g s").unsqueeze(3).broadcast_to([P, GB, T, GP])

    def y(q):
        return x[:, q].unsqueeze(2).broadcast_to([P, GB, T, GP])
    do.free(tt(tmp[:, 0], p(0), y(0), ALU.mult))
    do(tt(tmp[:, 1], p(1), y(1), ALU.mult))
    do(tt(out[:, 0], tmp[:, 0], tmp[:, 1], ALU.subtract))
    do.free(tt(tmp[:, 0], p(0), y(1), ALU.mult))
    do(tt(tmp[:, 1], p(1), y(0), ALU.mult))
    if sign > 0:
        return tt(out[:, 1], tmp[:, 0], tmp[:, 1], ALU.add)
    flat = [z.rearrange("p g s q -> p (g s q)") for z in (out[:, 1], tmp[:, 0], tmp[:, 1])]
    return v.scalar_tensor_tensor(flat[0], flat[1], -1.0, flat[2], ALU.mult, ALU.subtract)


def s5_states(nc, c, d, t):
    with stage(nc) as s:
        us = s.sb("us", [P, G, CH])
        tab = s.sb("tab", [P, 2, GB, T, GP])
        tmp = s.sb("tmp", [P, 2, GB, T, GP])
        wl = s.sb("w_in", [P, GB, 2, P])
        tp = [s.ps(f"tp{b}", 512) for b in range(2)]
        zp = [s.ps(f"zp{b}", 512) for b in range(4)]
        loaded = s.sem("u_loaded")
        built = s.flag("table_built")
        turned = s.flag("turned", per=4, credit=4)
        copied = s.flag("weights_copied", per=4, credit=4)
        summed = s.flag("summed", per=GB, credit=GB)
        stored = s.flag("stored", per=GB, credit=GB)
        steps = s.sem("dve_steps")
        uv = d["u"].rearrange("g p s c -> s p g c")
        with nc.Block() as block:
            @block.sync
            def _(sp):
                for j in range(T):
                    sp.dma_start(us[j * GP:(j + 1) * GP, :, :], uv[j]).then_inc(loaded, 16)

            @block.vector
            def _(dve):
                do = Steps(dve, steps)
                do.free(nc.vector.memset(t["Z"][:, 0, :, :], 0.0))
                with do.loop(G // GB, 5) as i:
                    turned.wait(dve, i, 0)
                    g = bass.ds(i * GB, GB)
                    complex_table(nc, do, tab, tmp,
                                  t["pw_in"][:, :, :, g].rearrange("p s q g -> p q s g"),
                                  t["B"][:, :, g, :], 1).then_inc(built.sem, 1)

            @block.tensor
            def _(pe):
                turned.start(pe)
                summed.start(pe)
                pe.wait_ge(loaded, 16 * T)
                with pe.Fori(0, G // GB) as i:
                    built.wait(pe, i, 1)
                    for m in range(4):
                        copied.wait(pe, i, m - 1)
                        for n in range(4):
                            g, q = 2 * m + n // 2, n % 2
                            last = nc.tensor.transpose(tp[m % 2][:, n * P:(n + 1) * P],
                                                       tab[:, q, g].rearrange("p s q -> p (s q)"), c["ident"][:, :])
                        last.then_inc(turned.sem, 1)
                    for g in range(GB):
                        if g % 2 == 0:
                            copied.wait(pe, i, g // 2 + 1)
                        stored.wait(pe, i, g - 3)
                        for q in range(2):
                            last = nc.tensor.matmul(zp[g % 4][:, q * CH:(q + 1) * CH], wl[:, g, q, :],
                                                    us[:, bass.ds(i * GB + g, 1), :].rearrange("p g c -> p (g c)"),
                                                    start=True, stop=True)
                        last.then_inc(summed.sem, 1)

            @block.scalar
            def _(act):
                copied.start(act)
                stored.start(act)
                with act.Fori(0, G // GB) as i:
                    for m in range(4):
                        turned.wait(act, i, m + 1)
                        summed.wait(act, i, 2 * m + 2 - GB)
                        nc.scalar.activation(wl[:, 2 * m:2 * m + 2, :, :].rearrange("p g q m -> p (g q m)"),
                                             tp[m % 2][:, :], ACT.Copy).then_inc(copied.sem, 1)
                    for g in range(GB):
                        summed.wait(act, i, g + 1)
                        gg = bass.ds(i * GB + g, 1)
                        f, r = slice(0, NS), slice(NS, P)
                        src = zp[g % 4][:, 0:2 * CH].rearrange("p (q c) -> p q c", q=2)
                        nc.scalar.activation(
                            t["Z"][f, 1:CH + 1, :, gg].rearrange("p c q g -> p q (c g)"), src[f], ACT.Copy)
                        nc.scalar.activation(
                            t["Z"][r, 1:CH + 1, :, gg].rearrange("p c q g -> p q (c g)"),
                            src[r, :, ::-1], ACT.Copy).then_inc(stored.sem, 1)


def s5_scan(nc, gp, t, tmp, steps, turns):
    do = Steps(gp, steps)
    tt = nc.gpsimd.tensor_tensor
    with do.loop(CH // 2, 8) as i:
        for b in range(2):
            now = t["Z"][:, bass.ds(i * 2 + b, 1), :, :].rearrange("p k q g -> p (k q) g")
            nxt = t["Z"][:, bass.ds(i * 2 + (b + 1), 1), :, :].rearrange("p k q g -> p (k q) g")
            gp.sem_inc(turns, 1)
            do.free(tt(tmp[:, 0], now, t["step_re"][:, :, :], ALU.mult))
            do(tt(tmp[:, 1], now, t["step_im"][:, :, :], ALU.mult))
            do(tt(tmp[:, 0], tmp[:, 0], tmp[:, 1, ::-1, :], ALU.add))
            gp.sem_inc(turns, 1)
            do(tt(nxt, nxt, tmp[:, 0], ALU.add))


def s5_outputs(nc, c, d, t):
    K = 2 * (T - 1) * GP + GP
    with stage(nc) as s:
        us = s.sb("us", [P, GB, CH])
        bb = s.sb("bb", [P, 2, GB, GP])
        cb = s.sb("cb", [P, 3, GB, GP])
        tab = s.sb("tab", [P, 2, GB, T, GP])
        tmp = s.sb("tmp", [P, 2, GB, T, GP])
        kt = s.sb("kt", [GP, GB, K])
        toe = s.sb("toe", [P, GB, P])
        diag = s.sb("diag", [P, GB, P])
        rhs = s.sb("rhs", [P, GB, 2, CH])
        ys = s.sb("ys", [P, GB, CH])
        kb = [s.ps(f"kb{b}", 512) for b in range(2)]
        kf = [s.ps(f"kf{b}", 512) for b in range(2)]
        yp = [s.ps(f"yp{b}", 512) for b in range(3)]
        u_loaded = s.sem("u_loaded")
        built = s.flag("table_built", per=1)
        gathered = s.flag("states_gathered", per=2)
        lag = s.flag("lags_done", per=GB, credit=GB)
        lagc = s.flag("lags_copied", per=GB, credit=GB)
        windowed = s.flag("windows_loaded", per=16 * T, credit=16)
        toe_ready = s.flag("toeplitz_ready", per=1)
        done = s.flag("outputs_done", per=GB, credit=GB)
        ycop = s.flag("outputs_copied", per=GB, credit=GB)
        ysto = s.flag("outputs_stored", per=16 * T, credit=16)
        steps = s.sem("dve_steps")
        uv = d["u"].rearrange("g p s c -> s p g c")
        yv = d["y"].rearrange("g p s c -> s p g c")
        NB = G // GB
        with nc.Block() as block:
            @block.sync
            def _(sp):
                with sp.Fori(0, NB) as i:
                    g = bass.ds(i * GB, GB)
                    done.wait(sp, i, 0)
                    for j in range(T):
                        sp.dma_start(us[j * GP:(j + 1) * GP, :, :], uv[j][:, g, :]).then_inc(u_loaded, 16)
                    lagc.wait(sp, i, GB)
                    for j in range(T):
                        off = (T - 1 - j) * GP
                        sp.dma_start(toe[j * GP:(j + 1) * GP, :, :], kt[:, :, off:off + P]).then_inc(windowed.sem, 16)

            @block.vector
            def _(dve):
                do = Steps(dve, steps)
                lagc.start(dve)
                windowed.start(dve)
                with do.loop(NB, 9) as i:
                    g = bass.ds(i * GB, GB)
                    done.wait(dve, i, 0)
                    do.free(nc.vector.tensor_copy(bb[:, :, :, :], t["B"][:, :, g, :]))
                    do.free(nc.vector.tensor_copy(cb[:, :, :, :], t["C"][:, :, g, :]))
                    complex_table(nc, do, tab, tmp,
                                  t["pw_out"][:, :, :, g].rearrange("p s q g -> p q s g"),
                                  t["C"][:, :, g, :], -1).then_inc(built.sem, 1)
                    for n in range(GB):
                        lag.wait(dve, i, n + 1)
                        if n == 0:
                            windowed.wait(dve, i, 0)
                        nc.vector.tensor_copy(kt[:, n, 0:(T - 1) * GP], kb[n % 2][0:GP, 0:(T - 1) * GP])
                        nc.vector.tensor_copy(kt[:, n, (T - 1) * GP:K], kf[n % 2][0:GP, 0:T * GP])\
                            .then_inc(lagc.sem, 1)
                    do(nc.vector.tensor_tensor(
                        diag[:, :, :], c["ident"][:, :].unsqueeze(1).broadcast_to([P, GB, P]),
                        t["skip"][:, g].unsqueeze(2).broadcast_to([P, GB, P]), ALU.mult))
                    windowed.wait(dve, i, 16 * T)
                    do(nc.vector.tensor_tensor(toe[:, :, :], toe[:, :, :], diag[:, :, :], ALU.add))
                    dve.sem_inc(toe_ready.sem, 1)

            @block.tensor
            def _(pe):
                lag.start(pe)
                done.start(pe)
                with pe.Fori(0, NB) as i:
                    built.wait(pe, i, 1)
                    f, r = slice(0, NS), slice(NS, P)
                    flat = "p t q -> p (t q)"
                    for n in range(GB):
                        lagc.wait(pe, i, n - 1)
                        ob, o = kb[n % 2][0:GP, :], kf[n % 2][0:GP, :]
                        for q in range(2):
                            nc.tensor.matmul(o[:, 0:GP], bb[:, q, n, :],
                                                    cb[:, 2 * q, n, :], start=(q == 0), stop=(q == 1))
                        for q in range(2):
                            nc.tensor.matmul(ob[:, 0:(T - 1) * GP], bb[r, q, n, :],
                                             tab[r, q, n, 1:T, :].rearrange(flat), start=(q == 0), stop=(q == 1))
                        for q in range(2):
                            last = nc.tensor.matmul(o[:, GP:T * GP], bb[f, q, n, :],
                                                    tab[f, q, n, 0:T - 1, :].rearrange(flat), start=(q == 0), stop=(q == 1))
                        last.then_inc(lag.sem, 1)
                    pe.wait_ge(u_loaded, (i + 1) * (16 * T))
                    gathered.wait(pe, i, 2)
                    toe_ready.wait(pe, i, 1)
                    for n in range(GB):
                        ycop.wait(pe, i, n - 2)
                        o = yp[n % 3][:, 0:CH]
                        nc.tensor.matmul(o, toe[:, n, :], us[:, n, :], start=True, stop=False)
                        nc.tensor.matmul(o, tab[:, 0, n].rearrange(flat), rhs[:, n, 0, :], start=False, stop=False)
                        nc.tensor.matmul(o, tab[:, 1, n].rearrange(flat), rhs[:, n, 1, :],
                                         start=False, stop=True).then_inc(done.sem, 1)

            @block.scalar
            def _(act):
                ycop.start(act)
                ysto.start(act)
                with act.Fori(0, NB) as i:
                    g = bass.ds(i * GB, GB)
                    done.wait(act, i, 0)
                    for rows, order in ((slice(0, NS), slice(None)), (slice(NS, P), slice(None, None, -1))):
                        for q in range(2):
                            ins = nc.scalar.activation(
                                rhs[rows, :, q, order], t["Z"][rows, 0:CH, q, g].rearrange("p c g -> p g c"), ACT.Copy)
                        ins.then_inc(gathered.sem, 1)
                    ysto.wait(act, i, 0)
                    for n in range(GB):
                        done.wait(act, i, n + 1)
                        nc.scalar.activation(ys[:, n, :], yp[n % 3][:, 0:CH], ACT.Copy).then_inc(ycop.sem, 1)
                    ycop.wait(act, i, GB)
                    for j in range(T):
                        act.dma_start(yv[j][:, bass.ds(i * GB, GB), :],
                                      ys[j * GP:(j + 1) * GP, :, :]).then_inc(ysto.sem, 16)
                ysto.wait(act, NB, 0)




SCALE = HD ** -0.5


def keys_values(nc, a, c, h, kr, vt):
    with stage(nc) as s:
        weights = Weights(nc, s, 4)
        rope, swap = s.sb("rope", [P, 2, L]), s.sb("swap", [P, P])
        kg, sq = s.sb("kg", [P, L]), s.sb("sq", [P, L])
        rs, tm = s.sb("rs", [P, L]), s.sb("tm", [P, L])
        kt, vf = s.sb("kt", [P, L]), s.sb("vf", [P, L])
        reg = [s.ps("product", 1536), s.ps("side", 1536)]
        load = s.sem("loaded")
        qg_ready, ss, sw = s.sem("gained"), s.sem("squares_summed"), s.sem("swapped")
        side_free, k_done, k_hi = s.sem("side_free"), s.sem("k_done"), s.sem("k_hi")
        v_copied, v_turned, v_out = s.sem("v_copied"), s.sem("v_turned"), s.sem("v_out")
        steps = s.sem("dve_steps")
        win = a["w_in_even"].rearrange("(k p) n -> p k n", p=P)
        with nc.Block() as block:
            @block.sync
            def _(sp):
                sp.dma_start(rope[:, :, :], a["rope"]).then_inc(load, 16)
                sp.dma_start(swap[:, :], a["swap"]).then_inc(load, 16)
                for u in range(4):
                    weights.load(sp, 0, u, win[:, :, K0 + u * P:K0 + (u + 1) * P])

            @block.gpsimd
            def _(gp):
                weights.split_all(gp, 1, c["ones"])

            @block.tensor
            def _(pe):
                weights.used.start(pe)
                pe.wait_ge(load, 32)
                for n in range(KV):
                    if n:
                        pe.wait_ge(qg_ready, 2 * n)
                    weights.product(pe, 0, n, reg[0], pair(h))
                    pe.wait_ge(qg_ready, 2 * n + 2)
                    if n:
                        pe.wait_ge(side_free, 2 * n)
                    for off, m in PIECES:
                        last = nc.tensor.matmul(reg[1][:, PO + off:PO + off + m], c["ones"][:, :],
                                                sq[:, off:off + m], start=True, stop=True)
                    last.then_inc(ss, 1)
                    pe.wait_ge(side_free, 2 * n + 1)
                    for off, m in PIECES:
                        last = nc.tensor.matmul(reg[1][:, PO + off:PO + off + m], swap[:, :],
                                                kg[:, off:off + m], start=True, stop=True)
                    last.then_inc(sw, 1)
                for n in range(KV):
                    if n:
                        pe.wait_ge(v_copied, n)
                    weights.product(pe, 0, KV + n, reg[0], pair(h))
                    pe.wait_ge(v_copied, n + 1)
                    pe.wait_ge(side_free, 2 * KV)
                    if n:
                        pe.wait_ge(v_out, n)
                    for t, (off, m) in enumerate(TILES):
                        last = nc.tensor.transpose(reg[1][0:m, t * P:(t + 1) * P], vf[:, off:off + m],
                                                   c["ident"][:, :])
                    last.then_inc(v_turned, 1)

            @block.scalar
            def _(act):
                for n in range(KV):
                    weights.used.wait(act, 0, n + 1)
                    if n:
                        act.wait_ge(k_done, n)
                    nc.scalar.activation(kg[:, :], rows_of(reg[0]), ACT.Copy,
                                         scale=c["col"]("k_norm", 0)).then_inc(qg_ready, 1)
                    nc.scalar.activation(sq[:, :], rows_of(reg[0]), ACT.Square).then_inc(qg_ready, 1)
                    act.wait_ge(ss, n + 1)
                    nc.scalar.activation(rs[:, :], rows_of(reg[1]), ACT.Sqrt, bias=c["eps"][:, :],
                                         scale=1.0 / HD).then_inc(side_free, 1)
                    act.wait_ge(k_done, n + 1)
                    nc.scalar.activation(kr[0][:, n, :], kt[:, :], ACT.Copy).then_inc(k_hi, 1)
                for n in range(KV):
                    weights.used.wait(act, 0, KV + n + 1)
                    if n:
                        act.wait_ge(v_turned, n)
                    nc.scalar.activation(vf[:, :], rows_of(reg[0]), ACT.Copy).then_inc(v_copied, 1)
                    act.wait_ge(v_turned, n + 1)
                    N, dn = NT - 1, slice(n * HD, (n + 1) * HD)
                    nc.scalar.activation(vt[:, 0:N, dn],
                                         reg[1][:, 0:N * P].rearrange("p (t f) -> p t f", f=P), ACT.Copy)
                    nc.scalar.activation(vt[0:TILES[N][1], N, dn], reg[1][0:TILES[N][1], N * P:NT * P],
                                         ACT.Copy).then_inc(v_out, 1)

            @block.vector
            def _(dve):
                do = Steps(dve, steps)
                for n in range(KV):
                    dve.wait_ge(side_free, 2 * n + 1)
                    do(nc.vector.reciprocal(rs[:, :], rs[:, :]))
                    if n:
                        dve.wait_ge(k_hi, n)
                    do(nc.vector.tensor_tensor(kt[:, :], kg[:, :], rope[:, 0, :], ALU.mult))
                    dve.wait_ge(sw, n + 1)
                    do(nc.vector.tensor_tensor(tm[:, :], rows_of(reg[1]), rope[:, 1, :], ALU.mult))
                    dve.sem_inc(side_free, 1)
                    do(nc.vector.tensor_tensor(kt[:, :], kt[:, :], tm[:, :], ALU.add))
                    do(nc.vector.tensor_tensor(kt[:, :], kt[:, :], rs[:, :], ALU.mult))
                    dve.sem_inc(k_done, 1)
                    dve.wait_ge(k_hi, n + 1)
                    do(nc.vector.tensor_tensor(kr[1][:, n, :], kt[:, :], kr[0][:, n, :].bitcast(F32),
                                               ALU.subtract))


def queries_gates(nc, a, c, d, h):
    base = (Q0, GA0, GB0)
    dest = (d["q"], d["ga"], d["gb"])
    with stage(nc) as s:
        weights = Weights(nc, s, 6)
        rope, swap = s.sb("rope", [P, 2, L]), s.sb("swap", [P, P])
        qg, sq, rs, tm = (s.sb(n, [P, L]) for n in ("qg", "sq", "rs", "tm"))
        res = s.sb("result", [P, 2, L])
        reg = [s.ps(f"r{b}", 1536) for b in range(2)]
        bank = s.ps("sums", 512), s.ps("swaps", 512)
        load = s.sem("loaded")
        read = [s.flag(f"region_read{b}", per=3, credit=1) for b in range(2)]
        gained = s.flag("q_gained", per=4)
        ss = s.flag("squares_summed", per=6)
        root = s.flag("root_done", per=6, credit=6)
        sw = s.flag("swapped", per=6)
        swr = s.flag("swaps_read", per=6, credit=6)
        sig = s.flag("sigmoid_done", per=4)
        made = s.flag("result_made", per=6, credit=6)
        stored = [s.flag(f"stored{b}", per=48, credit=16) for b in range(2)]
        steps = s.sem("dve_steps")
        win = a["w_in_even"].rearrange("(k p) n -> p k n", p=P)
        with nc.Block() as block:
            @block.sync
            def _(sp):
                sp.dma_start(rope[:, :, :], a["rope"]).then_inc(load, 16)
                sp.dma_start(swap[:, :], a["swap"]).then_inc(load, 16)
                with sp.Fori(0, KC // 2) as i:
                    for u in range(6):
                        weights.load(sp, i, u, win[:, :, bass.ds(i * 256 + (base[u % 3] + (u // 3) * P), P)])

            @block.gpsimd
            def _(gp):
                weights.split_all(gp, KC // 2, c["ones"])

            @block.tensor
            def _(pe):
                weights.used.start(pe)
                pe.wait_ge(load, 32)
                with pe.Fori(0, KC // 2) as i:
                    for u in range(6):
                        def between(k, u=u):
                            if u % 3 != 1 or k not in (2, 4, 6):
                                return
                            j, n = u // 3, k // 2 - 1
                            off, m = PIECES[n]
                            if n == 0:
                                gained.wait(pe, i, 2 * j + 2)
                            root.wait(pe, i, 3 * j + n)
                            nc.tensor.matmul(bank[0][:, 0:m], c["ones"][:, :], sq[:, off:off + m],
                                             start=True, stop=True).then_inc(ss.sem, 1)
                            swr.wait(pe, i, 3 * j + n)
                            nc.tensor.matmul(bank[1][:, 0:m], swap[:, :], qg[:, off:off + m],
                                             start=True, stop=True).then_inc(sw.sem, 1)
                        read[u % 2].wait(pe, i, u // 2)
                        weights.product(pe, i, u, reg[u % 2], pair(h), between=between)

            @block.scalar
            def _(act):
                for b in range(2):
                    stored[b].start(act)

                def store(i, u):
                    made.wait(act, i, u + 1)
                    act.dma_start(dest[u % 3][i * 2 + u // 3], res[:, u % 2, :]).then_inc(stored[u % 2].sem, 16)
                with act.Fori(0, KC // 2) as i:
                    for u in range(6):
                        weights.used.wait(act, i, u + 1)
                        j, r = u // 3, rows_of(reg[u % 2])
                        if u % 3 == 0:
                            made.wait(act, i, u - 2)
                            nc.scalar.activation(qg[:, :], r, ACT.Copy,
                                                 scale=c["col"]("q_norm", 0)).then_inc(gained.sem, 1)
                            nc.scalar.activation(sq[:, :], r, ACT.Square).then_inc(gained.sem, 1)
                            gained.wait(act, i, 2 * j + 2)
                            act.sem_inc(read[u % 2].sem, 1)
                            for n, (off, m) in enumerate(PIECES):
                                ss.wait(act, i, 3 * j + n + 1)
                                nc.scalar.activation(rs[:, off:off + m], bank[0][:, 0:m], ACT.Sqrt,
                                                     bias=c["eps"][:, :], scale=1.0 / HD).then_inc(root.sem, 1)
                        else:
                            stored[u % 2].wait(act, i, 16 * (u // 2))
                            nc.scalar.activation(res[:, u % 2, :], r, ACT.Sigmoid).then_inc(sig.sem, 1)
                        if u:
                            store(i, u - 1)
                    store(i, 5)
                for b in range(2):
                    stored[b].wait(act, KC // 2, 0)

            @block.vector
            def _(dve):
                v = nc.vector
                for x in (root, swr, made, read[0], read[1]):
                    x.start(dve)
                do = Steps(dve, steps)
                dve.wait_ge(load, 32)
                with do.loop(KC // 2, 2 * (3 + 3 + 2) + 2 + 4) as i:
                    for j in range(2):
                        u = 3 * j
                        b = u % 2
                        gained.wait(dve, i, 2 * j + 2)
                        stored[b].wait(dve, i, 16 * (u // 2))
                        do(v.tensor_tensor(res[:, b, :], qg[:, :], rope[:, 0, :], ALU.mult))
                        for n, (off, m) in enumerate(PIECES):
                            sw.wait(dve, i, 3 * j + n + 1)
                            do(v.tensor_tensor(tm[:, off:off + m], bank[1][:, 0:m], rope[:, 1, off:off + m], ALU.mult))
                            dve.sem_inc(swr.sem, 1)
                        for n, (off, m) in enumerate(PIECES):
                            root.wait(dve, i, 3 * j + n + 1)
                            ins = v.reciprocal(rs[:, off:off + m], rs[:, off:off + m])
                            do(ins) if n == 2 else do.free(ins)
                        do(v.tensor_tensor(res[:, b, :], res[:, b, :], tm[:, :], ALU.add))
                        do(v.tensor_tensor(res[:, b, :], res[:, b, :], rs[:, :], ALU.mult))
                        dve.sem_inc(made.sem, 1)
                        for g in range(2):
                            w = u + 1 + g
                            sig.wait(dve, i, 2 * j + g + 1)
                            do(v.tensor_tensor(res[:, w % 2, :], res[:, w % 2, :], rows_of(reg[w % 2]), ALU.mult))
                            dve.sem_inc(made.sem, 1)
                            dve.sem_inc(read[w % 2].sem, 1)


def heads(nc, c, d, kr, vt, t):
    REP = HEADS // KV
    NQ = len(QT)
    with stage(nc) as s:
        qf = s.sb("q", [P, 2, L])
        q = s.sb("q_hi", [P, L], F32R), s.sb("q_lo", [P, L], F32R)
        gate = s.sb("gate", [P, 2, L])
        prob = s.sb("prob", [P, 2, L])
        pt = s.sb("prob_t", [P, 2, NT, P])
        y = s.sb("y", [P, 2, L])
        mx, sm = s.sb("mx", [P, 2, 2]), s.sb("sm", [P, 2, 2])
        scan_tmp = s.sb("scan", [P, 2, 2, G])
        sreg, treg = s.ps("scores", 1536), s.ps("turned", 1536)
        op = [s.ps(f"o{b}", 512) for b in range(2)]
        ql = [s.sem(f"q_loaded{b}") for b in range(2)]
        hid = s.flag("q_hi_done", per=2)
        q_done = s.flag("q_split", per=2)
        sc = s.flag("scores_done", per=2 * NQ)
        mxd = s.flag("max_done", per=2 * NQ)
        ex = s.flag("exp_done", per=2 * NQ)
        nd = s.flag("normalised", per=2 * NQ)
        tu = s.flag("prob_turned", per=2 * NQ)
        tc = s.flag("turned_copied", per=2 * NQ * 2, credit=4)
        pv = s.flag("mixed", per=2 * NQ, credit=4)
        yd = s.flag("y_ready", per=2 * NQ, credit=2 * NQ)
        stored = [s.flag(f"stored{b}", per=16, credit=16) for b in range(2)]
        steps, scan_steps, scan_turns = s.sem("dve_steps"), s.sem("scan_steps"), s.sem("scan_turns")
        tview = treg[:, :].rearrange("p (b n) -> p b n", b=3)[:, :, 0:3 * P].rearrange("p b (k q) -> p b k q", k=3)
        with nc.Block() as block:
            @block.sync
            def _(sp):
                with sp.Fori(0, REP) as i:
                    for g in range(KV):
                        yd.wait(sp, i, g * NQ + NQ - 2 * NQ)
                        sp.dma_start(qf[:, g, :], d["q"][i + g * REP]).then_inc(ql[g], 16)
                        sp.dma_start(gate[:, g, :], d["ga"][i + g * REP]).then_inc(ql[g], 16)

            @block.gpsimd
            def _(gp):
                s5_scan(nc, gp, t, scan_tmp, scan_steps, scan_turns)

            @block.tensor
            def _(pe):
                pv.start(pe)
                with pe.Fori(0, REP) as i:
                    for g in range(KV):
                        def scores(t):
                            off, m = QT[t]
                            for o, n in PIECES:
                                for x, z in ((0, 1), (0, 0), (1, 0)):
                                    last = nc.tensor.matmul(sreg[0:m, PO + o:PO + o + n], q[x][:, off:off + m],
                                                            kr[z][:, g, o:o + n], start=(z == 1), stop=(x == 1))
                            last.then_inc(sc.sem, 1)

                        def turn(t):
                            off, m = QT[t]
                            for k, (ko, kn) in enumerate(TILES):
                                last = nc.tensor.transpose(tview[0:kn, k // 3, k % 3, 0:m],
                                                           prob[0:m, (g * NQ + t) % 2, ko:ko + kn],
                                                           c["ident"][0:m, 0:m])
                            last.then_inc(tu.sem, 1)

                        def mix(t):
                            off, m = QT[t]
                            b = (g * NQ + t) % 2
                            for k, (ko, kn) in enumerate(TILES):
                                last = nc.tensor.matmul(op[b][:, 0:m], vt[0:kn, k, g * HD:(g + 1) * HD],
                                                        pt[0:kn, b, k, 0:m], start=(k == 0), stop=(k == NT - 1))
                            last.then_inc(pv.sem, 1)

                        q_done.wait(pe, i, g + 1)
                        scores(0)
                        for t in range(NQ):
                            n = g * NQ + t
                            if t + 1 < NQ:
                                ex.wait(pe, i, n + 1)
                                scores(t + 1)
                            if t:
                                tc.wait(pe, i, 2 * n)
                                yd.wait(pe, i, n - 2)
                                mix(t - 1)
                            nd.wait(pe, i, n + 1)
                            turn(t)
                        tc.wait(pe, i, 2 * (g + 1) * NQ)
                        yd.wait(pe, i, (g + 1) * NQ - 2)
                        mix(NQ - 1)

            @block.scalar
            def _(act):
                for b in range(2):
                    stored[b].start(act)
                with act.Fori(0, REP) as i:
                    for g in range(KV):
                        act.wait_ge(ql[g], i * 32 + 32)
                        nc.scalar.activation(q[0][:, :], qf[:, g, :], ACT.Copy).then_inc(hid.sem, 1)
                        for t in range(NQ + 1):
                            n = g * NQ + t
                            if t < NQ:
                                off, m = QT[t]
                                mxd.wait(act, i, n + 1)
                                if t >= 2:
                                    tu.wait(act, i, n - 1)
                                nc.scalar.activation(prob[0:m, n % 2, :], rows_of(sreg)[0:m], ACT.Exp,
                                                     bias=mx[0:m, n % 2, 1:2], scale=SCALE,
                                                     accum_out=sm[0:m, n % 2, 0:1]).then_inc(ex.sem, 1)
                            if t:
                                off, m = QT[t - 1]
                                tu.wait(act, i, n)
                                pv.wait(act, i, n - 2)
                                b = (n - 1) % 2
                                nc.scalar.activation(pt[:, b, 0:3, 0:m], tview[:, 0, :, 0:m], ACT.Copy)
                                nc.scalar.activation(pt[:, b, 3:6, 0:m], tview[:, 1, :, 0:m],
                                                     ACT.Copy).then_inc(tc.sem, 1)
                        yd.wait(act, i, (g + 1) * NQ)
                        act.dma_start(d["cat"][i + g * REP], y[:, g, :]).then_inc(stored[g].sem, 16)
                for b in range(2):
                    stored[b].wait(act, REP, 0)

            @block.vector
            def _(dve):
                v = nc.vector
                for x in (yd, tc):
                    x.start(dve)
                do = Steps(dve, steps)
                with do.loop(REP, 2 * (1 + 2 * NQ)) as i:
                    for g in range(KV):
                        hid.wait(dve, i, g + 1)
                        do(v.tensor_tensor(q[1][:, :], qf[:, g, :], q[0][:, :].bitcast(F32), ALU.subtract))
                        dve.sem_inc(q_done.sem, 1)
                        stored[g].wait(dve, i, 0)
                        for t in range(NQ + 1):
                            n = g * NQ + t
                            if t < NQ:
                                off, m = QT[t]
                                sc.wait(dve, i, n + 1)
                                do(v.tensor_reduce(mx[0:m, n % 2, 0:1], rows_of(sreg)[0:m], AX, ALU.max))
                                v.tensor_scalar(mx[0:m, n % 2, 1:2], mx[0:m, n % 2, 0:1], -SCALE, None,
                                                ALU.mult).then_inc(mxd.sem, 1)
                            if t:
                                off, m = QT[t - 1]
                                tu.wait(dve, i, n)
                                pv.wait(dve, i, n - 2)
                                b = (n - 1) % 2
                                v.tensor_copy(pt[:, b, 6:8, 0:m], tview[:, 2, 0:2, 0:m])
                                v.tensor_copy(pt[0:TILES[-1][1], b, 8, 0:m],
                                              tview[0:TILES[-1][1], 2, 2, 0:m]).then_inc(tc.sem, 1)
                            if t < NQ:
                                off, m = QT[t]
                                ex.wait(dve, i, n + 1)
                                do(v.reciprocal(sm[0:m, n % 2, 1:2], sm[0:m, n % 2, 0:1]))
                                v.tensor_scalar(prob[0:m, n % 2, :], prob[0:m, n % 2, :], sm[0:m, n % 2, 1:2], None,
                                                ALU.mult).then_inc(nd.sem, 1)
                            if t:
                                off, m = QT[t - 1]
                                pv.wait(dve, i, n)
                                v.tensor_tensor(y[:, g, off:off + m], op[(n - 1) % 2][:, 0:m],
                                                gate[:, g, off:off + m], ALU.mult).then_inc(yd.sem, 1)


def s5_glu(nc, a, c, d):
    with stage(nc) as s:
        weights = Weights(nc, s, 2)
        y = s.sb("y", [P, KC, L])
        yr = [s.sb(n, [P, KC, L], F32R) for n in ("y_hi", "y_lo")]
        yin = s.sb("y_in", [P, 2, T, CH])
        sg, gate, out = s.sb("sigmoid", [P, 2, L]), s.sb("gate", [P, 2, L]), s.sb("out", [P, 2, L])
        reg = [s.ps(f"r{b}", 1536) for b in range(2)]
        yl = [s.sem(f"y_loaded{b}") for b in range(2)]
        gl = [s.sem(f"gate_loaded{b}") for b in range(2)]
        gelu, hid, lod = s.sem("gelu_done"), s.sem("hi_done"), s.sem("lo_done")
        sig = s.flag("sigmoid_done", per=2, credit=2)
        gated = s.flag("gated", per=2, credit=2)
        stored = [s.flag(f"stored{b}", per=16, credit=16) for b in range(2)]
        steps = s.sem("dve_steps")
        yv = d["y"].rearrange("(j g) p s c -> j (g p) (s c)", j=KC)
        glu = a["w_glu"].rearrange("(k p) n -> p k n", p=P)
        with nc.Block() as block:
            @block.sync
            def _(sp):
                for j in range(KC):
                    if j >= 2:
                        sp.wait_ge(gelu, j - 1)
                    sp.dma_start(yin[:, j % 2, :, :], yv[j]).then_inc(yl[j % 2], 16)
                with sp.Fori(0, KC // 2) as i:
                    for b in range(2):
                        weights.load(sp, i, b, glu[:, :, bass.ds(i * 256 + b * P, P)])
                        gated.wait(sp, i, b - 1)
                        sp.dma_start(gate[:, b, :], d["gb"][i * 2 + b]).then_inc(gl[b], 16)

            @block.gpsimd
            def _(gp):
                weights.split_all(gp, KC // 2, c["ones"])

            @block.tensor
            def _(pe):
                weights.used.start(pe)
                pe.wait_ge(lod, KC)
                with pe.Fori(0, KC // 2) as i:
                    for b in range(2):
                        sig.wait(pe, i, b - 1)
                        weights.product(pe, i, b, reg[b], pair(yr))

            @block.scalar
            def _(act):
                sig.start(act)
                for b in range(2):
                    stored[b].start(act)
                for j in range(KC):
                    act.wait_ge(yl[j % 2], 16 * (j // 2 + 1))
                    nc.scalar.activation(y[:, j, :].rearrange("p (c s) -> p s c", s=T), yin[:, j % 2, :, :],
                                         ACT.Gelu_apprx_tanh).then_inc(gelu, 1)
                    act.wait_ge(gelu, j + 1)
                    nc.scalar.activation(yr[0][:, j, :], y[:, j, :], ACT.Copy).then_inc(hid, 1)
                with act.Fori(0, KC // 2) as i:
                    for b in range(2):
                        weights.used.wait(act, i, b + 1)
                        gated.wait(act, i, b - 1)
                        nc.scalar.activation(sg[:, b, :], rows_of(reg[b]), ACT.Sigmoid,
                                             bias=c["cols_a"][:, bass.ds(i * 2 + (c["b_glu"] + b), 1)]
                                             ).then_inc(sig.sem, 1)
                    for b in range(2):
                        gated.wait(act, i, b + 1)
                        act.dma_start(d["cat"][i * 2 + (KC + b)], out[:, b, :]).then_inc(stored[b].sem, 16)
                for b in range(2):
                    stored[b].wait(act, KC // 2, 0)

            @block.vector
            def _(dve):
                gated.start(dve)
                do = Steps(dve, steps)
                for j in range(KC):
                    dve.wait_ge(hid, j + 1)
                    nc.vector.tensor_tensor(yr[1][:, j, :], y[:, j, :], yr[0][:, j, :].bitcast(F32),
                                            ALU.subtract).then_inc(lod, 1)
                with do.loop(KC // 2, 2) as i:
                    for b in range(2):
                        dve.wait_ge(gl[b], i * 16 + 16)
                        stored[b].wait(dve, i, 0)
                        do(nc.vector.tensor_tensor(out[:, b, :], gate[:, b, :],
                                                   y[:, bass.ds(i * 2 + b, 1), :].rearrange("p k t -> p (k t)"),
                                                   ALU.mult))
                        sig.wait(dve, i, b + 1)
                        nc.vector.tensor_tensor(out[:, b, :], out[:, b, :], sg[:, b, :],
                                                ALU.mult).then_inc(gated.sem, 1)


def project(nc, w_out, cat, z, c, y):
    SLOTS = 4
    with stage(nc) as s:
        x = [s.sb(n, [P, 2 * KC, L], F32R) for n in ("x_hi", "x_lo")]
        weights = Weights(nc, s, 4)
        reg = [s.ps(f"r{b}", 1536) for b in range(2)]
        xl = [s.sem(f"x_loaded{b}") for b in range(SLOTS)]
        muld, hid, lod = s.sem("x_times_z"), s.sem("hi_done"), s.sem("lo_done")
        cop = s.flag("copied", per=2, credit=2)
        steps = s.sem("dve_steps")
        wv = w_out.rearrange("(h k p) n -> h p k n", p=P, k=KC)
        parts = 1 if z is None else 2
        raw = [y[:, b, :] for b in range(2 * SLOTS)]
        with nc.Block() as block:
            @block.sync
            def _(sp):
                with sp.Fori(0, KC // 2) as i:
                    for u in range(4):
                        weights.load(sp, i, u, wv[u % 2, :, :, bass.ds(i * 256 + (u // 2) * P, P)])

            @block.gpsimd
            def _(gp):
                weights.split_all(gp, KC // 2, c["ones"])

            @block.tensor
            def _(pe):
                weights.used.start(pe)
                with pe.Fori(0, KC // 2) as i:
                    for u in range(4):
                        def rows(k, u=u):
                            k += KC * (u % 2)
                            pe.wait_ge(lod, k + 1)
                            return x[0][:, k, :], x[1][:, k, :]
                        if u % 2 == 0:
                            cop.wait(pe, i, u // 2 - 1)
                        weights.product(pe, i, u, reg[u // 2], rows, first=(u % 2 == 0), last=(u % 2 == 1))

            @block.scalar
            def _(act):
                cop.start(act)
                for k in range(2 * KC + SLOTS - 1):
                    if k < 2 * KC:
                        if k >= SLOTS:
                            act.wait_ge(lod, k - SLOTS + 1)
                        act.dma_start(raw[k % SLOTS], cat[k]).then_inc(xl[k % SLOTS], 16)
                        if z is not None:
                            act.dma_start(raw[SLOTS + k % SLOTS], z[k]).then_inc(xl[k % SLOTS], 16)
                    t = k - SLOTS + 1
                    if t >= 0:
                        if z is None:
                            act.wait_ge(xl[t % SLOTS], 16 * (t // SLOTS + 1))
                        else:
                            act.wait_ge(muld, t + 1)
                        nc.scalar.activation(x[0][:, t, :], raw[t % SLOTS], ACT.Copy).then_inc(hid, 1)
                with act.Fori(0, KC // 2) as i:
                    for b in range(2):
                        weights.used.wait(act, i, 2 * b + 2)
                        nc.scalar.activation(y[:, bass.ds(i * 2 + b, 1), :].rearrange("p k t -> p (k t)"),
                                             rows_of(reg[b]), ACT.Copy).then_inc(cop.sem, 1)

            @block.vector
            def _(dve):
                for k in range(2 * KC + 1):
                    if z is not None and k < 2 * KC:
                        dve.wait_ge(xl[k % SLOTS], 16 * parts * (k // SLOTS + 1))
                        nc.vector.tensor_tensor(raw[k % SLOTS], raw[k % SLOTS], raw[SLOTS + k % SLOTS],
                                                ALU.mult).then_inc(muld, 1)
                    if k:
                        t = k - 1
                        dve.wait_ge(hid, k)
                        nc.vector.tensor_tensor(x[1][:, t, :], raw[t % SLOTS], x[0][:, t, :].bitcast(F32),
                                                ALU.subtract).then_inc(lod, 1)


def leave(nc, c, res, out):
    with stage(nc) as s:
        ot = s.sb("ot", [P, 2, D])
        pt = [s.ps(f"pt{b}", 512) for b in range(4)]
        turned, copied, stored = s.sem("turned"), s.sem("copied"), [s.sem("stored0"), s.sem("stored1")]
        n_tiles = (L - META) // P
        with nc.Block() as block:
            @block.tensor
            def _(pe):
                for i in range(n_tiles):
                    for half in range(2):
                        n = 2 * i + half
                        if n >= 4:
                            pe.wait_ge(copied, n - 3)
                        for k in range(4):
                            last = nc.tensor.transpose(pt[n % 4][:, k * P:(k + 1) * P],
                                                       res[:, 4 * half + k, META + i * P:META + (i + 1) * P],
                                                       c["ident"][:, :])
                        last.then_inc(turned, 1)

            @block.vector
            def _(dve):
                for n in range(2 * n_tiles):
                    i = n // 2
                    dve.wait_ge(turned, n + 1)
                    if i >= 2 and n % 2 == 0:
                        dve.wait_ge(stored[i % 2], 16 * (i // 2))
                    nc.vector.tensor_copy(ot[:, i % 2, 512 * (n % 2):512 * (n % 2) + 512],
                                          pt[n % 4][:, :]).then_inc(copied, 1)

            @block.sync
            def _(sp):
                for i in range(n_tiles):
                    sp.wait_ge(copied, 2 * i + 2)
                    sp.dma_start(out[i * P:(i + 1) * P, :], ot[:, i % 2, :]).then_inc(stored[i % 2], 16)
                for b in range(2):
                    sp.wait_ge(stored[b], 16 * n_tiles // 2)


def conv_values_z(nc, a, c, d, h):
    EDGE = CONV // 2
    with stage(nc) as s:
        weights = Weights(nc, s, 4)
        wv = s.sb("w_v", [P, 2, MV])
        xm = s.sb("xm", [P, 2, L + 2 * EDGE])
        acc, sg, zs = s.sb("acc", [P, 2, L]), s.sb("sg", [P, 2, L]), s.sb("zs", [P, 2, L])
        vs = s.sb("vs", [P, NT, MV])
        reg = [s.ps(f"r{b}", 1536) for b in range(2)]
        vp = [s.ps(f"v{b}", 512) for b in range(2)]
        wvl = s.sem("wv_loaded")
        cop = s.flag("xm_copied", per=2, credit=2)
        vmm = s.flag("v_projected", per=NT, credit=NT)
        vcop = s.flag("v_copied", per=NT, credit=NT)
        conv = s.flag("convolved", per=2, credit=2)
        sig = s.flag("sigmoid_done", per=2)
        zsig = s.flag("z_sigmoid_done", per=2)
        zdone = s.flag("z_done", per=2, credit=2)
        act_done = s.flag("xc_done", per=2, credit=2)
        stored = [s.flag(f"stored_{n}", per=16, credit=16) for n in ("v", "xc", "z")]
        steps = s.sem("dve_steps")
        win = a["w_in_odd"].rearrange("(k p) n -> p k n", p=P)
        wvv = a["w_v"].rearrange("h (c p) n -> h p c n", p=P)
        with nc.Block() as block:
            @block.sync
            def _(sp):
                with sp.Fori(0, MH) as i:
                    for u in range(4):
                        weights.load(sp, i, u, win[:, :, bass.ds(i * 256 + (W2 * (u // 2) + (u % 2) * P), P)])
                        if u == 1:
                            vmm.wait(sp, i, 0)
                            sp.dma_start(wv[:, :, :], wvv[i]).then_inc(wvl, 16)

            @block.gpsimd
            def _(gp):
                weights.split_all(gp, MH, c["ones"])

            @block.tensor
            def _(pe):
                weights.used.start(pe)
                vmm.start(pe)
                with pe.Fori(0, MH) as i:
                    for b in range(2):
                        zdone.wait(pe, i, b - 1)
                        weights.product(pe, i, b, reg[b], pair(h))
                    cop.wait(pe, i, 1)
                    weights.product(pe, i, 2, reg[0], pair(h))
                    pe.wait_ge(wvl, i * 16 + 16)
                    cop.wait(pe, i, 2)
                    for t, (off, m) in enumerate(TILES):
                        vcop.wait(pe, i, t - 1)
                        for b in range(2):
                            last = nc.tensor.matmul(vp[t % 2][0:m, 0:MV], xm[:, b, EDGE + off:EDGE + off + m],
                                                    wv[:, b, :], start=(b == 0), stop=(b == 1))
                        last.then_inc(vmm.sem, 1)
                    weights.product(pe, i, 3, reg[1], pair(h))
                    vcop.wait(pe, i, NT)

            @block.scalar
            def _(act):
                cop.start(act)
                vcop.start(act)
                for x in stored:
                    x.start(act)
                with act.Fori(0, MH) as i:
                    for b in range(2):
                        weights.used.wait(act, i, b + 1)
                        conv.wait(act, i, b - 1)
                        vmm.wait(act, i, 0)
                        nc.scalar.activation(xm[:, b, EDGE:EDGE + L], rows_of(reg[b]), ACT.Copy).then_inc(cop.sem, 1)
                    weights.used.wait(act, i, 3)
                    stored[2].wait(act, i, 0)
                    nc.scalar.activation(zs[:, 0, :], rows_of(reg[0]), ACT.Sigmoid).then_inc(zsig.sem, 1)
                    stored[0].wait(act, i, 0)
                    for t, (off, m) in enumerate(TILES):
                        vmm.wait(act, i, t + 1)
                        nc.scalar.activation(vs[0:m, t, :], vp[t % 2][0:m, 0:MV], ACT.Copy).then_inc(vcop.sem, 1)
                    vcop.wait(act, i, NT)
                    act.dma_start(d["v"][i], vs[:, :, :]).then_inc(stored[0].sem, 16)
                    stored[1].wait(act, i, 0)
                    for b in range(2):
                        conv.wait(act, i, b + 1)
                        nc.scalar.activation(sg[:, b, :], acc[:, b, :], ACT.Sigmoid).then_inc(sig.sem, 1)
                    act_done.wait(act, i, 2)
                    act.dma_start(d["xc"][bass.ds(i * 2, 2), :, :].rearrange("b p t -> p b t"), sg[:, :, :])\
                        .then_inc(stored[1].sem, 16)
                    weights.used.wait(act, i, 4)
                    nc.scalar.activation(zs[:, 1, :], rows_of(reg[1]), ACT.Sigmoid).then_inc(zsig.sem, 1)
                    zdone.wait(act, i, 2)
                    act.dma_start(d["z"][bass.ds(i * 2, 2), :, :].rearrange("b p t -> p b t"), zs[:, :, :])\
                        .then_inc(stored[2].sem, 16)
                for x in stored:
                    x.wait(act, MH, 0)

            @block.vector
            def _(dve):
                do = Steps(dve, steps)
                do.free(nc.vector.memset(vs[:, NT - 1, :], 0.0))
                for b in range(2):
                    do.free(nc.vector.memset(xm[:, b, 0:EDGE], 0.0))
                    do(nc.vector.memset(xm[:, b, EDGE + L:], 0.0))
                conv.start(dve)
                act_done.start(dve)
                zdone.start(dve)
                with do.loop(MH, 2 * (CONV - 1)) as i:
                    def tap(n, b):
                        return c["conv_w"][:, bass.ds(i * 2 + (n * 2 * KC + b), 1)]

                    def z(b):
                        zsig.wait(dve, i, b + 1)
                        nc.vector.tensor_tensor(zs[:, b, :], zs[:, b, :], rows_of(reg[b]),
                                                ALU.mult).then_inc(zdone.sem, 1)
                    for b in range(2):
                        cop.wait(dve, i, b + 1)
                        act_done.wait(dve, i, b - 1)
                        do(nc.vector.tensor_scalar(acc[:, b, :], xm[:, b, 0:L], tap(0, b),
                                                   c["cols_a"][:, bass.ds(i * 2 + (c["conv_b"] + b), 1)],
                                                   ALU.mult, ALU.add))
                        for n in range(1, CONV):
                            ins = nc.vector.scalar_tensor_tensor(acc[:, b, :], xm[:, b, n:n + L], tap(n, b),
                                                                 acc[:, b, :], ALU.mult, ALU.add)
                            if n < CONV - 1:
                                do(ins)
                        ins.then_inc(conv.sem, 1)
                    z(0)
                    for b in range(2):
                        sig.wait(dve, i, b + 1)
                        nc.vector.tensor_tensor(sg[:, b, :], acc[:, b, :], sg[:, b, :],
                                                ALU.mult).then_inc(act_done.sem, 1)
                    z(1)


def odd_gates(nc, a, c, d, raw):
    SLOTS = 4
    F, B = slice(0, MH), slice(32, 40)
    with stage(nc) as s:
        x = [s.sb(n, [P, 2 * KC, L], F32R) for n in ("xc_hi", "xc_lo")]
        weights = Weights(nc, s, 6, tiles=(2, 2, KC, KC, KC, KC))
        buf = s.sb("buffer", [P, SLOTS, L])
        kt = s.sb("kt", [P, NT, MK])
        wg = s.sb("wg", [P, 2 * KC, 104])
        bias = s.sb("bias", [P, 1])
        reg = [s.ps(f"r{b}", 1536) for b in range(2)]
        bank = [s.ps(f"kt{b}", 512) for b in range(2)]
        xl = [s.sem(f"x_loaded{b}") for b in range(SLOTS)]
        cleared, wld = s.sem("cleared"), s.sem("gate_weights_loaded")
        gmm, copied = s.sem("gate_products"), s.sem("gates_copied")
        hid, lod = s.sem("hi_done"), s.sem("lo_done")
        read = s.flag("region_read", per=4, credit=2)
        ktt = s.flag("kt_turned", per=3)
        ktc = s.flag("kt_copied", per=3, credit=3)
        stored = [s.flag(f"stored_{n}", per=16, credit=16) for n in ("q", "k", "o0", "o1", "kt")]
        wog = a["w_ogate"].rearrange("(h k p) n -> h p k n", p=P, k=KC)
        wqv = [a[n].rearrange("h (c p) n -> h p c n", p=P) for n in ("w_q", "w_k")]
        N = NT - 1
        parts = [(0, 4, 0), (4, 8, 1), (8, 9, 0)]
        with nc.Block() as block:
            @block.sync
            def _(sp):
                sp.wait_ge(cleared, 1)
                for n, name in enumerate(("igate", "fgate")):
                    for r in range(2):
                        at = 64 * n + 32 * r
                        sp.dma_start(wg[:, :, at:at + MH],
                                     a["w_" + name][r].rearrange("(k p) h -> p k h", p=P)).then_inc(wld, 16)
                        sp.dma_start(bias[at:at + MH, :], a["b_" + name][r].unsqueeze(1)).then_inc(wld, 16)
                with sp.Fori(0, MH) as i:
                    for u in range(6):
                        if u < 2:
                            weights.load(sp, i, u, wqv[u][i])
                        else:
                            weights.load(sp, i, u, wog[u % 2, :, :, bass.ds(i * 256 + (u // 2 - 1) * P, P)])

            @block.gpsimd
            def _(gp):
                weights.split_all(gp, MH, c["ones"])

            @block.tensor
            def _(pe):
                weights.used.start(pe)
                pe.wait_ge(wld, 16 * 8)
                for k in range(2 * KC):
                    pe.wait_ge(xl[k % SLOTS], 16 * (k // SLOTS + 1))
                    for off, n in PIECES:
                        last = nc.tensor.matmul(reg[0][0:104, PO + off:PO + off + n], wg[:, k, :],
                                                buf[:, k % SLOTS, off:off + n],
                                                start=(k == 0), stop=(k == 2 * KC - 1))
                    last.then_inc(gmm, 1)
                pe.wait_ge(lod, 2 * KC)
                pe.wait_ge(copied, 4)
                with pe.Fori(0, MH) as i:
                    for u in range(2):
                        def rows(k):
                            return tuple(z[:, bass.ds(i * 2 + k, 1), :].rearrange("p k t -> p (k t)") for z in x)
                        read.wait(pe, i, u - 1)
                        weights.product(pe, i, u, reg[u], rows)
                    for u in range(2, 6):
                        def rows(k, u=u):
                            k += KC * (u % 2)
                            return x[0][:, k, :], x[1][:, k, :]

                        def between(k, u=u):
                            if u != 3 or k not in (0, 2, 4):
                                return
                            n = k // 2
                            t0, t1, b = parts[n]
                            if n == 0:
                                read.wait(pe, i, 2)
                            ktc.wait(pe, i, (0, 0, 1)[n])
                            for t in range(t0, t1):
                                off, m = TILES[t]
                                last = nc.tensor.transpose(bank[b][0:m, (t - t0) * P:(t - t0 + 1) * P],
                                                           buf[:, 1, off:off + m], c["ident"][:, :])
                            last.then_inc(ktt.sem, 1)
                        if u % 2 == 0:
                            read.wait(pe, i, u // 2)
                        weights.product(pe, i, u, reg[u // 2 - 1], rows, first=(u % 2 == 0), last=(u % 2 == 1),
                                        between=between)

            @block.scalar
            def _(act):
                for x_ in stored:
                    x_.start(act)
                for k in range(2 * KC + SLOTS - 1):
                    if k < 2 * KC:
                        if k >= SLOTS:
                            act.wait_ge(lod, k - SLOTS + 1)
                            act.wait_ge(gmm, k - SLOTS + 1)
                        act.dma_start(buf[:, k % SLOTS, :], d["xc"][k]).then_inc(xl[k % SLOTS], 16)
                    t = k - SLOTS + 1
                    if t >= 0:
                        act.wait_ge(xl[t % SLOTS], 16 * (t // SLOTS + 1))
                        nc.scalar.activation(x[0][:, t, :], buf[:, t % SLOTS, :], ACT.Copy).then_inc(hid, 1)
                act.wait_ge(gmm, 2 * KC)
                act.wait_ge(cleared, 2)
                act.wait_ge(lod, 2 * KC)
                g = rows_of(reg[0])
                for dst, at in ((raw[0], 0), (raw[1], 64)):
                    nc.scalar.activation(dst[F, :], g[at:at + MH], ACT.Identity,
                                         bias=bias[at:at + MH, :]).then_inc(copied, 1)
                    nc.scalar.activation(dst[B, :], g[at + 32:at + 32 + MH, ::-1], ACT.Identity,
                                         bias=bias[at + 32:at + 32 + MH, :]).then_inc(copied, 1)
                read.start(act)
                with act.Fori(0, MH) as i:
                    weights.used.wait(act, i, 1)
                    stored[0].wait(act, i, 0)
                    nc.scalar.activation(buf[:, 0, :], rows_of(reg[0]), ACT.Copy,
                                         scale=MK ** -0.5).then_inc(read.sem, 1)
                    weights.used.wait(act, i, 2)
                    stored[1].wait(act, i, 0)
                    nc.scalar.activation(buf[:, 1, :], rows_of(reg[1]), ACT.Copy).then_inc(read.sem, 1)
                    for n in range(2):
                        read.wait(act, i, n + 1)
                        act.dma_start(d["qk"][i][n], buf[:, n, :]).then_inc(stored[n].sem, 16)
                    for b in range(2):
                        weights.used.wait(act, i, 2 * b + 4)
                        stored[2 + b].wait(act, i, 0)
                        nc.scalar.activation(buf[:, 2 + b, :], rows_of(reg[b]), ACT.Sigmoid,
                                             bias=c["cols_a"][:, bass.ds(i * 2 + (c["b_ogate"] + b), 1)]
                                             ).then_inc(read.sem, 1)
                        read.wait(act, i, b + 3)
                        act.dma_start(d["o"][i * 2 + b], buf[:, 2 + b, :]).then_inc(stored[2 + b].sem, 16)
                    ktc.wait(act, i, 3)
                    act.dma_start(d["kt"][i], kt[:, :, :]).then_inc(stored[4].sem, 16)
                for x_ in stored:
                    x_.wait(act, MH, 0)

            @block.vector
            def _(dve):
                v = nc.vector
                v.memset(wg[:, :, :], 0.0).then_inc(cleared, 1)
                v.memset(raw[0][:, :], 0.0)
                v.memset(kt[:, N, :], 0.0)
                v.memset(raw[1][:, :], 0.0).then_inc(cleared, 1)
                ktc.start(dve)
                for k in range(2 * KC):
                    dve.wait_ge(hid, k + 1)
                    v.tensor_tensor(x[1][:, k, :], buf[:, k % SLOTS, :], x[0][:, k, :].bitcast(F32),
                                    ALU.subtract).then_inc(lod, 1)
                with dve.Fori(0, MH) as i:
                    for n, (t0, t1, b) in enumerate(parts):
                        ktt.wait(dve, i, n + 1)
                        if n == 0:
                            stored[4].wait(dve, i, 0)
                        m = TILES[t1 - 1][1]
                        v.tensor_copy(kt[0:m, t0:t1, :],
                                      bank[b][0:m, 0:(t1 - t0) * P].rearrange("p (t k) -> p t k", k=MK)
                                      ).then_inc(ktc.sem, 1)


def gate_rows(nc, a, c, d, raw, cols):
    R = 40
    F, B = slice(0, MH), slice(32, 40)
    with stage(nc) as s:
        keep = s.sb("keep", [R, L])
        li, fx = raw
        lf, e1, mn = (s.sb(n, [R, L]) for n in ("lf", "e1", "mn"))
        b_, m_ = s.sb("b", [R, L]), s.sb("m", [R, L])
        bn, m_n, ln = s.sb("bn", [R, L]), s.sb("mn2", [R, L]), s.sb("ln", [R, L])
        row = s.sb("row", [R, 3, L])
        bm = s.sb("bm", [R, L])
        end = s.sb("end", [R, 6, NT])
        ends = s.sb("ends", [R, 2, NT])
        tp = [s.ps(f"tp{q}", 512) for q in range(3)]
        load = s.sem("loaded")
        logged = s.sem("log_done")
        asked, answered = s.sem("function_asked"), s.sem("function_done")
        rows, turned, stored = s.sem("rows_ready"), s.sem("turned"), s.sem("stored")
        steps, asteps = s.sem("dve_steps"), s.sem("act_steps")
        with nc.Block() as block:
            @block.sync
            def _(sp):
                sp.dma_start(keep[:, :], a["starts"]).then_inc(load, 16)
                sp.wait_ge(rows, 1)
                for r, part in enumerate((F, B)):
                    sp.dma_start(d["bm"][r], bm[part, :]).then_inc(stored, 16)
                    sp.dma_start(d["ends"][r], ends[part, :, :]).then_inc(stored, 16)
                sp.wait_ge(stored, 64)

            @block.tensor
            def _(pe):
                pe.wait_ge(rows, 1)
                for q in range(3):
                    for t, (off, m) in enumerate(TILES):
                        last = nc.tensor.transpose(tp[q][0:m, R * t:R * t + R], row[:, q, off:off + m],
                                                   c["ident"][0:R, 0:R])
                    last.then_inc(turned, 1)

            @block.scalar
            def _(act):
                do = Steps(act, asteps)
                do(nc.scalar.activation(e1[:, :], fx[:, :], ACT.Abs))
                do(nc.scalar.activation(e1[:, :], e1[:, :], ACT.Exp, scale=-1.0))
                nc.scalar.activation(lf[:, :], e1[:, :], ACT.Ln, bias=1.0).then_inc(logged, 1)
                act.wait_ge(asked, 1)
                nc.scalar.activation(row[:, 1, :], row[:, 1, :], ACT.Exp)
                nc.scalar.activation(row[:, 2, :], m_n[:, :], ACT.Exp, scale=-1.0)
                nc.scalar.activation(ends[:, 1, :], end[:, 4, :], ACT.Exp).then_inc(answered, 1)

            @block.vector
            def _(dve):
                v = nc.vector
                do = Steps(dve, steps)
                for x in (bn, m_n, ln):
                    do.free(v.memset(x[:, :], 0.0))
                do.free(v.memset(end[:, :, :], 0.0))
                do(v.memset(cols[:, NT - 1, :, :], 0.0))
                dve.wait_ge(load, 16)
                dve.wait_ge(logged, 1)
                do(v.tensor_scalar(mn[:, :], fx[:, :], 0.0, None, ALU.min))
                do(v.tensor_tensor(lf[:, :], mn[:, :], lf[:, :], ALU.subtract))
                do.free(v.tensor_tensor_scan(b_[:, :], keep[:, :], lf[:, :], 0.0, ALU.mult, ALU.add))
                do(v.tensor_tensor_scan(m_[:, :], lf[:, :], li[:, :], 0.0, ALU.add, ALU.max))
                for dst, src in ((bn, b_), (m_n, m_), (ln, li)):
                    do.free(v.tensor_copy(dst[F, :], src[F, :]))
                    do(v.tensor_copy(dst[B, :], src[B, ::-1]))
                N = NT - 1
                for q, src in ((0, bn), (1, m_n)):
                    do.free(v.tensor_copy(end[F, q, 0:N], src[F, P - 1:N * P:P]))
                    do.free(v.tensor_copy(end[F, q, N:NT], src[F, L - 1:L]))
                    do(v.tensor_copy(end[B, q, 0:NT], src[B, 0:L:P]))
                do.free(v.tensor_copy(end[F, 2, 1:NT], end[F, 1, 0:N]))
                do(v.tensor_copy(end[B, 2, 0:N], end[B, 1, 1:NT]))
                do(v.tensor_copy(ends[:, 0, :], end[:, 2, :]))
                do(v.tensor_tensor(end[:, 3, :], end[:, 0, :], end[:, 1, :], ALU.subtract))
                do(v.tensor_tensor(end[:, 4, :], end[:, 3, :], end[:, 2, :], ALU.add))
                do(v.tensor_tensor(row[:, 0, :], ln[:, :], bn[:, :], ALU.subtract))
                do(v.tensor_tensor(bm[:, :], bn[:, :], m_n[:, :], ALU.subtract))
                for t, (off, m) in enumerate(TILES):
                    do(v.tensor_scalar(row[:, 1, off:off + m], row[:, 0, off:off + m], end[:, 3, t:t + 1], None, ALU.add))
                dve.sem_inc(asked, 1)
                dve.wait_ge(answered, 1)
                dve.sem_inc(rows, 1)
                for q in range(3):
                    dve.wait_ge(turned, q + 1)
                    view = tp[q][:, 0:R * NT].rearrange("p (t r) -> p t r", r=R)
                    v.tensor_copy(cols[:, 0:N, q, :], view[:, 0:N, :])
                    v.tensor_copy(cols[0:TILES[N][1], N, q, :], view[0:TILES[N][1], N, :])


def mlstm(nc, a, c, d, cols):
    LS, WS, FLOOR = 0, 1, 2
    N = NT - 1
    VW = MV + 1
    LANES = range(2)
    with stage(nc) as s:
        def lanes(make, name, *args, **kw):
            return [make(f"{name}{l}", *args, **kw) for l in LANES]
        masks = s.sb("masks", [P, 2, P])
        endb = s.sb("ends_b", [P, 2, MH, 2, NT])
        v1 = [lanes(s.sb, f"v{b}_", [P, NT, VW]) for b in range(2)]
        qk = [lanes(s.sb, f"qk{b}_", [P, 2, L]) for b in range(2)]
        kt = [lanes(s.sb, f"kt{b}_", [P, NT, MK]) for b in range(2)]
        bmb = lanes(s.sb, "bm_b", [P, 2, L])
        xc, og = lanes(s.sb, "xc", [P, 2, L]), lanes(s.sb, "og", [P, 2, L])
        kw = lanes(s.sb, "kw", [P, 2, MK])
        cb, cf = lanes(s.sb, "state_b", [P, N, VW]), lanes(s.sb, "state_f", [P, 2, VW])
        D_, qe = lanes(s.sb, "D", [P, 2, P]), lanes(s.sb, "qe", [P, 2, P])
        sw, qs = lanes(s.sb, "sw", [P, 2, P]), lanes(s.sb, "qs", [P, 2, P])
        dn, rd = lanes(s.sb, "dn", [P, 2]), lanes(s.sb, "rd", [P, 2])
        hf, hs = lanes(s.sb, "hf", [P, MV]), lanes(s.sb, "hs", [P, NT, MV])
        ssq, rstd = lanes(s.sb, "ssq", [P, NT]), lanes(s.sb, "rstd", [P, NT])
        psum = s.ps("psum", 4096)
        R = [psum[:, 2048 * l:2048 * l + 2048] for l in LANES]
        kq = [R[l][:, 0:512] for l in LANES]
        hbank = [(R[l][:, 512:1024], R[l][:, 1024:1536]) for l in LANES]
        ub = [R[l][:, 1536:2048] for l in LANES]
        turned_at = [(R[l][:, 0:L], R[l][:, 7 * P:7 * P + L]) for l in LANES]
        once, ones_set = s.sem("once_loaded"), s.sem("ones_set")
        kvl = [lanes(s.sem, f"kv{b}_loaded") for b in range(2)]
        qkl = [lanes(s.sem, f"qk{b}_loaded") for b in range(2)]
        bml, xol = lanes(s.sem, "bm_loaded"), lanes(s.sem, "xc_o_loaded")
        kwd = lanes(s.flag, "kw_ready", per=2 * N)
        um = lanes(s.flag, "update_made", per=2 * N, credit=1)
        us = lanes(s.flag, "update_added", per=2 * N, credit=1)
        dd = lanes(s.flag, "D_ready", per=NT)
        de = lanes(s.flag, "D_exp_done", per=NT)
        qed = lanes(s.flag, "qe_done", per=NT)
        kqd = lanes(s.flag, "kq_done", per=NT)
        swd = lanes(s.flag, "sw_ready", per=NT, credit=1)
        qsd = lanes(s.flag, "qs_ready", per=NT, credit=1)
        hd = lanes(s.flag, "h_made", per=NT, credit=NT + 1)
        rdd = lanes(s.flag, "den_ready", per=NT)
        hfd = lanes(s.flag, "hf_done", per=NT)
        hsd = lanes(s.flag, "hs_done", per=NT, credit=1)
        sqd = lanes(s.flag, "squares_done", per=NT)
        root = lanes(s.flag, "root_done")
        hscaled = lanes(s.flag, "h_scaled")
        turned = lanes(s.flag, "h_turned", per=2)
        gated = lanes(s.flag, "gated", per=2, credit=1)
        stored = lanes(s.flag, "stored", per=16, credit=16)
        steps = s.sem("dve_steps")
        with nc.Block() as block:
            @block.sync
            def _(sp):
                sp.dma_start(masks[:, :, :], a["masks"]).then_inc(once, 16)
                for r in range(2):
                    sp.dma_start(endb[:, r, :, :, :].rearrange("p h e t -> p (h e t)"),
                                 d["ends"][r].rearrange("h e t -> (h e t)").unsqueeze(0)
                                 .broadcast_to([P, MH * 2 * NT])).then_inc(once, 16)
                sp.wait_ge(ones_set, 1)
                with sp.Fori(0, MH // 4) as i:
                    for b in range(2):
                        j = i * 2 + b
                        for l in LANES:
                            hd[l].wait(sp, j, -NT)
                            sp.dma_start(v1[b][l][:, :, 0:MV], d["v"][j * 2 + l]).then_inc(kvl[b][l], 16)
                            sp.dma_start(kt[b][l][:, :, :], d["kt"][j * 2 + l]).then_inc(kvl[b][l], 16)
                        for l in LANES:
                            sp.dma_start(qk[b][l][:, :, :],
                                         d["qk"][j * 2 + l].rearrange("n p t -> p n t")).then_inc(qkl[b][l], 16)
                        for l in LANES:
                            qsd[l].wait(sp, j, 0)
                            sp.dma_start(bmb[l][:, :, :], d["bm"][:, bass.ds(j * 2 + l, 1), :]
                                         .rearrange("r h t -> h r t").broadcast_to([P, 2, L])).then_inc(bml[l], 16)
                        for l in LANES:
                            stored[l].wait(sp, j, 0)
                            heads = bass.ds((j * 2 + l) * 2, 2)
                            sp.dma_start(xc[l][:, :, :],
                                         d["xc"][heads, :, :].rearrange("b p t -> p b t")).then_inc(xol[l], 16)
                            sp.dma_start(og[l][:, :, :],
                                         d["o"][heads, :, :].rearrange("b p t -> p b t")).then_inc(xol[l], 16)

            @block.tensor
            def _(pe):
                for l in LANES:
                    hd[l].start(pe)
                    um[l].start(pe)
                with pe.Fori(0, MH // 4) as i:
                    for b in range(2):
                        j = i * 2 + b

                        def update(l, n, t):
                            off, m = TILES[t]
                            kwd[l].wait(pe, j, n + 1)
                            us[l].wait(pe, j, n)
                            nc.tensor.matmul(ub[l][:, 0:VW], kw[l][0:m, n % 2, :], v1[b][l][0:m, t, :],
                                             start=True, stop=True).then_inc(um[l].sem, 1)

                        def scores(l, t):
                            off, m = TILES[t]
                            swd[l].wait(pe, j, t)
                            nc.tensor.matmul(kq[l][0:m, 0:m], qk[b][l][:, 1, off:off + m],
                                             qk[b][l][:, 0, off:off + m],
                                             start=True, stop=True).then_inc(kqd[l].sem, 1)

                        for n, t in enumerate(range(N, 0, -1)):
                            for l in LANES:
                                if n == 0:
                                    pe.wait_ge(kvl[b][l], i * 32 + 32)
                                    gated[l].wait(pe, j, 0)
                                update(l, n, t)
                        for l in LANES:
                            pe.wait_ge(qkl[b][l], i * 16 + 16)
                            scores(l, 0)
                        for t, (off, m) in enumerate(TILES):
                            for l in LANES:
                                if t < N:
                                    update(l, N + t, t)
                                    scores(l, t + 1)
                                swd[l].wait(pe, j, t + 1)
                                qsd[l].wait(pe, j, t + 1)
                                hsd[l].wait(pe, j, t)
                                if t:
                                    us[l].wait(pe, j, N + t)
                                for r, bank in enumerate(hbank[l]):
                                    state = cf[l][:, t % 2, :] if r == 0 else cb[l][:, min(t, N - 1), :]
                                    has = t > 0 if r == 0 else t < N
                                    if has:
                                        nc.tensor.matmul(bank[0:m, 0:VW], qs[l][:, r, 0:m], state,
                                                         start=True, stop=False)
                                    last = nc.tensor.matmul(bank[0:m, 0:VW], sw[l][0:m, r, 0:m],
                                                            v1[b][l][0:m, t, :], start=not has, stop=True)
                                last.then_inc(hd[l].sem, 1)
                        for f in range(2):
                            for l in LANES:
                                if f == 0:
                                    hscaled[l].wait(pe, j, 1)
                                else:
                                    gated[l].wait(pe, j, 1)
                                for t, (off, m) in enumerate(TILES):
                                    last = nc.tensor.transpose(turned_at[l][f][:, off:off + m],
                                                               hs[l][0:m, t, f * P:(f + 1) * P],
                                                               c["ident"][0:m, 0:m])
                                last.then_inc(turned[l].sem, 1)

            @block.scalar
            def _(act):
                for l in LANES:
                    stored[l].start(act)
                act.wait_ge(once, 48)
                with act.Fori(0, MH // 4) as i:
                    for b in range(2):
                        j = i * 2 + b

                        def weights_of(l, t):
                            off, m = TILES[t]
                            qsd[l].wait(act, j, t)
                            for r in range(2):
                                last = nc.scalar.activation(
                                    qe[l][:, r, 0:m], bmb[l][:, r, off:off + m], ACT.Exp,
                                    bias=endb[:, r, bass.ds(j * 2 + l, 1), 0, t:t + 1].rearrange("p h t -> p (h t)"))
                            last.then_inc(qed[l].sem, 1)

                        def exp(l, t):
                            m = TILES[t][1]
                            dd[l].wait(act, j, t + 1)
                            nc.scalar.activation(D_[l][0:m, :, 0:m], D_[l][0:m, :, 0:m], ACT.Exp).then_inc(de[l].sem, 1)
                        for l in LANES:
                            act.wait_ge(bml[l], j * 16 + 16)
                            weights_of(l, 0)
                            exp(l, 0)
                        for t in range(NT + 1):
                            for l in LANES:
                                if t:
                                    m = TILES[t - 1][1]
                                    rdd[l].wait(act, j, t)
                                    nc.scalar.activation(hf[l][0:m, :], hbank[l][0][0:m, 0:MV], ACT.Copy,
                                                         scale=rd[l][0:m, 0:1]).then_inc(hfd[l].sem, 1)
                                if t < N:
                                    weights_of(l, t + 1)
                                if t:
                                    hsd[l].wait(act, j, t)
                                    nc.scalar.activation(hf[l][0:m, :], hs[l][0:m, t - 1, :], ACT.Square,
                                                         accum_out=ssq[l][0:m, t - 1:t]).then_inc(sqd[l].sem, 1)
                                if t < N:
                                    exp(l, t + 1)
                        for l in LANES:
                            sqd[l].wait(act, j, NT)
                            nc.scalar.activation(rstd[l][:, :], ssq[l][:, :], ACT.Sqrt, bias=c["eps"][:, :],
                                                 scale=1.0 / MV).then_inc(root[l].sem, 1)
                        for l in LANES:
                            gated[l].wait(act, j, 2)
                            act.dma_start(d["hh"][bass.ds((j * 2 + l) * 2, 2), :, :].rearrange("b p t -> p b t"),
                                          og[l][:, :, :]).then_inc(stored[l].sem, 16)
                for l in LANES:
                    stored[l].wait(act, MH // 2, 0)

            @block.vector
            def _(dve):
                v = nc.vector
                do = Steps(dve, steps)
                for l in LANES:
                    for flag in (us[l], swd[l], qsd[l], hsd[l], gated[l]):
                        flag.start(dve)
                    v.memset(ssq[l][:, :], 0.0)
                    for b in range(2):
                        ins = v.memset(v1[b][l][:, :, MV:VW], 1.0)
                ins.then_inc(ones_set, 1)
                dve.wait_ge(once, 48)
                with do.loop(MH // 4, 2 * 2 * LANE_STEPS) as i:
                    for b in range(2):
                        j = i * 2 + b

                        def col(l, t, q, r, m):
                            return cols[0:m, t, q, bass.ds(j * 2 + (l + 32 * r), 1)]

                        def decay(l, t, r):
                            return endb[:, r, bass.ds(j * 2 + l, 1), 1, t:t + 1].rearrange("p h t -> p (h t)")

                        def weigh(l, n, t, r):
                            m = TILES[t][1]
                            um[l].wait(dve, j, max(n - 1, 0))
                            v.tensor_scalar(kw[l][0:m, n % 2, :], kt[b][l][0:m, t, :], col(l, t, WS, r, m), None,
                                            ALU.mult).then_inc(kwd[l].sem, 1)

                        def exponent(l, t):
                            off, m = TILES[t]
                            for r in range(2):
                                last = v.scalar_tensor_tensor(D_[l][0:m, r, 0:m], bmb[l][0:m, r, off:off + m],
                                                              col(l, t, LS, r, m), masks[0:m, r, 0:m],
                                                              ALU.add, ALU.add)
                            last.then_inc(dd[l].sem, 1)

                        def add(l, n, dst, src, t, r):
                            um[l].wait(dve, j, n + 1)
                            if src is None:
                                do(v.tensor_copy(dst, ub[l][:, 0:VW]))
                            else:
                                do(v.scalar_tensor_tensor(dst, src, decay(l, t, r), ub[l][:, 0:VW],
                                                          ALU.mult, ALU.add))
                            dve.sem_inc(us[l].sem, 1)

                        for l in LANES:
                            dve.wait_ge(kvl[b][l], i * 32 + 32)
                            weigh(l, 0, N, 1)
                        for n, t in enumerate(range(N, 0, -1)):
                            for l in LANES:
                                if n + 1 < N:
                                    weigh(l, n + 1, t - 1, 1)
                                add(l, n, cb[l][:, t - 1, :], None if t == N else cb[l][:, t, :], t, 1)
                        for l in LANES:
                            dve.wait_ge(bml[l], j * 16 + 16)
                            exponent(l, 0)
                            weigh(l, N, 0, 0)
                        for t in range(NT + 1):
                            for l in LANES:
                                if t:
                                    p, mp = t - 1, TILES[t - 1][1]
                                    hd[l].wait(dve, j, t)
                                    for r, bank in enumerate(hbank[l]):
                                        ins = v.tensor_scalar(dn[l][0:mp, r:r + 1], bank[0:mp, MV:VW], -1.0,
                                                              col(l, p, FLOOR, r, mp), ALU.mult, ALU.max)
                                        do(ins) if r else do.free(ins)
                                    for r, bank in enumerate(hbank[l]):
                                        ins = v.tensor_tensor(dn[l][0:mp, r:r + 1], bank[0:mp, MV:VW],
                                                              dn[l][0:mp, r:r + 1], ALU.max)
                                        do(ins) if r else do.free(ins)
                                    do(v.reciprocal(rd[l][0:mp, :], dn[l][0:mp, :]))
                                    dve.sem_inc(rdd[l].sem, 1)
                                if t < NT:
                                    off, m = TILES[t]
                                    de[l].wait(dve, j, t + 1)
                                    kqd[l].wait(dve, j, t + 1)
                                    do(v.tensor_tensor(sw[l][0:m, :, 0:m], D_[l][0:m, :, 0:m],
                                                       kq[l][0:m, 0:m].unsqueeze(1).broadcast_to([m, 2, m]),
                                                       ALU.mult))
                                    dve.sem_inc(swd[l].sem, 1)
                                    qed[l].wait(dve, j, t + 1)
                                    v.tensor_tensor(qs[l][:, :, 0:m], qe[l][:, :, 0:m],
                                                    qk[b][l][:, 0, off:off + m].unsqueeze(1).broadcast_to([P, 2, m]),
                                                    ALU.mult).then_inc(qsd[l].sem, 1)
                                if t < N:
                                    exponent(l, t + 1)
                                if t:
                                    hfd[l].wait(dve, j, t)
                                    v.scalar_tensor_tensor(hs[l][0:mp, p, :], hbank[l][1][0:mp, 0:MV],
                                                           rd[l][0:mp, 1:2], hf[l][0:mp, :],
                                                           ALU.mult, ALU.add).then_inc(hsd[l].sem, 1)
                                if t < N:
                                    if t + 1 < N:
                                        weigh(l, N + t + 1, t + 1, 0)
                                    add(l, N + t, cf[l][:, (t + 1) % 2, :], None if t == 0 else cf[l][:, t % 2, :],
                                        t, 0)
                        for l in LANES:
                            root[l].wait(dve, j, 1)
                            do(v.reciprocal(rstd[l][:, :], rstd[l][:, :]))
                            for t, (off, m) in enumerate(TILES):
                                ins = v.tensor_scalar(hs[l][0:m, t, :], hs[l][0:m, t, :], rstd[l][0:m, t:t + 1],
                                                      None, ALU.mult)
                                do(ins) if t == N else do.free(ins)
                            dve.sem_inc(hscaled[l].sem, 1)
                        for f in range(2):
                            for l in LANES:
                                if f == 0:
                                    dve.wait_ge(xol[l], j * 32 + 32)
                                turned[l].wait(dve, j, f + 1)
                                feature = (j * 2 + l) * 2 + f
                                do(v.scalar_tensor_tensor(og[l][:, f, :], turned_at[l][f],
                                                          c["cols_a"][:, bass.ds(feature + c["head_norm"], 1)],
                                                          og[l][:, f, :], ALU.mult, ALU.mult))
                                v.scalar_tensor_tensor(og[l][:, f, :], xc[l][:, f, :],
                                                       c["cols_a"][:, bass.ds(feature + c["mlstm_skip"], 1)],
                                                       og[l][:, f, :], ALU.mult, ALU.add).then_inc(gated[l].sem, 1)


LANE_STEPS = 2 * (NT - 1) + 6 * NT + 1 + NT + 2


def rope_tables():
    n = L - META
    pos = np.zeros((2, L), np.float32)
    pos[0, META:] = np.repeat(np.arange(n // GRID_W, dtype=np.float32), GRID_W)
    pos[1, META:] = np.tile(np.arange(GRID_W, dtype=np.float32), n // GRID_W)
    axis = HD // 2
    freqs = (np.float32(10000.0) ** (-np.arange(0, axis, 2, dtype=np.float32) / np.float32(axis))).astype(np.float32)
    angle = np.stack([pos[f // axis] * freqs[f % (axis // 2)] for f in range(HD)])
    return np.stack([np.cos(angle), np.sin(angle)], axis=1).astype(np.float32)


def rope_swap():
    swap = np.zeros((HD, HD), np.float32)
    half = HD // 4
    for f in range(HD):
        first = f % (2 * half) < half
        swap[f + half if first else f - half, f] = -1.0 if first else 1.0
    return swap


def before_masks():
    s, t = np.arange(P)[:, None], np.arange(P)[None, :]
    return np.stack([np.where(s <= t, 0.0, -1e30), np.where(s >= t, 0.0, -1e30)], axis=1).astype(np.float32)


def scan_starts():
    keep = np.ones((40, L), np.float32)
    keep[0:32, [o for o, _ in TILES]] = 0.0
    keep[32:40, [L - o - n for o, n in TILES]] = 0.0
    return keep


_INS = ["x", "meta_tokens", "norm_pre", "norm_post", "w_in_even", "q_norm", "k_norm", "ssm_a_re", "ssm_a_im",
        "ssm_log_dt", "ssm_b_re", "ssm_b_im", "ssm_c_re", "ssm_c_im", "ssm_d", "w_glu", "b_glu", "w_out_even",
        "w_in_odd", "conv_w", "conv_b", "w_q", "w_k", "w_v", "w_igate", "b_igate", "w_fgate", "b_fgate",
        "w_ogate", "b_ogate", "head_norm", "mlstm_skip", "w_out_odd"]
_FLAT = ("norm_pre", "norm_post")


def kernel(**inputs):
    import concourse.bacc as bacc
    from concourse.bass_utils import run_bass_kernel_spmd
    nc = bacc.Bacc("TRN2", target_bir_lowering=False, num_devices=1)
    arrays = {}
    for name in _INS:
        v = np.asarray(inputs[name])
        if name in _FLAT:
            v = v.reshape(-1)
        elif name != "meta_tokens":
            v = v[0]
        arrays[name] = np.ascontiguousarray(v)
    arrays["ident"] = np.eye(P, dtype=np.float32)
    arrays["rope"] = rope_tables()
    arrays["swap"] = rope_swap()
    arrays["masks"] = before_masks()
    arrays["starts"] = scan_starts()
    a = {n: nc.dram_tensor(f"in_{n}", v.shape, mybir.dt.from_np(v.dtype), kind="ExternalInput").ap()
         for n, v in arrays.items()}
    out = nc.dram_tensor("out", (L - META, D), F32, kind="ExternalOutput").ap()
    trunk(nc, a, out)
    result = run_bass_kernel_spmd(nc, [{f"in_{n}": v for n, v in arrays.items()}], core_ids=[0])
    return result.results[0]["out"][None]
```

```python
from contextlib import ExitStack, contextmanager
import math

import numpy as np

import concourse.bass as bass
from concourse import mybir

D = 1024
L = 1040
META = 16
P = 128
KC = D // P
HEADS, KV, HD = 8, 2, 128
G, GP, NS = 64, 16, 64
T = P // GP
CH = L // T
GB = 8
W2 = 2048
MH, MV, MK = 8, 256, 128
CONV = 5
GRID_W = 64
EPS = 1e-6
Q0, K0 = 0, HEADS * HD
GA0 = K0 + 2 * KV * HD
U0 = GA0 + HEADS * HD
GB0 = U0 + D
TILES = [(i * P, min(P, L - i * P)) for i in range(-(-L // P))]
NT = len(TILES)
PO = 248
PIECES = [(0, 264), (264, 512), (776, 264)]
QT = [(0, 120), (120, 120), (240, 112), (352, 120), (472, 112), (584, 112),
      (696, 120), (816, 112), (928, 112)]

F32 = mybir.dt.float32
F32R = mybir.dt.float32r
I32 = mybir.dt.int32
ACT = mybir.ActivationFunctionType
ALU = mybir.AluOpType
AX = mybir.AxisListType.X


class Signal:

    def __init__(self, sem, per=1, credit=0):
        self.sem, self.per, self.credit = sem, per, credit

    def start(self, eng):
        eng.sem_inc(self.sem, self.credit)

    def wait(self, eng, i, k):
        eng.wait_ge(self.sem, i * self.per + (k + self.credit))


class Steps:

    def __init__(self, eng, sem):
        self.eng, self.sem, self.n, self.base = eng, sem, 0, 0

    def __call__(self, instruction):
        instruction.then_inc(self.sem, 1)
        self.n += 1
        self.eng.wait_ge(self.sem, self.base + self.n)
        return instruction

    def free(self, instruction):
        instruction.then_inc(self.sem, 1)
        self.n += 1
        return instruction

    @contextmanager
    def loop(self, count, per):
        before = self.n
        with self.eng.Fori(0, count) as i:
            self.n, self.base = 0, i * per + before
            yield i
            assert self.n == per, (self.n, per)
        self.n, self.base = before + count * per, 0


def trunk(nc, a, out):
    outer = ExitStack()
    Stage.finished = []
    with outer:
        top = Stage(nc, outer)
        c = {}

        def dram(name, *shape, dtype=F32):
            return nc.dram_tensor(f"{name}_d", shape, dtype).ap()
        d = dict(
            res=dram("res", P, KC, L), u=dram("u", G, GP, T, CH), y=dram("y", G, GP, T, CH),
            q=dram("q", HEADS, P, L), ga=dram("ga", HEADS, P, L), gb=dram("gb", KC, P, L),
            cat=dram("cat", 2 * KC, P, L), v=dram("v", MH, P, NT, MV), xc=dram("xc", 2 * KC, P, L),
            z=dram("z", 2 * KC, P, L), xz=dram("xz", 2 * KC, P, L), o=dram("o", 2 * KC, P, L), qk=dram("qk", MH, 2, P, L),
            kt=dram("kt", MH, P, NT, MK),
            bm=dram("bm", 2, MH, L), ends=dram("ends", 2, MH, 2, NT), hh=dram("hh", 2 * KC, P, L),
        )
        constants(nc, top, a, c)
        with ExitStack() as even:
            se = Stage(nc, even)
            t = s5_tensors(se)
            kr = se.sb("k_hi", [P, KV, L], F32R), se.sb("k_lo", [P, KV, L], F32R)
            vt = se.sb("v", [P, NT, KV * HD])
            with ExitStack() as with_h:
                sh = Stage(nc, with_h)
                h = [sh.sb(n, [P, KC, L], F32R) for n in ("h_hi", "h_lo")]
                given = s5_given(sh)
                enter(nc, a, c, d, h, given)
                s5_inputs(nc, a, c, d, h, t, given)
                keys_values(nc, a, c, h, kr, vt)
                queries_gates(nc, a, c, d, h)
            t["Z"] = se.sb("Z", [P, CH + 1, 2, G])
            s5_states(nc, c, d, t)
            heads(nc, c, d, kr, vt, t)
            s5_outputs(nc, c, d, t)
        s5_glu(nc, a, c, d)
        with ExitStack() as cell:
            cols = Stage(nc, cell).sb("cols", [P, NT, 3, 64])
            with ExitStack() as with_gates:
                sg = Stage(nc, with_gates)
                gates = gate_memory(sg)
                with ExitStack() as with_h:
                    sh = Stage(nc, with_h)
                    hi = sh.sb("h_hi", [P, KC, L], F32R)
                    y = hi[:, :, :].bitcast(F32)
                    project(nc, a["w_out_even"], d["cat"], c, y)
                    h = [hi, sh.sb("h_lo", [P, KC, L], F32R)]
                    with stage(nc) as s:
                        res = s.sb("res", [P, KC, L])
                        norm_block(nc, c, y, lambda k: c["col"]("norm_post", k), dst=res, resid=d["res"],
                                   save=d["res"])
                        norm_block(nc, c, res, lambda k: c["col"]("norm_pre", KC + k), split=h)
                    conv_values_z(nc, a, c, d, h, gates)
                raw = sg.sb("li", [40, L]), sg.sb("fx", [40, L])
                odd_gates(nc, a, c, d, gates, raw)
                gate_rows(nc, a, c, d, raw, cols)
            mlstm(nc, a, c, d, cols)
        with stage(nc) as s:
            y = s.sb("y", [P, KC, L])
            project(nc, a["w_out_odd"], d["hh"], c, y[:, :, :])
            res = s.sb("res", [P, KC, L])
            norm_block(nc, c, y, lambda k: c["col"]("norm_post", KC + k), dst=res, resid=d["res"])
            leave(nc, c, res, out)


class Stage:

    count = 0
    finished = []

    def __init__(self, nc, stack):
        self.nc, self.stack, self.sems = nc, stack, []

    def sb(self, name, shape, dtype=F32):
        Stage.count += 1
        return self.stack.enter_context(self.nc.sbuf_tensor(f"{name}_{Stage.count}", shape, dtype))

    def ps(self, name, columns):
        Stage.count += 1
        return self.stack.enter_context(self.nc.psum_tensor(f"{name}_{Stage.count}", [P, columns], F32))

    def sem(self, name):
        Stage.count += 1
        self.sems.append(self.nc.alloc_semaphore(f"{name}_{Stage.count}"))
        return self.sems[-1]

    def flag(self, name, per=1, credit=0):
        return Signal(self.sem(name), per, credit)


@contextmanager
def stage(nc):
    with ExitStack() as stack:
        s = Stage(nc, stack)
        yield s
        Stage.finished += s.sems
        if len(Stage.finished) > 50:
            nc.clear_and_free_semaphores(Stage.finished)
            nc.all_engine_barrier()
            Stage.finished = []


def rows_of(region):
    return region[:, PO:PO + L]


COLS_A = [("norm_pre", 16), ("norm_post", 16), ("q_norm", 1), ("k_norm", 1), ("b_glu", 8),
          ("conv_b", 16), ("b_ogate", 16), ("head_norm", 16), ("mlstm_skip", 16)]


def constants(nc, top, a, c):
    c["ident"] = top.sb("ident", [P, P])
    c["ones"] = top.sb("ones", [P, P])
    c["cols_a"] = top.sb("cols_a", [P, 112])
    c["conv_w"] = top.sb("conv_w", [P, CONV * 2 * KC])
    c["eps"] = top.sb("eps", [P, 1])
    with stage(nc) as s:
        ra, rb = s.sb("ra", [P, P]), s.sb("rb", [P, P])
        pt = s.ps("pt", 512)
        loaded, turned = s.sem("params_loaded"), s.sem("turned")
        with nc.Block() as block:
            @block.sync
            def _(sp):
                sp.dma_start(c["ident"][:, :], a["ident"]).then_inc(loaded, 16)
                at = 0
                for name, n in COLS_A:
                    c[name] = at
                    sp.dma_start(ra[at:at + n, :], a[name].rearrange("(r p) -> r p", p=P)).then_inc(loaded, 16)
                    at += n
                sp.dma_start(rb[0:CONV * 16, :], a["conv_w"].rearrange("w (r p) -> (w r) p", p=P)).then_inc(loaded, 16)

            @block.vector
            def _(dve):
                nc.vector.memset(c["ones"][:, :], 1.0)
                nc.vector.memset(c["eps"][:, :], EPS)
                dve.wait_ge(turned, 1)
                nc.vector.tensor_copy(c["cols_a"][:, 0:106], pt[:, 0:106])
                nc.vector.tensor_copy(c["conv_w"][:, :], pt[:, 128:128 + CONV * 16])

            @block.tensor
            def _(pe):
                pe.wait_ge(loaded, 16 * (len(COLS_A) + 2))
                nc.tensor.transpose(pt[:, 0:106], ra[0:106, :], c["ident"][0:106, 0:106])
                nc.tensor.transpose(pt[:, 128:128 + CONV * 16], rb[0:CONV * 16, :],
                                    c["ident"][0:CONV * 16, 0:CONV * 16]).then_inc(turned, 1)
    a_cols = c["cols_a"]
    c["col"] = lambda name, i: a_cols[:, c[name] + i:c[name] + i + 1]


class Weights:

    def __init__(self, nc, s, units, tiles=None):
        assert units % 2 == 0
        self.nc, self.units = nc, units
        self.tiles = tiles or (KC,) * units
        self.raw = s.sb("w_raw", [P, 2, KC, P])
        self.hi, self.lo = s.sb("w_hi", [P, 2, KC, P], F32R), s.sb("w_lo", [P, 2, KC, P], F32R)
        self.loaded = [[s.sem(f"w_loaded{b}{part}") for part in range(2)] for b in range(2)]
        self.split = s.flag("w_split", per=2 * units, credit=4)
        self.used = s.flag("w_used", per=units, credit=2)
        self.steps = s.sem("split_steps")

    def load(self, sp, i, u, source):
        self.split.wait(sp, i, 2 * (u - 1))
        half = self.tiles[u] // 2
        for part in range(2):
            tiles = slice(part * half, (part + 1) * half)
            sp.dma_start(self.raw[:, u % 2, tiles, :], source[:, tiles, :]).then_inc(self.loaded[u % 2][part], 16)

    def split_all(self, gp, turns, ones):
        self.split.start(gp)
        do = Steps(gp, self.steps)
        with do.loop(turns, 2 * self.units) as i:
            for u in range(self.units):
                b, half = u % 2, self.tiles[u] // 2
                for part in range(2):
                    gp.wait_ge(self.loaded[b][part], i * (8 * self.units) + 16 * (u // 2 + 1))
                    if part == 0:
                        self.used.wait(gp, i, u - 1)
                    tiles = slice(part * half, (part + 1) * half)
                    hi, lo, raw = self.hi[:, b, tiles], self.lo[:, b, tiles], self.raw[:, b, tiles]
                    one = ones[:, 0:1].unsqueeze(2).broadcast_to([P, half, P])
                    do(self.nc.gpsimd.tensor_tensor(hi, raw, one, ALU.mult))
                    self.nc.gpsimd.tensor_tensor(lo, raw, hi.bitcast(F32), ALU.subtract).then_inc(self.split.sem, 1)

    def product(self, pe, i, u, region, x, first=True, last=True, between=None):
        b, kc = u % 2, self.tiles[u]
        for k in range(kc):
            if k % (kc // 2) == 0:
                self.split.wait(pe, i, 2 * u + 1 + k // (kc // 2))
            hi, lo = x(k)
            for w, z in ((self.hi, lo), (self.hi, hi), (self.lo, hi)):
                for off, n in PIECES:
                    ins = self.nc.tensor.matmul(region[:, PO + off:PO + off + n], w[:, b, k, :], z[:, off:off + n],
                                                start=(first and k == 0 and w is self.hi and z is lo),
                                                stop=(last and k == kc - 1 and w is self.lo))
            if between is not None and k < kc - 1:
                between(k)
        ins.then_inc(self.used.sem, 1)
        return ins


def pair(x):
    return lambda k: (x[0][:, k, :], x[1][:, k, :])


def norm_block(nc, c, src, gain, dst=None, split=None, resid=None, save=None):
    with stage(nc) as s:
        sq = s.sb("sq", [P, 2, L])
        rstd = s.sb("rstd", [P, L])
        rt = s.sb("resid", [P, KC, L]) if resid is not None else None
        tmp = s.sb("tmp", [P, 4 if split is not None else 2, L])
        region = s.ps("sumsq", 1536)
        squared = s.flag("squared")
        used = s.flag("squares_used", credit=2)
        root = s.sem("root_done")
        loaded = s.sem("resid_loaded")
        scaled, saved, leading = s.sem("scaled"), s.sem("saved"), s.sem("hi_done")
        steps = s.sem("dve_steps")
        rest = s.sem("lo_done")
        with nc.Block() as block:
            @block.gpsimd
            def _(gp):
                if split is not None:
                    for k in range(1, KC, 2):
                        gp.wait_ge(leading, k + 1)
                        nc.gpsimd.tensor_tensor(split[1][:, k, :], tmp[:, k % 4, :],
                                                split[0][:, k, :].bitcast(F32), ALU.subtract).then_inc(rest, 1)

            @block.sync
            def _(sp):
                if resid is not None:
                    sp.dma_start(rt[:, :, :], resid).then_inc(loaded, 16)
                if save is not None:
                    for k in range(KC):
                        sp.wait_ge(scaled, k + 1)
                        sp.dma_start(save[:, k, :], dst[:, k, :]).then_inc(saved, 16)
                    sp.wait_ge(saved, 16 * KC)

            @block.scalar
            def _(act):
                for k in range(KC):
                    used.wait(act, 0, k - 1)
                    nc.scalar.activation(sq[:, k % 2, :], src[:, k, :], ACT.Square).then_inc(squared.sem, 1)
                used.wait(act, 0, KC)
                nc.scalar.activation(rstd[:, :], rows_of(region), ACT.Sqrt, bias=c["eps"][:, :],
                                     scale=1.0 / D).then_inc(root, 1)
                if split is not None:
                    for k in range(KC):
                        act.wait_ge(scaled, k + 1)
                        nc.scalar.activation(split[0][:, k, :], tmp[:, k % 4, :], ACT.Copy).then_inc(leading, 1)

            @block.tensor
            def _(pe):
                used.start(pe)
                for k in range(KC):
                    squared.wait(pe, 0, k + 1)
                    for off, n in PIECES:
                        last = nc.tensor.matmul(region[:, PO + off:PO + off + n], c["ones"][:, :],
                                                sq[:, k % 2, off:off + n], start=(k == 0), stop=(k == KC - 1))
                    last.then_inc(used.sem, 1)

            @block.vector
            def _(dve):
                do = Steps(dve, steps)
                dve.wait_ge(root, 1)
                do(nc.vector.reciprocal(rstd[:, :], rstd[:, :]))
                if resid is not None:
                    dve.wait_ge(loaded, 16)
                for k in range(KC + 1):
                    if k < KC and split is not None:
                        if k >= 4:
                            dve.wait_ge(leading, k - 3)
                            if k % 2:
                                dve.wait_ge(rest, k // 2 - 1)
                        nc.vector.scalar_tensor_tensor(tmp[:, k % 4, :], src[:, k, :], gain(k), rstd[:, :],
                                                       ALU.mult, ALU.mult).then_inc(scaled, 1)
                    if k % 2 and split is not None:
                        dve.wait_ge(leading, k)
                        do(nc.vector.tensor_tensor(split[1][:, k - 1, :], tmp[:, (k - 1) % 4, :],
                                                   split[0][:, k - 1, :].bitcast(F32), ALU.subtract))
                    if k < KC and split is None:
                        do(nc.vector.scalar_tensor_tensor(tmp[:, k % 2, :], src[:, k, :], gain(k), rstd[:, :],
                                                          ALU.mult, ALU.mult))
                        nc.vector.tensor_tensor(dst[:, k, :], tmp[:, k % 2, :], rt[:, k, :],
                                                ALU.add).then_inc(scaled, 1)


def enter(nc, a, c, d, h, given):
    with stage(nc) as s0:
        res = s0.sb("res", [P, KC, L])
        with stage(nc) as s:
            xt = s.sb("xt", [P, 2, D])
            mt = s.sb("mt", [META, D])
            pt = [s.ps(f"pt{i}", 512) for i in range(4)]
            xl = [s.sem("x_loaded0"), s.sem("x_loaded1")]
            ml = s.sem("meta_loaded")
            turned = s.flag("turned", per=4, credit=4)
            evac = s.flag("evac", per=4, credit=4)
            meta_turned = s.sem("meta_turned")
            saved = s.sem("saved")
            x_tiles = a["x"].rearrange("(i p) f -> i p f", p=P)
            with nc.Block() as block:
                @block.sync
                def _(sp):
                    sp.dma_start(mt[:, :], a["meta_tokens"]).then_inc(ml, 16)
                    with sp.Fori(0, 4) as i:
                        for b in range(2):
                            turned.wait(sp, i, 2 * b - 2)
                            sp.dma_start(xt[:, b, :], x_tiles[i * 2 + b]).then_inc(xl[b], 16)

                @block.scalar
                def _(act):
                    load_given(act, a, given)

                @block.tensor
                def _(pe):
                    turned.start(pe)
                    with pe.Fori(0, 4) as i:
                        for b in range(2):
                            pe.wait_ge(xl[b], i * 16 + 16)
                            for half in range(2):
                                evac.wait(pe, i, 2 * b + half - 3)
                                for k in range(4):
                                    last = nc.tensor.transpose(pt[2 * b + half][:, k * P:(k + 1) * P],
                                                               xt[:, b, (4 * half + k) * P:(4 * half + k + 1) * P],
                                                               c["ident"][:, :])
                                last.then_inc(turned.sem, 1)
                    pe.wait_ge(ml, 16)
                    evac.wait(pe, 3, 4)
                    for k in range(KC):
                        last = nc.tensor.transpose(pt[0][:, k * META:(k + 1) * META], mt[:, k * P:(k + 1) * P],
                                                   c["ident"][0:META, 0:META])
                    last.then_inc(meta_turned, 1)

                @block.vector
                def _(dve):
                    evac.start(dve)
                    with dve.Fori(0, 4) as i:
                        for b in range(2):
                            for half in range(2):
                                turned.wait(dve, i, 2 * b + half + 1)
                                nc.vector.tensor_copy(
                                    res[:, 4 * half:4 * half + 4, bass.ds(i * 256 + (b * P + META), P)],
                                    pt[2 * b + half][:, :].rearrange("p (k t) -> p k t", k=4)).then_inc(evac.sem, 1)
                    dve.wait_ge(meta_turned, 1)
                    nc.vector.tensor_copy(res[:, :, 0:META], pt[0][:, 0:P].rearrange("p (k t) -> p k t", k=KC))
        with stage(nc) as s:
            saved = s.sem("saved")
            with nc.Block() as block:
                @block.sync
                def _(sp):
                    sp.dma_start(d["res"], res[:, :, :]).then_inc(saved, 16)
                    sp.wait_ge(saved, 16)
        norm_block(nc, c, res, lambda k: c["col"]("norm_pre", k), split=h)


def s5_tensors(s):
    t = {}
    t["B"] = s.sb("B", [P, 2, G, GP])
    t["C"] = s.sb("C", [P, 3, G, GP])
    t["pw_in"] = s.sb("pw_in", [P, T, 2, G])
    t["pw_out"] = s.sb("pw_out", [P, T, 2, G])
    t["step_re"] = s.sb("step_re", [P, 2, G])
    t["step_im"] = s.sb("step_im", [P, 2, G])
    t["skip"] = s.sb("skip", [P, G])
    return t


ROUND = 1.5 * 2.0 ** 23
LN2_HI, LN2_LO = 0.693359375, -2.12194440e-4
PI2_A, PI2_B = 6.28125, 0.0019350051879882812
PI2_C = 2 * math.pi - PI2_A - PI2_B


GIVEN_LOADS = 16 * (6 + T)


def s5_given(s):
    return dict(a=s.sb("a_in", [G, 2, P]), d=s.sb("d_rows", [G, T, GP]), log_dt=s.sb("log_dt", [P, G]),
                b=s.sb("b_in", [P, 2, G, GP]), c=s.sb("c_in", [P, 2, KC, P]), loaded=s.sem("given_loaded"),
                b_loaded=s.sem("b_loaded"), c_loaded=s.sem("c_loaded"))


def load_given(eng, a, given):
    loaded = given["loaded"]
    for r in range(2):
        rows = slice(r * NS, (r + 1) * NS)
        for q, part in enumerate(("re", "im")):
            eng.dma_start(given["a"][:, q, rows], a["ssm_a_" + part][r]).then_inc(loaded, 16)
        eng.dma_start(given["log_dt"][rows, :],
                      a["ssm_log_dt"][r:r + 1, :].broadcast_to([NS, G])).then_inc(loaded, 16)
    for j in range(T):
        eng.dma_start(given["d"][:, j, :], a["ssm_d"].rearrange("(g p) -> g p", p=GP)).then_inc(loaded, 16)
    for r in range(2):
        rows = slice(r * NS, (r + 1) * NS)
        for q, part in enumerate(("re", "im")):
            eng.dma_start(given["b"][rows, q, :, :],
                          a["ssm_b_" + part][r].rearrange("g n p -> n g p")).then_inc(given["b_loaded"], 16)
            eng.dma_start(given["c"][:, q, :, rows],
                          a["ssm_c_" + part][r].rearrange("(k g) q n -> (g q) k n", k=KC)).then_inc(given["c_loaded"], 16)


def s5_inputs(nc, a, c, d, h, t, given):
    with stage(nc) as s:
        weights = Weights(nc, s, 2)
        st = s.sb("staged", [P, 2, T, CH])
        a0 = s.sb("a", [P, 2, G])
        raw, dr, logdt, b_in, c_in = (given[n] for n in ("a", "d", "log_dt", "b", "c"))
        params, bl, cl = (given[n] for n in ("loaded", "b_loaded", "c_loaded"))
        x = s.sb("x", [P, 24, G])
        xi = s.sb("xi", [P, G], I32)
        pw = s.sb("pw", [P, T + 1, 2, G])
        pt = s.sb("pt", [P, 2, 4, G])
        bt = s.sb("bt", [P, 2, G, GP])
        reg = [s.ps(f"u{b}", 1536) for b in range(2)]
        pa, pc = s.ps("pa", 512), s.ps("pc", 512)
        mm = weights.used
        evac = s.flag("u_copied", per=2, credit=2)
        st_sem = [s.flag(f"u_stored{b}", per=16, credit=16) for b in range(2)]
        at, ac, acc = s.sem("a_turned"), s.sem("c_turned"), s.sem("c_copied")
        steps = s.sem("dve_steps")
        asked, answered = s.sem("function_asked"), s.sem("function_done")
        wv = a["w_in_even"].rearrange("(k p) n -> p k n", p=P)
        uv = d["u"].rearrange("(j g) p s c -> j (g p) (s c)", j=KC)
        with nc.Block() as block:
            @block.sync
            def _(sp):
                with sp.Fori(0, KC // 2) as i:
                    for b in range(2):
                        weights.load(sp, i, b, wv[:, :, bass.ds(i * 256 + (U0 + b * P), P)])

            @block.gpsimd
            def _(gp):
                weights.split_all(gp, KC // 2, c["ones"])

            @block.tensor
            def _(pe):
                weights.used.start(pe)
                pe.wait_ge(params, GIVEN_LOADS)
                for q in range(2):
                    nc.tensor.transpose(pa[:, q * G:(q + 1) * G], raw[:, q, :], c["ident"][0:G, 0:G])
                last = nc.tensor.transpose(pa[:, 2 * G:3 * G], dr[:, :, :].rearrange("g s p -> g (s p)"),
                                           c["ident"][0:G, 0:G])
                last.then_inc(at, 1)
                with pe.Fori(0, KC // 2) as i:
                    for b in range(2):
                        evac.wait(pe, i, b - 1)
                        weights.product(pe, i, b, reg[b], pair(h))
                pe.wait_ge(cl, 16 * 4)
                for q in range(2):
                    for k in range(0, KC, 4):
                        if q or k:
                            pe.wait_ge(acc, 2 * q + k // 4)
                        for kk in range(4):
                            last = nc.tensor.transpose(pc[:, kk * P:(kk + 1) * P], c_in[:, q, k + kk, :],
                                                       c["ident"][:, :])
                        last.then_inc(ac, 1)

            calls = [(ACT.Tanh, 3, 4, 0.5), (ACT.Sin, 8, 9, 1.0), (ACT.Sin, 8, 10, 0.5), (ACT.Tanh, 6, 11, 0.5)]

            @block.scalar
            def _(act):
                evac.start(act)
                for b in range(2):
                    st_sem[b].start(act)
                for n, (f, src, dst, scale) in enumerate(calls):
                    act.wait_ge(asked, 1 if n == 0 else 2)
                    nc.scalar.activation(x[:, dst, :], x[:, src, :], f, scale=scale).then_inc(answered, 1)
                with act.Fori(0, KC // 2) as i:
                    for b in range(2):
                        mm.wait(act, i, b + 1)
                        st_sem[b].wait(act, i, 0)
                        nc.scalar.activation(st[:, b, :, :].rearrange("p s c -> p c s"),
                                             rows_of(reg[b]).rearrange("p (c s) -> p c s", s=T),
                                             ACT.Copy).then_inc(evac.sem, 1)
                        evac.wait(act, i, b + 1)
                        act.dma_start(uv[i * 2 + b], st[:, b, :, :]).then_inc(st_sem[b].sem, 16)
                for b in range(2):
                    st_sem[b].wait(act, KC // 2, 0)

            @block.vector
            def _(dve):
                v = nc.vector
                do = Steps(dve, steps)

                def two(o, i0, s1, op0, s2=None, op1=None):
                    do(v.tensor_scalar(o, i0, s1, s2, op0, op1) if op1 is not None else
                       v.tensor_scalar(o, i0, s1, None, op0))

                def tt(o, i0, i1, op):
                    do(v.tensor_tensor(o, i0, i1, op))

                def X(n):
                    return x[:, n, :]

                dve.wait_ge(params, GIVEN_LOADS)
                two(X(0), logdt[:, :], -87.0, ALU.max)
                two(X(1), X(0), 1 / math.log(2), ALU.mult)
                two(X(1), X(1), ROUND, ALU.add)
                two(X(1), X(1), ROUND, ALU.subtract)
                do(v.scalar_tensor_tensor(X(2), X(1), -LN2_HI, X(0), ALU.mult, ALU.add))
                do(v.scalar_tensor_tensor(X(3), X(1), -LN2_LO, X(2), ALU.mult, ALU.add))
                two(xi[:, :], X(1), 127.0, ALU.add)
                do(v.tensor_single_scalar(xi[:, :], xi[:, :], 23, ALU.logical_shift_left))
                dve.sem_inc(asked, 1)
                dve.wait_ge(answered, 1)
                two(X(5), X(4), -1.0, ALU.mult, 1.0, ALU.add)
                do(v.reciprocal(X(5), X(5)))
                do(v.scalar_tensor_tensor(X(4), X(4), 1.0, X(5), ALU.add, ALU.mult))
                tt(X(12), X(4), xi[:, :].bitcast(F32), ALU.mult)
                dve.wait_ge(at, 1)
                do(v.tensor_copy(a0[:, :, :], pa[:, 0:2 * G].rearrange("p (q g) -> p q g", q=2)))
                do(v.tensor_copy(t["skip"][:, :], pa[:, 2 * G:3 * G]))
                tt(X(6), a0[:, 0, :], X(12), ALU.mult)
                tt(X(7), a0[:, 1, :], X(12), ALU.mult)
                two(X(13), X(7), 1 / (2 * math.pi), ALU.mult)
                two(X(13), X(13), ROUND, ALU.add)
                two(X(13), X(13), ROUND, ALU.subtract)
                for part in (PI2_A, PI2_B, PI2_C):
                    do(v.scalar_tensor_tensor(X(7), X(13), -part, X(7), ALU.mult, ALU.add))
                two(X(8), X(7), 3.1415925, ALU.min, -3.1415925, ALU.max)
                dve.sem_inc(asked, 1)
                dve.wait_ge(answered, 4)
                two(X(14), X(11), -1.0, ALU.mult, 1.0, ALU.add)
                do(v.reciprocal(X(14), X(14)))
                do(v.scalar_tensor_tensor(X(14), X(11), 2.0, X(14), ALU.mult, ALU.mult))
                do(v.scalar_tensor_tensor(X(15), X(10), -2.0, X(10), ALU.mult, ALU.mult))
                do(v.scalar_tensor_tensor(X(16), X(15), 1.0, X(14), ALU.add, ALU.mult))
                tt(X(16), X(16), X(15), ALU.add)
                do(v.scalar_tensor_tensor(X(17), X(14), 1.0, X(9), ALU.add, ALU.mult))
                tt(X(18), a0[:, 0, :], a0[:, 0, :], ALU.mult)
                tt(X(19), a0[:, 1, :], a0[:, 1, :], ALU.mult)
                tt(X(18), X(18), X(19), ALU.add)
                do(v.reciprocal(X(18), X(18)))
                tt(X(19), X(16), a0[:, 0, :], ALU.mult)
                tt(X(20), X(17), a0[:, 1, :], ALU.mult)
                tt(X(19), X(19), X(20), ALU.add)
                tt(X(21), X(19), X(18), ALU.mult)
                tt(X(19), X(17), a0[:, 0, :], ALU.mult)
                tt(X(20), X(16), a0[:, 1, :], ALU.mult)
                tt(X(19), X(19), X(20), ALU.subtract)
                tt(X(22), X(19), X(18), ALU.mult)
                do(v.memset(pw[:, 0, 0, :], 1.0))
                do(v.memset(pw[:, 0, 1, :], 0.0))
                two(pw[:, 1, 0, :], X(16), 1.0, ALU.add)
                do(v.tensor_copy(pw[:, 1, 1, :], X(17)))
                n = 1
                while n < T:
                    lo = pw[:, 1:n + 1, :, :]

                    def last(q, n=n):
                        return pw[:, n:n + 1, q, :].broadcast_to([P, n, G])
                    tt(pt[:, 0, 0:n, :], lo[:, :, 0, :], last(0), ALU.mult)
                    tt(pt[:, 1, 0:n, :], lo[:, :, 1, :], last(1), ALU.mult)
                    tt(pw[:, n + 1:2 * n + 1, 0, :], pt[:, 0, 0:n, :], pt[:, 1, 0:n, :], ALU.subtract)
                    tt(pt[:, 0, 0:n, :], lo[:, :, 0, :], last(1), ALU.mult)
                    tt(pt[:, 1, 0:n, :], lo[:, :, 1, :], last(0), ALU.mult)
                    tt(pw[:, n + 1:2 * n + 1, 1, :], pt[:, 0, 0:n, :], pt[:, 1, 0:n, :], ALU.add)
                    n *= 2
                f, r = slice(0, NS), slice(NS, P)
                for e in range(T):
                    do.free(v.tensor_copy(t["pw_in"][f, e, :, :], pw[f, T - 1 - e, :, :]))
                    do.free(v.tensor_copy(t["pw_in"][r, e, :, :], pw[r, e, :, :]))
                    do.free(v.tensor_copy(t["pw_out"][f, e, :, :], pw[f, e + 1, :, :]))
                    do.free(v.tensor_copy(t["pw_out"][r, e, :, :], pw[r, T - e, :, :]))
                do.free(v.tensor_copy(t["step_re"][:, 0, :], pw[:, T, 0, :]))
                do.free(v.tensor_copy(t["step_re"][:, 1, :], pw[:, T, 0, :]))
                two(t["step_im"][:, 1, :], pw[:, T, 1, :], -1.0, ALU.mult)
                do.free(v.tensor_copy(t["step_im"][:, 0, :], pw[:, T, 1, :]))
                dve.wait_ge(bl, 16 * 4)
                g = [X(21 + q).unsqueeze(2).broadcast_to([P, G, GP]) for q in range(2)]
                tt(bt[:, 0], b_in[:, 0], g[0], ALU.mult)
                tt(bt[:, 1], b_in[:, 1], g[1], ALU.mult)
                tt(t["B"][:, 0], bt[:, 0], bt[:, 1], ALU.subtract)
                tt(bt[:, 0], b_in[:, 0], g[1], ALU.mult)
                tt(bt[:, 1], b_in[:, 1], g[0], ALU.mult)
                tt(t["B"][:, 1], bt[:, 0], bt[:, 1], ALU.add)
                for q in range(2):
                    for k in range(2):
                        dve.wait_ge(ac, 2 * q + k + 1)
                        v.tensor_copy(t["C"][:, q, 32 * k:32 * k + 32, :],
                                      pc[:, :].rearrange("p (g q) -> p g q", q=GP)).then_inc(acc, 1)
                dve.wait_ge(acc, 4)
                do(v.tensor_scalar(t["C"][:, 2], t["C"][:, 1], -1.0, None, ALU.mult))


def complex_table(nc, do, out, tmp, pw, x, sign, groups=GB):
    v, tt = nc.vector, nc.vector.tensor_tensor

    def p(q):
        return pw[:, q].rearrange("p s g -> p g s").unsqueeze(3).broadcast_to([P, groups, T, GP])

    def y(q):
        return x[:, q].unsqueeze(2).broadcast_to([P, groups, T, GP])
    do.free(tt(tmp[:, 0], p(0), y(0), ALU.mult))
    do(tt(tmp[:, 1], p(1), y(1), ALU.mult))
    do(tt(out[:, 0], tmp[:, 0], tmp[:, 1], ALU.subtract))
    do.free(tt(tmp[:, 0], p(0), y(1), ALU.mult))
    do(tt(tmp[:, 1], p(1), y(0), ALU.mult))
    if sign > 0:
        return tt(out[:, 1], tmp[:, 0], tmp[:, 1], ALU.add)
    flat = [z.rearrange("p g s q -> p (g s q)") for z in (out[:, 1], tmp[:, 0], tmp[:, 1])]
    return v.scalar_tensor_tensor(flat[0], flat[1], -1.0, flat[2], ALU.mult, ALU.subtract)


def s5_states(nc, c, d, t):
    with stage(nc) as s:
        us = s.sb("us", [P, G, CH])
        table = s.sb("tab", [P, 2, 2, GB, T, GP])
        tmp = s.sb("tmp", [P, 2, GB, T, GP])
        wl = s.sb("w_in", [P, GB, 2, P])
        tp = [s.ps(f"tp{b}", 512) for b in range(2)]
        zp = [s.ps(f"zp{b}", 512) for b in range(4)]
        loaded = s.sem("u_loaded")
        built = s.flag("table_built")
        turned = s.flag("turned", per=4, credit=8)
        copied = s.flag("weights_copied", per=4, credit=4)
        summed = s.flag("summed", per=GB, credit=GB)
        stored = s.flag("stored", per=GB, credit=GB)
        steps = s.sem("dve_steps")
        uv = d["u"].rearrange("g p s c -> s p g c")
        with nc.Block() as block:
            @block.sync
            def _(sp):
                for j in range(T):
                    sp.dma_start(us[j * GP:(j + 1) * GP, :, :], uv[j]).then_inc(loaded, 16)

            @block.vector
            def _(dve):
                do = Steps(dve, steps)
                do.free(nc.vector.memset(t["Z"][:, 0, :, :], 0.0))
                with do.loop(G // GB // 2, 12) as i:
                    for b in range(2):
                        n = i * 2 + b
                        turned.wait(dve, n, -4)
                        g = bass.ds(n * GB, GB)
                        do(complex_table(nc, do, table[:, b], tmp,
                                         t["pw_in"][:, :, :, g].rearrange("p s q g -> p q s g"),
                                         t["B"][:, :, g, :], 1))
                        dve.sem_inc(built.sem, 1)

            @block.tensor
            def _(pe):
                turned.start(pe)
                summed.start(pe)
                pe.wait_ge(loaded, 16 * T)
                with pe.Fori(0, G // GB // 2) as i:
                    for b in range(2):
                        nb = i * 2 + b
                        built.wait(pe, nb, 1)
                        for m in range(4):
                            copied.wait(pe, nb, m - 1)
                            for n in range(4):
                                g, q = 2 * m + n // 2, n % 2
                                last = nc.tensor.transpose(tp[m % 2][:, n * P:(n + 1) * P],
                                                           table[:, b, q, g].rearrange("p s q -> p (s q)"), c["ident"][:, :])
                            last.then_inc(turned.sem, 1)
                        for g in range(GB):
                            if g % 2 == 0:
                                copied.wait(pe, nb, g // 2 + 1)
                            stored.wait(pe, nb, g - 3)
                            for q in range(2):
                                last = nc.tensor.matmul(zp[g % 4][:, q * CH:(q + 1) * CH], wl[:, g, q, :],
                                                        us[:, bass.ds(nb * GB + g, 1), :].rearrange("p g c -> p (g c)"),
                                                        start=True, stop=True)
                            last.then_inc(summed.sem, 1)

            @block.scalar
            def _(act):
                copied.start(act)
                stored.start(act)
                with act.Fori(0, G // GB // 2) as i:
                    for b in range(2):
                        nb = i * 2 + b
                        for m in range(4):
                            turned.wait(act, nb, m + 1)
                            summed.wait(act, nb, 2 * m + 2 - GB)
                            nc.scalar.activation(wl[:, 2 * m:2 * m + 2, :, :].rearrange("p g q m -> p (g q m)"),
                                                 tp[m % 2][:, :], ACT.Copy).then_inc(copied.sem, 1)
                        for g in range(GB):
                            summed.wait(act, nb, g + 1)
                            gg = bass.ds(nb * GB + g, 1)
                            f, r = slice(0, NS), slice(NS, P)
                            src = zp[g % 4][:, 0:2 * CH].rearrange("p (q c) -> p q c", q=2)
                            nc.scalar.activation(
                                t["Z"][f, 1:CH + 1, :, gg].rearrange("p c q g -> p q (c g)"), src[f], ACT.Copy)
                            nc.scalar.activation(
                                t["Z"][r, 1:CH + 1, :, gg].rearrange("p c q g -> p q (c g)"),
                                src[r, :, ::-1], ACT.Copy).then_inc(stored.sem, 1)


def s5_scan(nc, gp, t, tmp, steps, turns):
    do = Steps(gp, steps)
    tt = nc.gpsimd.tensor_tensor
    with do.loop(CH // 2, 8) as i:
        for b in range(2):
            now = t["Z"][:, bass.ds(i * 2 + b, 1), :, :].rearrange("p k q g -> p (k q) g")
            nxt = t["Z"][:, bass.ds(i * 2 + (b + 1), 1), :, :].rearrange("p k q g -> p (k q) g")
            gp.sem_inc(turns, 1)
            do.free(tt(tmp[:, 0], now, t["step_re"][:, :, :], ALU.mult))
            do(tt(tmp[:, 1], now, t["step_im"][:, :, :], ALU.mult))
            do(tt(tmp[:, 0], tmp[:, 0], tmp[:, 1, ::-1, :], ALU.add))
            gp.sem_inc(turns, 1)
            do(tt(nxt, nxt, tmp[:, 0], ALU.add))


TABLE_STEPS = 4 + 2 * 6


def s5_outputs(nc, c, d, t):
    BACK = (T - 1) * GP
    K = 2 * BACK + GP
    HALF = GB // 2
    with stage(nc) as s:
        us = s.sb("us", [P, 2, GB, CH])
        bb = s.sb("bb", [P, 2, GB, GP])
        apart = s.sb("b_apart", [P, 2, GB, 32 + GP])
        cb = s.sb("cb", [P, 3, GB, GP])
        table = s.sb("tab", [P, 2, 2, GB, T, GP])
        tmp = s.sb("tmp", [P, 2, GB // 2, T, GP])
        kt = s.sb("kt", [GP, GB, K])
        toe = s.sb("toe", [P, 2, GB, P])
        rhs = s.sb("rhs", [P, 2, GB, 2, CH])
        ys = s.sb("ys", [P, GB, CH])
        ends = [s.ps(f"lags{b}", 512) for b in range(2)]
        zero = [s.ps(f"lag_zero{b}", 512) for b in range(2)]
        yp = [s.ps(f"yp{b}", 512) for b in range(3)]
        u_loaded = [s.flag(f"u_loaded{b}", per=8 * T) for b in range(2)]
        built = s.flag("table_built", per=2)
        gathered = s.flag("states_gathered", per=2)
        lag = s.flag("lags_done", per=2, credit=2)
        lagc = s.flag("lags_copied", per=2, credit=2)
        windowed = s.flag("windows_loaded", per=16 * T, credit=16)
        toe_ready = s.flag("toeplitz_ready", per=1)
        done = s.flag("outputs_done", per=GB, credit=2 * GB)
        ycop = s.flag("outputs_copied", per=GB, credit=GB)
        ysto = s.flag("outputs_stored", per=16 * T, credit=16)
        steps = s.sem("dve_steps")
        uv = d["u"].rearrange("g p s c -> s p g c")
        yv = d["y"].rearrange("g p s c -> s p g c")
        NB = G // GB

        def blocks(eng, body, do=None, counted=0):
            with (do.loop(NB // 2 - 1, 2 * counted) if do else eng.Fori(0, NB // 2 - 1)) as i:
                for b in range(2):
                    body(i * 2 + b, b, True)
            for b in range(2):
                body(NB - 2 + b, b, b == 0)
        with nc.Block() as block:
            @block.sync
            def _(sp):
                def load_u(n, b):
                    done.wait(sp, n, -GB)
                    for j in range(T):
                        sp.dma_start(us[j * GP:(j + 1) * GP, b, :, :],
                                     uv[j][:, bass.ds(n * GB, GB), :]).then_inc(u_loaded[b].sem, 16)

                def load(n, b, more):
                    lagc.wait(sp, n, 2)
                    for j in range(T):
                        off = (T - 1 - j) * GP
                        sp.dma_start(toe[j * GP:(j + 1) * GP, b, :, :],
                                     kt[:, :, off:off + P]).then_inc(windowed.sem, 16)
                    if more:
                        load_u(n + 1, 1 - b)
                load_u(0, 0)
                blocks(sp, load)

            @block.vector
            def _(dve):
                v = nc.vector
                do = Steps(dve, steps)
                lagc.start(dve)
                windowed.start(dve)

                f, r = slice(0, NS), slice(NS, P)
                do(v.memset(apart[:, :, :, :], 0.0))

                def tables(n, b):
                    g = bass.ds(n * GB, GB)
                    lag.wait(dve, n, 0)
                    do.free(v.tensor_copy(bb[:, :, :, :], t["B"][:, :, g, :]))
                    do.free(v.tensor_copy(apart[f, :, :, 0:GP], t["B"][f, :, g, :]))
                    do.free(v.tensor_copy(apart[r, :, :, 32:32 + GP], t["B"][r, :, g, :]))
                    do.free(v.tensor_copy(cb[:, :, :, :], t["C"][:, :, g, :]))
                    for m in range(2):
                        done.wait(dve, n, -2 * GB + HALF * (m + 1))
                        half = bass.ds(n * GB + m * HALF, HALF)
                        do(complex_table(nc, do, table[:, b, :, m * HALF:(m + 1) * HALF], tmp,
                                         t["pw_out"][:, :, :, half].rearrange("p s q g -> p q s g"),
                                         t["C"][:, :, half, :], -1, HALF))
                        dve.sem_inc(built.sem, 1)

                def lags(n, b):
                    for m in range(2):
                        lag.wait(dve, n, m + 1)
                        if m == 0:
                            windowed.wait(dve, n, 0)
                        dst = kt[:, m * HALF:(m + 1) * HALF, :]
                        src = ends[m][:, 0:HALF * P].rearrange("p (g k) -> p g k", g=HALF)
                        v.tensor_copy(dst[:, :, 0:BACK], src[32:32 + GP, :, GP:P])
                        v.tensor_copy(dst[:, :, BACK:BACK + GP],
                                      zero[m][0:GP, 0:HALF * GP].rearrange("p (g k) -> p g k", g=HALF))
                        v.tensor_copy(dst[:, :, BACK + GP:K], src[0:GP, :, 0:BACK]).then_inc(lagc.sem, 1)

                def turn(n, b, more):
                    windowed.wait(dve, n, 16 * T)
                    for m in range(GB):
                        ins = v.scalar_tensor_tensor(toe[:, b, m, :], c["ident"][:, :],
                                                     t["skip"][:, bass.ds(n * GB + m, 1)],
                                                     toe[:, b, m, :], ALU.mult, ALU.add)
                        do(ins) if m == GB - 1 else do.free(ins)
                    dve.sem_inc(toe_ready.sem, 1)
                    if more:
                        tables(n + 1, 1 - b)
                        lags(n + 1, 1 - b)
                tables(0, 0)
                lags(0, 0)
                blocks(dve, turn, do, TABLE_STEPS + GB)

            @block.tensor
            def _(pe):
                lag.start(pe)
                done.start(pe)
                flat = "p t q -> p (t q)"

                def lags(n, b):
                    for m in range(GB):
                        h, at = m // HALF, m % HALF
                        if at == 0:
                            built.wait(pe, n, h + 1)
                            lagc.wait(pe, n, h - 1)
                        for q in range(2):
                            nc.tensor.matmul(zero[h][0:GP, at * GP:(at + 1) * GP], bb[:, q, m, :],
                                             cb[:, 2 * q, m, :], start=(q == 0), stop=(q == 1))
                        for q in range(2):
                            last = nc.tensor.matmul(ends[h][0:32 + GP, at * P:(at + 1) * P], apart[:, q, m, :],
                                                    table[:, b, q, m].rearrange(flat),
                                                    start=(q == 0), stop=(q == 1))
                        if at == HALF - 1:
                            last.then_inc(lag.sem, 1)

                def turn(n, b, more):
                    if more:
                        lags(n + 1, 1 - b)
                    u_loaded[b].wait(pe, n, 8 * T * (2 - b))
                    gathered.wait(pe, n, 2)
                    toe_ready.wait(pe, n, 1)
                    for m in range(GB):
                        ycop.wait(pe, n, max(m - 2, 0))
                        o = yp[m % 3][:, 0:CH]
                        nc.tensor.matmul(o, toe[:, b, m, :], us[:, b, m, :], start=True, stop=False)
                        for q in range(2):
                            last = nc.tensor.matmul(o, table[:, b, q, m].rearrange(flat), rhs[:, b, m, q, :],
                                                    start=False, stop=(q == 1))
                        last.then_inc(done.sem, 1)
                lags(0, 0)
                blocks(pe, turn)

            @block.scalar
            def _(act):
                ycop.start(act)
                ysto.start(act)

                def gather(n, b):
                    done.wait(act, n, -GB)
                    for rows, order in ((slice(0, NS), slice(None)), (slice(NS, P), slice(None, None, -1))):
                        for q in range(2):
                            ins = nc.scalar.activation(
                                rhs[rows, b, :, q, order],
                                t["Z"][rows, 0:CH, q, bass.ds(n * GB, GB)].rearrange("p c g -> p g c"), ACT.Copy)
                        ins.then_inc(gathered.sem, 1)

                def turn(n, b, more):
                    if more:
                        gather(n + 1, 1 - b)
                    ysto.wait(act, n, 0)
                    for m in range(GB):
                        done.wait(act, n, m + 1)
                        nc.scalar.activation(ys[:, m, :], yp[m % 3][:, 0:CH], ACT.Copy).then_inc(ycop.sem, 1)
                    ycop.wait(act, n, GB)
                    for j in range(T):
                        act.dma_start(yv[j][:, bass.ds(n * GB, GB), :],
                                      ys[j * GP:(j + 1) * GP, :, :]).then_inc(ysto.sem, 16)
                gather(0, 0)
                blocks(act, turn)
                ysto.wait(act, NB, 0)




SCALE = HD ** -0.5


def keys_values(nc, a, c, h, kr, vt):
    with stage(nc) as s:
        weights = Weights(nc, s, 4)
        rope, swap = s.sb("rope", [P, 2, L]), s.sb("swap", [P, P])
        kg, sq = s.sb("kg", [P, L]), s.sb("sq", [P, L])
        rs, tm = s.sb("rs", [P, L]), s.sb("tm", [P, L])
        kt, vf = s.sb("kt", [P, L]), s.sb("vf", [P, L])
        reg = [s.ps("product", 1536), s.ps("side", 1536)]
        load = s.sem("loaded")
        qg_ready, ss, sw = s.sem("gained"), s.sem("squares_summed"), s.sem("swapped")
        side_free, k_done, k_hi = s.sem("side_free"), s.sem("k_done"), s.sem("k_hi")
        v_copied, v_turned, v_out = s.sem("v_copied"), s.sem("v_turned"), s.sem("v_out")
        steps = s.sem("dve_steps")
        win = a["w_in_even"].rearrange("(k p) n -> p k n", p=P)
        with nc.Block() as block:
            @block.sync
            def _(sp):
                sp.dma_start(rope[:, :, :], a["rope"]).then_inc(load, 16)
                sp.dma_start(swap[:, :], a["swap"]).then_inc(load, 16)
                for u in range(4):
                    weights.load(sp, 0, u, win[:, :, K0 + u * P:K0 + (u + 1) * P])

            @block.gpsimd
            def _(gp):
                weights.split_all(gp, 1, c["ones"])

            @block.tensor
            def _(pe):
                weights.used.start(pe)
                pe.wait_ge(load, 32)
                for n in range(KV):
                    if n:
                        pe.wait_ge(qg_ready, 2 * n)
                    weights.product(pe, 0, n, reg[0], pair(h))
                    pe.wait_ge(qg_ready, 2 * n + 2)
                    if n:
                        pe.wait_ge(side_free, 2 * n)
                    for off, m in PIECES:
                        last = nc.tensor.matmul(reg[1][:, PO + off:PO + off + m], c["ones"][:, :],
                                                sq[:, off:off + m], start=True, stop=True)
                    last.then_inc(ss, 1)
                    pe.wait_ge(side_free, 2 * n + 1)
                    for off, m in PIECES:
                        last = nc.tensor.matmul(reg[1][:, PO + off:PO + off + m], swap[:, :],
                                                kg[:, off:off + m], start=True, stop=True)
                    last.then_inc(sw, 1)
                for n in range(KV):
                    if n:
                        pe.wait_ge(v_copied, n)
                    weights.product(pe, 0, KV + n, reg[0], pair(h))
                    pe.wait_ge(v_copied, n + 1)
                    pe.wait_ge(side_free, 2 * KV)
                    if n:
                        pe.wait_ge(v_out, n)
                    for t, (off, m) in enumerate(TILES):
                        last = nc.tensor.transpose(reg[1][0:m, t * P:(t + 1) * P], vf[:, off:off + m],
                                                   c["ident"][:, :])
                    last.then_inc(v_turned, 1)

            @block.scalar
            def _(act):
                for n in range(KV):
                    weights.used.wait(act, 0, n + 1)
                    if n:
                        act.wait_ge(k_done, n)
                    nc.scalar.activation(kg[:, :], rows_of(reg[0]), ACT.Copy,
                                         scale=c["col"]("k_norm", 0)).then_inc(qg_ready, 1)
                    nc.scalar.activation(sq[:, :], rows_of(reg[0]), ACT.Square).then_inc(qg_ready, 1)
                    act.wait_ge(ss, n + 1)
                    nc.scalar.activation(rs[:, :], rows_of(reg[1]), ACT.Sqrt, bias=c["eps"][:, :],
                                         scale=1.0 / HD).then_inc(side_free, 1)
                    act.wait_ge(k_done, n + 1)
                    nc.scalar.activation(kr[0][:, n, :], kt[:, :], ACT.Copy).then_inc(k_hi, 1)
                for n in range(KV):
                    weights.used.wait(act, 0, KV + n + 1)
                    if n:
                        act.wait_ge(v_turned, n)
                    nc.scalar.activation(vf[:, :], rows_of(reg[0]), ACT.Copy).then_inc(v_copied, 1)
                    act.wait_ge(v_turned, n + 1)
                    N, dn = NT - 1, slice(n * HD, (n + 1) * HD)
                    nc.scalar.activation(vt[:, 0:N, dn],
                                         reg[1][:, 0:N * P].rearrange("p (t f) -> p t f", f=P), ACT.Copy)
                    nc.scalar.activation(vt[0:TILES[N][1], N, dn], reg[1][0:TILES[N][1], N * P:NT * P],
                                         ACT.Copy).then_inc(v_out, 1)

            @block.vector
            def _(dve):
                do = Steps(dve, steps)
                for n in range(KV):
                    dve.wait_ge(side_free, 2 * n + 1)
                    do(nc.vector.reciprocal(rs[:, :], rs[:, :]))
                    if n:
                        dve.wait_ge(k_hi, n)
                    do(nc.vector.tensor_tensor(kt[:, :], kg[:, :], rope[:, 0, :], ALU.mult))
                    dve.wait_ge(sw, n + 1)
                    do(nc.vector.tensor_tensor(tm[:, :], rows_of(reg[1]), rope[:, 1, :], ALU.mult))
                    dve.sem_inc(side_free, 1)
                    do(nc.vector.tensor_tensor(kt[:, :], kt[:, :], tm[:, :], ALU.add))
                    do(nc.vector.tensor_tensor(kt[:, :], kt[:, :], rs[:, :], ALU.mult))
                    dve.sem_inc(k_done, 1)
                    dve.wait_ge(k_hi, n + 1)
                    do(nc.vector.tensor_tensor(kr[1][:, n, :], kt[:, :], kr[0][:, n, :].bitcast(F32),
                                               ALU.subtract))


def queries_gates(nc, a, c, d, h):
    base = (Q0, GA0, GB0)
    dest = (d["q"], d["ga"], d["gb"])
    with stage(nc) as s:
        weights = Weights(nc, s, 6)
        rope, swap = s.sb("rope", [P, 2, L]), s.sb("swap", [P, P])
        qg, sq, rs, tm = (s.sb(n, [P, L]) for n in ("qg", "sq", "rs", "tm"))
        res = s.sb("result", [P, 2, L])
        reg = [s.ps(f"r{b}", 1536) for b in range(2)]
        bank = s.ps("sums", 512), s.ps("swaps", 512)
        load = s.sem("loaded")
        read = [s.flag(f"region_read{b}", per=3, credit=1) for b in range(2)]
        gained = s.flag("q_gained", per=4)
        ss = s.flag("squares_summed", per=6)
        root = s.flag("root_done", per=6, credit=6)
        sw = s.flag("swapped", per=6)
        swr = s.flag("swaps_read", per=6, credit=6)
        sig = s.flag("sigmoid_done", per=4)
        made = s.flag("result_made", per=6, credit=6)
        stored = [s.flag(f"stored{b}", per=48, credit=16) for b in range(2)]
        steps = s.sem("dve_steps")
        win = a["w_in_even"].rearrange("(k p) n -> p k n", p=P)
        with nc.Block() as block:
            @block.sync
            def _(sp):
                sp.dma_start(rope[:, :, :], a["rope"]).then_inc(load, 16)
                sp.dma_start(swap[:, :], a["swap"]).then_inc(load, 16)
                with sp.Fori(0, KC // 2) as i:
                    for u in range(6):
                        weights.load(sp, i, u, win[:, :, bass.ds(i * 256 + (base[u % 3] + (u // 3) * P), P)])

            @block.gpsimd
            def _(gp):
                weights.split_all(gp, KC // 2, c["ones"])

            @block.tensor
            def _(pe):
                weights.used.start(pe)
                pe.wait_ge(load, 32)
                with pe.Fori(0, KC // 2) as i:
                    for u in range(6):
                        def between(k, u=u):
                            if u % 3 != 1 or k not in (2, 4, 6):
                                return
                            j, n = u // 3, k // 2 - 1
                            off, m = PIECES[n]
                            if n == 0:
                                gained.wait(pe, i, 2 * j + 2)
                            root.wait(pe, i, 3 * j + n)
                            nc.tensor.matmul(bank[0][:, 0:m], c["ones"][:, :], sq[:, off:off + m],
                                             start=True, stop=True).then_inc(ss.sem, 1)
                            swr.wait(pe, i, 3 * j + n)
                            nc.tensor.matmul(bank[1][:, 0:m], swap[:, :], qg[:, off:off + m],
                                             start=True, stop=True).then_inc(sw.sem, 1)
                        read[u % 2].wait(pe, i, u // 2)
                        weights.product(pe, i, u, reg[u % 2], pair(h), between=between)

            @block.scalar
            def _(act):
                for b in range(2):
                    stored[b].start(act)

                def store(i, u):
                    made.wait(act, i, u + 1)
                    act.dma_start(dest[u % 3][i * 2 + u // 3], res[:, u % 2, :]).then_inc(stored[u % 2].sem, 16)
                with act.Fori(0, KC // 2) as i:
                    for u in range(6):
                        weights.used.wait(act, i, u + 1)
                        j, r = u // 3, rows_of(reg[u % 2])
                        if u % 3 == 0:
                            made.wait(act, i, u - 2)
                            nc.scalar.activation(qg[:, :], r, ACT.Copy,
                                                 scale=c["col"]("q_norm", 0)).then_inc(gained.sem, 1)
                            nc.scalar.activation(sq[:, :], r, ACT.Square).then_inc(gained.sem, 1)
                            gained.wait(act, i, 2 * j + 2)
                            act.sem_inc(read[u % 2].sem, 1)
                            for n, (off, m) in enumerate(PIECES):
                                ss.wait(act, i, 3 * j + n + 1)
                                nc.scalar.activation(rs[:, off:off + m], bank[0][:, 0:m], ACT.Sqrt,
                                                     bias=c["eps"][:, :], scale=1.0 / HD).then_inc(root.sem, 1)
                        else:
                            stored[u % 2].wait(act, i, 16 * (u // 2))
                            nc.scalar.activation(res[:, u % 2, :], r, ACT.Sigmoid).then_inc(sig.sem, 1)
                        if u:
                            store(i, u - 1)
                    store(i, 5)
                for b in range(2):
                    stored[b].wait(act, KC // 2, 0)

            @block.vector
            def _(dve):
                v = nc.vector
                for x in (root, swr, made, read[0], read[1]):
                    x.start(dve)
                do = Steps(dve, steps)
                dve.wait_ge(load, 32)
                with do.loop(KC // 2, 2 * (3 + 3 + 2) + 2 + 4) as i:
                    for j in range(2):
                        u = 3 * j
                        b = u % 2
                        gained.wait(dve, i, 2 * j + 2)
                        stored[b].wait(dve, i, 16 * (u // 2))
                        do(v.tensor_tensor(res[:, b, :], qg[:, :], rope[:, 0, :], ALU.mult))
                        for n, (off, m) in enumerate(PIECES):
                            sw.wait(dve, i, 3 * j + n + 1)
                            do(v.tensor_tensor(tm[:, off:off + m], bank[1][:, 0:m], rope[:, 1, off:off + m], ALU.mult))
                            dve.sem_inc(swr.sem, 1)
                        for n, (off, m) in enumerate(PIECES):
                            root.wait(dve, i, 3 * j + n + 1)
                            ins = v.reciprocal(rs[:, off:off + m], rs[:, off:off + m])
                            do(ins) if n == 2 else do.free(ins)
                        do(v.tensor_tensor(res[:, b, :], res[:, b, :], tm[:, :], ALU.add))
                        do(v.tensor_tensor(res[:, b, :], res[:, b, :], rs[:, :], ALU.mult))
                        dve.sem_inc(made.sem, 1)
                        for g in range(2):
                            w = u + 1 + g
                            sig.wait(dve, i, 2 * j + g + 1)
                            do(v.tensor_tensor(res[:, w % 2, :], res[:, w % 2, :], rows_of(reg[w % 2]), ALU.mult))
                            dve.sem_inc(made.sem, 1)
                            dve.sem_inc(read[w % 2].sem, 1)


def heads(nc, c, d, kr, vt, t):
    REP = HEADS // KV
    NQ = len(QT)
    ROW = [(g, t) for g in range(KV) for t in range(NQ)]
    NR = len(ROW)
    with stage(nc) as s:
        qf = s.sb("q", [P, 2, L])
        q = s.sb("q_hi", [P, 2, L], F32R), s.sb("q_lo", [P, 2, L], F32R)
        gate = s.sb("gate", [P, 2, L])
        prob = s.sb("prob", [P, 2, L])
        pt = s.sb("prob_t", [P, 2, NT, P])
        y = s.sb("y", [P, 2, L])
        mx, sm = s.sb("mx", [P, 2, 3]), s.sb("sm", [P, 2, 2])
        scan_tmp = s.sb("scan", [P, 2, 2, G])
        sreg, treg = s.ps("scores", 1536), s.ps("turned", 1536)
        op = [s.ps(f"o{b}", 512) for b in range(2)]
        ql = [s.sem(f"q_loaded{b}") for b in range(2)]
        hid = s.flag("q_hi_done", per=2)
        q_done = s.flag("q_split", per=2)
        sc = s.flag("scores_done", per=2 * NR)
        mxd = s.flag("max_done", per=NR)
        ex = s.flag("exp_done", per=NR, credit=NR)
        nd = s.flag("normalised", per=NR)
        tu = s.flag("prob_turned", per=NR)
        tc = s.flag("turned_copied", per=NR * 2, credit=2 * NR)
        pv = s.flag("mixed", per=NR, credit=NR)
        yd = s.flag("y_ready", per=NR, credit=NR)
        stored = [s.flag(f"stored{b}", per=16, credit=16) for b in range(2)]
        steps, scan_steps, scan_turns = s.sem("dve_steps"), s.sem("scan_steps"), s.sem("scan_turns")
        tview = treg[:, :].rearrange("p (b n) -> p b n", b=3)[:, :, 0:3 * P].rearrange("p b (k q) -> p b k q", k=3)
        LATE = PIECES[-1][0]
        with nc.Block() as block:
            @block.sync
            def _(sp):
                with sp.Fori(0, REP) as i:
                    for g in range(KV):
                        yd.wait(sp, i, (g + 1) * NQ - NR)
                        sp.dma_start(qf[:, g, :], d["q"][i + g * REP]).then_inc(ql[g], 16)
                        sp.dma_start(gate[:, g, :], d["ga"][i + g * REP]).then_inc(ql[g], 16)

            @block.gpsimd
            def _(gp):
                s5_scan(nc, gp, t, scan_tmp, scan_steps, scan_turns)

            @block.tensor
            def _(pe):
                pv.start(pe)
                with pe.Fori(0, REP) as i:
                    def scores(n):
                        g, t = ROW[n]
                        off, m = QT[t]
                        if t == 0:
                            q_done.wait(pe, i, g + 1)
                        ex.wait(pe, i, n)
                        for o, w in PIECES:
                            for x, z in ((0, 1), (0, 0), (1, 0)):
                                last = nc.tensor.matmul(sreg[0:m, PO + o:PO + o + w], q[x][:, g, off:off + m],
                                                        kr[z][:, g, o:o + w], start=(z == 1), stop=(x == 1))
                            if o:
                                last.then_inc(sc.sem, 1)

                    def turn(n):
                        m = QT[ROW[n][1]][1]
                        nd.wait(pe, i, n + 1)
                        tc.wait(pe, i, 2 * n)
                        for k, (ko, kn) in enumerate(TILES):
                            last = nc.tensor.transpose(tview[0:kn, k // 3, k % 3, 0:m],
                                                       prob[0:m, n % 2, ko:ko + kn], c["ident"][0:m, 0:m])
                        last.then_inc(tu.sem, 1)

                    def mix(n):
                        g, t = ROW[n]
                        m = QT[t][1]
                        tc.wait(pe, i, 2 * n + 2)
                        yd.wait(pe, i, n - 1)
                        for k, (ko, kn) in enumerate(TILES):
                            last = nc.tensor.matmul(op[n % 2][:, 0:m], vt[0:kn, k, g * HD:(g + 1) * HD],
                                                    pt[0:kn, n % 2, k, 0:m], start=(k == 0), stop=(k == NT - 1))
                        last.then_inc(pv.sem, 1)

                    scores(0)
                    for n in range(NR + 1):
                        if n + 1 < NR:
                            scores(n + 1)
                        if n < NR:
                            turn(n)
                        if n:
                            mix(n - 1)

            @block.scalar
            def _(act):
                for b in range(2):
                    stored[b].start(act)
                with act.Fori(0, REP) as i:
                    def leading(g):
                        act.wait_ge(ql[g], i * 32 + 32)
                        nc.scalar.activation(q[0][:, g, :], qf[:, g, :], ACT.Copy).then_inc(hid.sem, 1)
                    leading(0)
                    for n in range(NR + 1):
                        if n < NR:
                            m = QT[ROW[n][1]][1]
                            mxd.wait(act, i, n + 1)
                            if n >= 2:
                                tu.wait(act, i, n - 1)
                            nc.scalar.activation(prob[0:m, n % 2, :], rows_of(sreg)[0:m], ACT.Exp,
                                                 bias=mx[0:m, n % 2, 2:3], scale=SCALE,
                                                 accum_out=sm[0:m, n % 2, 0:1]).then_inc(ex.sem, 1)
                        if n:
                            m = QT[ROW[n - 1][1]][1]
                            tu.wait(act, i, n)
                            pv.wait(act, i, n - 2)
                            nc.scalar.activation(pt[:, (n - 1) % 2, 0:3, 0:m], tview[:, 0, :, 0:m],
                                                 ACT.Copy).then_inc(tc.sem, 1)
                        if n == 2:
                            leading(1)
                        if n in (NQ + 3, NR):
                            g = n // NR
                            yd.wait(act, i, (g + 1) * NQ)
                            act.dma_start(d["cat"][i + g * REP], y[:, g, :]).then_inc(stored[g].sem, 16)
                for b in range(2):
                    stored[b].wait(act, REP, 0)

            @block.vector
            def _(dve):
                v = nc.vector
                for x in (yd, tc, ex):
                    x.start(dve)
                do = Steps(dve, steps)
                with do.loop(REP, 2 + 3 * NR) as i:
                    def rest(g):
                        hid.wait(dve, i, g + 1)
                        do(v.tensor_tensor(q[1][:, g, :], qf[:, g, :], q[0][:, g, :].bitcast(F32), ALU.subtract))
                        dve.sem_inc(q_done.sem, 1)
                    rest(0)
                    for n in range(NR + 2):
                        b = n % 2
                        if n < NR:
                            m = QT[ROW[n][1]][1]
                            sc.wait(dve, i, 2 * n + 1)
                            do.free(v.tensor_reduce(mx[0:m, b, 0:1], rows_of(sreg)[0:m, 0:LATE], AX, ALU.max))
                            sc.wait(dve, i, 2 * n + 2)
                            do(v.tensor_reduce(mx[0:m, b, 1:2], rows_of(sreg)[0:m, LATE:L], AX, ALU.max))
                            v.tensor_scalar(mx[0:m, b, 2:3], mx[0:m, b, 0:1], mx[0:m, b, 1:2], -SCALE,
                                            ALU.max, ALU.mult).then_inc(mxd.sem, 1)
                        if 1 <= n <= NR:
                            m = QT[ROW[n - 1][1]][1]
                            tu.wait(dve, i, n)
                            pv.wait(dve, i, n - 2)
                            v.tensor_copy(pt[:, 1 - b, 3:6, 0:m],
                                          tview[:, 1, :, 0:m])
                            v.tensor_copy(pt[:, 1 - b, 6:8, 0:m], tview[:, 2, 0:2, 0:m])
                            v.tensor_copy(pt[0:TILES[-1][1], 1 - b, 8, 0:m],
                                          tview[0:TILES[-1][1], 2, 2, 0:m]).then_inc(tc.sem, 1)
                        if n == 2:
                            rest(1)
                        if n < NR:
                            m = QT[ROW[n][1]][1]
                            ex.wait(dve, i, n + 1)
                            do(v.reciprocal(sm[0:m, b, 1:2], sm[0:m, b, 0:1]))
                            v.tensor_scalar(prob[0:m, b, :], prob[0:m, b, :], sm[0:m, b, 1:2], None,
                                            ALU.mult).then_inc(nd.sem, 1)
                        if n >= 2:
                            g, t = ROW[n - 2]
                            off, m = QT[t]
                            if t == 0:
                                stored[g].wait(dve, i, 0)
                            pv.wait(dve, i, n - 1)
                            v.tensor_tensor(y[:, g, off:off + m], op[b][:, 0:m],
                                            gate[:, g, off:off + m], ALU.mult).then_inc(yd.sem, 1)


def s5_glu(nc, a, c, d):
    with stage(nc) as s:
        weights = Weights(nc, s, 2)
        y = s.sb("y", [P, KC, L])
        yr = [s.sb(n, [P, KC, L], F32R) for n in ("y_hi", "y_lo")]
        yin = s.sb("y_in", [P, 2, T, CH])
        sg, gate, out = s.sb("sigmoid", [P, 2, L]), s.sb("gate", [P, 2, L]), s.sb("out", [P, 2, L])
        reg = [s.ps(f"r{b}", 1536) for b in range(2)]
        yl = [s.sem(f"y_loaded{b}") for b in range(2)]
        gl = [s.sem(f"gate_loaded{b}") for b in range(2)]
        gelu, hid, lod = s.sem("gelu_done"), s.sem("hi_done"), s.sem("lo_done")
        sig = s.flag("sigmoid_done", per=2, credit=2)
        gated = s.flag("gated", per=2, credit=2)
        stored = [s.flag(f"stored{b}", per=16, credit=16) for b in range(2)]
        steps = s.sem("dve_steps")
        yv = d["y"].rearrange("(j g) p s c -> j (g p) (s c)", j=KC)
        glu = a["w_glu"].rearrange("(k p) n -> p k n", p=P)
        with nc.Block() as block:
            @block.sync
            def _(sp):
                for j in range(KC):
                    if j >= 2:
                        sp.wait_ge(gelu, j - 1)
                    sp.dma_start(yin[:, j % 2, :, :], yv[j]).then_inc(yl[j % 2], 16)
                with sp.Fori(0, KC // 2) as i:
                    for b in range(2):
                        weights.load(sp, i, b, glu[:, :, bass.ds(i * 256 + b * P, P)])
                        gated.wait(sp, i, b - 1)
                        sp.dma_start(gate[:, b, :], d["gb"][i * 2 + b]).then_inc(gl[b], 16)

            @block.gpsimd
            def _(gp):
                weights.split_all(gp, KC // 2, c["ones"])

            @block.tensor
            def _(pe):
                weights.used.start(pe)

                def rows(k):
                    pe.wait_ge(lod, k + 1)
                    return yr[0][:, k, :], yr[1][:, k, :]
                with pe.Fori(0, KC // 2) as i:
                    for b in range(2):
                        sig.wait(pe, i, b - 1)
                        weights.product(pe, i, b, reg[b], rows)

            @block.scalar
            def _(act):
                sig.start(act)
                for b in range(2):
                    stored[b].start(act)
                for j in range(KC):
                    act.wait_ge(yl[j % 2], 16 * (j // 2 + 1))
                    nc.scalar.activation(y[:, j, :].rearrange("p (c s) -> p s c", s=T), yin[:, j % 2, :, :],
                                         ACT.Gelu_apprx_tanh).then_inc(gelu, 1)
                    act.wait_ge(gelu, j + 1)
                    nc.scalar.activation(yr[0][:, j, :], y[:, j, :], ACT.Copy).then_inc(hid, 1)
                with act.Fori(0, KC // 2) as i:
                    for b in range(2):
                        weights.used.wait(act, i, b + 1)
                        gated.wait(act, i, b - 1)
                        nc.scalar.activation(sg[:, b, :], rows_of(reg[b]), ACT.Sigmoid,
                                             bias=c["cols_a"][:, bass.ds(i * 2 + (c["b_glu"] + b), 1)]
                                             ).then_inc(sig.sem, 1)
                    for b in range(2):
                        gated.wait(act, i, b + 1)
                        act.dma_start(d["cat"][i * 2 + (KC + b)], out[:, b, :]).then_inc(stored[b].sem, 16)
                for b in range(2):
                    stored[b].wait(act, KC // 2, 0)

            @block.vector
            def _(dve):
                gated.start(dve)
                do = Steps(dve, steps)
                for j in range(KC):
                    dve.wait_ge(hid, j + 1)
                    nc.vector.tensor_tensor(yr[1][:, j, :], y[:, j, :], yr[0][:, j, :].bitcast(F32),
                                            ALU.subtract).then_inc(lod, 1)
                with do.loop(KC // 2, 2) as i:
                    for b in range(2):
                        dve.wait_ge(gl[b], i * 16 + 16)
                        stored[b].wait(dve, i, 0)
                        do(nc.vector.tensor_tensor(out[:, b, :], gate[:, b, :],
                                                   y[:, bass.ds(i * 2 + b, 1), :].rearrange("p k t -> p (k t)"),
                                                   ALU.mult))
                        sig.wait(dve, i, b + 1)
                        nc.vector.tensor_tensor(out[:, b, :], out[:, b, :], sg[:, b, :],
                                                ALU.mult).then_inc(gated.sem, 1)


def project(nc, w_out, cat, c, y):
    SLOTS = 4
    with stage(nc) as s:
        x = [s.sb(n, [P, 2 * KC, L], F32R) for n in ("x_hi", "x_lo")]
        weights = Weights(nc, s, 4)
        reg = [s.ps(f"r{b}", 1536) for b in range(2)]
        xl = [s.sem(f"x_loaded{b}") for b in range(SLOTS)]
        hid, lod = s.sem("hi_done"), s.sem("lo_done")
        cop = s.flag("copied", per=2, credit=2)
        wv = w_out.rearrange("(h k p) n -> h p k n", p=P, k=KC)
        raw = [y[:, b, :] for b in range(SLOTS)]
        with nc.Block() as block:
            @block.sync
            def _(sp):
                with sp.Fori(0, KC // 2) as i:
                    for u in range(4):
                        weights.load(sp, i, u, wv[u // 2, :, :, bass.ds(i * 256 + (u % 2) * P, P)])

            @block.gpsimd
            def _(gp):
                weights.split_all(gp, KC // 2, c["ones"])

            @block.tensor
            def _(pe):
                weights.used.start(pe)
                with pe.Fori(0, KC // 2) as i:
                    for u in range(4):
                        def rows(k, u=u):
                            k += KC * (u // 2)
                            pe.wait_ge(lod, k + 1)
                            return x[0][:, k, :], x[1][:, k, :]
                        if u < 2:
                            cop.wait(pe, i, u - 1)
                        weights.product(pe, i, u, reg[u % 2], rows, first=(u < 2), last=(u >= 2))

            @block.scalar
            def _(act):
                cop.start(act)
                for k in range(2 * KC + SLOTS - 1):
                    if k < 2 * KC:
                        if k >= SLOTS:
                            act.wait_ge(lod, k - SLOTS + 1)
                        act.dma_start(raw[k % SLOTS], cat[k]).then_inc(xl[k % SLOTS], 16)
                    t = k - SLOTS + 1
                    if t >= 0:
                        act.wait_ge(xl[t % SLOTS], 16 * (t // SLOTS + 1))
                        nc.scalar.activation(x[0][:, t, :], raw[t % SLOTS], ACT.Copy).then_inc(hid, 1)
                with act.Fori(0, KC // 2) as i:
                    for b in range(2):
                        weights.used.wait(act, i, b + 3)
                        nc.scalar.activation(y[:, bass.ds(i * 2 + b, 1), :].rearrange("p k t -> p (k t)"),
                                             rows_of(reg[b]), ACT.Copy).then_inc(cop.sem, 1)

            @block.vector
            def _(dve):
                for t in range(2 * KC):
                    dve.wait_ge(hid, t + 1)
                    nc.vector.tensor_tensor(x[1][:, t, :], raw[t % SLOTS], x[0][:, t, :].bitcast(F32),
                                            ALU.subtract).then_inc(lod, 1)


def leave(nc, c, res, out):
    with stage(nc) as s:
        ot = s.sb("ot", [P, 2, D])
        pt = [s.ps(f"pt{b}", 512) for b in range(4)]
        turned, copied, stored = s.sem("turned"), s.sem("copied"), [s.sem("stored0"), s.sem("stored1")]
        n_tiles = (L - META) // P
        with nc.Block() as block:
            @block.tensor
            def _(pe):
                for i in range(n_tiles):
                    for half in range(2):
                        n = 2 * i + half
                        if n >= 4:
                            pe.wait_ge(copied, n - 3)
                        for k in range(4):
                            last = nc.tensor.transpose(pt[n % 4][:, k * P:(k + 1) * P],
                                                       res[:, 4 * half + k, META + i * P:META + (i + 1) * P],
                                                       c["ident"][:, :])
                        last.then_inc(turned, 1)

            @block.vector
            def _(dve):
                for n in range(2 * n_tiles):
                    i = n // 2
                    dve.wait_ge(turned, n + 1)
                    if i >= 2 and n % 2 == 0:
                        dve.wait_ge(stored[i % 2], 16 * (i // 2))
                    nc.vector.tensor_copy(ot[:, i % 2, 512 * (n % 2):512 * (n % 2) + 512],
                                          pt[n % 4][:, :]).then_inc(copied, 1)

            @block.sync
            def _(sp):
                for i in range(n_tiles):
                    sp.wait_ge(copied, 2 * i + 2)
                    sp.dma_start(out[i * P:(i + 1) * P, :], ot[:, i % 2, :]).then_inc(stored[i % 2], 16)
                for b in range(2):
                    sp.wait_ge(stored[b], 16 * n_tiles // 2)


def gate_memory(s):
    return dict(w=s.sb("w_gates", [P, 2 * KC, 104]), bias=s.sb("b_gates", [P, 1]),
                loaded=s.sem("gate_weights_loaded"))


def load_gates(eng, a, gates):
    for n, name in enumerate(("igate", "fgate")):
        for r in range(2):
            at = 64 * n + 32 * r
            eng.dma_start(gates["w"][:, :, at:at + MH],
                          a["w_" + name][r].rearrange("(k p) h -> p k h", p=P)).then_inc(gates["loaded"], 16)
            eng.dma_start(gates["bias"][at:at + MH, :],
                          a["b_" + name][r].unsqueeze(1)).then_inc(gates["loaded"], 16)


def conv_values_z(nc, a, c, d, h, gates):
    EDGE = CONV // 2
    with stage(nc) as s:
        weights = Weights(nc, s, 4)
        wv = s.sb("w_v", [P, 2, MV])
        xm = s.sb("xm", [P, 2, L + 2 * EDGE])
        acc, sg, zs, xz = (s.sb(n, [P, 2, L]) for n in ("acc", "sg", "zs", "xz"))
        vs = s.sb("vs", [P, NT, MV])
        reg = [s.ps(f"r{b}", 1536) for b in range(2)]
        vp = [s.ps(f"v{b}", 512) for b in range(2)]
        wvl = s.sem("wv_loaded")
        cop = s.flag("xm_copied", per=2, credit=2)
        vmm = s.flag("v_projected", per=NT, credit=NT)
        vcop = s.flag("v_copied", per=NT, credit=NT)
        conv = s.flag("convolved", per=2, credit=2)
        sig = s.flag("sigmoid_done", per=2)
        zsig = s.flag("z_sigmoid_done", per=2)
        zdone = s.flag("z_done", per=2, credit=2)
        act_done = s.flag("xc_done", per=2, credit=2)
        xzd = s.flag("xz_done", per=2, credit=2)
        stored = [s.flag(f"stored_{n}", per=16, credit=16) for n in ("v", "xc", "z", "xz")]
        steps = s.sem("dve_steps")
        cleared = s.sem("gate_weights_cleared")
        win = a["w_in_odd"].rearrange("(k p) n -> p k n", p=P)
        wvv = a["w_v"].rearrange("h (c p) n -> h p c n", p=P)
        with nc.Block() as block:
            @block.sync
            def _(sp):
                with sp.Fori(0, MH) as i:
                    for u in range(4):
                        weights.load(sp, i, u, win[:, :, bass.ds(i * 256 + (W2 * (u // 2) + (u % 2) * P), P)])
                        if u == 1:
                            vmm.wait(sp, i, 0)
                            sp.dma_start(wv[:, :, :], wvv[i]).then_inc(wvl, 16)

            @block.gpsimd
            def _(gp):
                weights.split_all(gp, MH, c["ones"])

            @block.tensor
            def _(pe):
                weights.used.start(pe)
                vmm.start(pe)
                with pe.Fori(0, MH) as i:
                    for b in range(2):
                        zdone.wait(pe, i, b - 1)
                        weights.product(pe, i, b, reg[b], pair(h))

                    def values(u):
                        def between(k):
                            t = k - 5 if u == 2 else k + 2
                            if not 0 <= t < NT:
                                return
                            if t == 0:
                                pe.wait_ge(wvl, i * 16 + 16)
                                cop.wait(pe, i, 2)
                            off, m = TILES[t]
                            vcop.wait(pe, i, t - 1)
                            for b in range(2):
                                last = nc.tensor.matmul(vp[t % 2][0:m, 0:MV], xm[:, b, EDGE + off:EDGE + off + m],
                                                        wv[:, b, :], start=(b == 0), stop=(b == 1))
                            last.then_inc(vmm.sem, 1)
                        return between
                    cop.wait(pe, i, 1)
                    weights.product(pe, i, 2, reg[0], pair(h), between=values(2))
                    cop.wait(pe, i, 2)
                    weights.product(pe, i, 3, reg[1], pair(h), between=values(3))
                    vcop.wait(pe, i, NT)

            @block.scalar
            def _(act):
                act.wait_ge(cleared, 1)
                load_gates(act, a, gates)
                cop.start(act)
                vcop.start(act)
                for x in stored:
                    x.start(act)
                with act.Fori(0, MH) as i:
                    for b in range(2):
                        weights.used.wait(act, i, b + 1)
                        conv.wait(act, i, b - 1)
                        vmm.wait(act, i, 0)
                        nc.scalar.activation(xm[:, b, EDGE:EDGE + L], rows_of(reg[b]), ACT.Copy).then_inc(cop.sem, 1)
                    stored[0].wait(act, i, 0)
                    for t, (off, m) in enumerate(TILES):
                        if t == 2:
                            weights.used.wait(act, i, 3)
                            stored[2].wait(act, i, 0)
                            xzd.wait(act, i, 0)
                            nc.scalar.activation(zs[:, 0, :], rows_of(reg[0]), ACT.Sigmoid).then_inc(zsig.sem, 1)
                        vmm.wait(act, i, t + 1)
                        nc.scalar.activation(vs[0:m, t, :], vp[t % 2][0:m, 0:MV], ACT.Copy).then_inc(vcop.sem, 1)
                    vcop.wait(act, i, NT)
                    act.dma_start(d["v"][i], vs[:, :, :]).then_inc(stored[0].sem, 16)
                    stored[1].wait(act, i, 0)
                    xzd.wait(act, i, 0)
                    for b in range(2):
                        conv.wait(act, i, b + 1)
                        nc.scalar.activation(sg[:, b, :], acc[:, b, :], ACT.Sigmoid).then_inc(sig.sem, 1)
                    act_done.wait(act, i, 2)
                    act.dma_start(d["xc"][bass.ds(i * 2, 2), :, :].rearrange("b p t -> p b t"), sg[:, :, :])\
                        .then_inc(stored[1].sem, 16)
                    weights.used.wait(act, i, 4)
                    nc.scalar.activation(zs[:, 1, :], rows_of(reg[1]), ACT.Sigmoid).then_inc(zsig.sem, 1)
                    zdone.wait(act, i, 2)
                    act.dma_start(d["z"][bass.ds(i * 2, 2), :, :].rearrange("b p t -> p b t"), zs[:, :, :])\
                        .then_inc(stored[2].sem, 16)
                    xzd.wait(act, i, 2)
                    act.dma_start(d["xz"][bass.ds(i * 2, 2), :, :].rearrange("b p t -> p b t"), xz[:, :, :])\
                        .then_inc(stored[3].sem, 16)
                for x in stored:
                    x.wait(act, MH, 0)

            @block.vector
            def _(dve):
                do = Steps(dve, steps)
                nc.vector.memset(gates["w"][:, :, :], 0.0).then_inc(cleared, 1)
                do.free(nc.vector.memset(vs[:, NT - 1, :], 0.0))
                for b in range(2):
                    do.free(nc.vector.memset(xm[:, b, 0:EDGE], 0.0))
                    do(nc.vector.memset(xm[:, b, EDGE + L:], 0.0))
                conv.start(dve)
                act_done.start(dve)
                zdone.start(dve)
                xzd.start(dve)
                with do.loop(MH, 2 * (CONV - 1)) as i:
                    def tap(n, b):
                        return c["conv_w"][:, bass.ds(i * 2 + (n * 2 * KC + b), 1)]

                    def z(b):
                        zsig.wait(dve, i, b + 1)
                        nc.vector.tensor_tensor(zs[:, b, :], zs[:, b, :], rows_of(reg[b]),
                                                ALU.mult).then_inc(zdone.sem, 1)
                    for b in range(2):
                        cop.wait(dve, i, b + 1)
                        act_done.wait(dve, i, b - 1)
                        do(nc.vector.tensor_scalar(acc[:, b, :], xm[:, b, 0:L], tap(0, b),
                                                   c["cols_a"][:, bass.ds(i * 2 + (c["conv_b"] + b), 1)],
                                                   ALU.mult, ALU.add))
                        for n in range(1, CONV):
                            ins = nc.vector.scalar_tensor_tensor(acc[:, b, :], xm[:, b, n:n + L], tap(n, b),
                                                                 acc[:, b, :], ALU.mult, ALU.add)
                            if n < CONV - 1:
                                do(ins)
                        ins.then_inc(conv.sem, 1)
                    z(0)
                    for b in range(2):
                        sig.wait(dve, i, b + 1)
                        nc.vector.tensor_tensor(sg[:, b, :], acc[:, b, :], sg[:, b, :],
                                                ALU.mult).then_inc(act_done.sem, 1)
                    z(1)
                    stored[3].wait(dve, i, 0)
                    act_done.wait(dve, i, 2)
                    zdone.wait(dve, i, 2)
                    for b in range(2):
                        nc.vector.tensor_tensor(xz[:, b, :], sg[:, b, :], zs[:, b, :],
                                                ALU.mult).then_inc(xzd.sem, 1)


def odd_gates(nc, a, c, d, gates, raw):
    SLOTS = 4
    F, B = slice(0, MH), slice(32, 40)
    with stage(nc) as s:
        x = [s.sb(n, [P, 2 * KC, L], F32R) for n in ("xc_hi", "xc_lo")]
        weights = Weights(nc, s, 6, tiles=(2, 2, KC, KC, KC, KC))
        buf = s.sb("buffer", [P, SLOTS, L])
        kt = s.sb("kt", [P, NT, MK])
        zt = s.sb("z", [P, 2, L])
        wg, bias = gates["w"], gates["bias"]
        reg = [s.ps(f"r{b}", 1536) for b in range(2)]
        bank = [s.ps(f"kt{b}", 512) for b in range(2)]
        xl = [s.sem(f"x_loaded{b}") for b in range(SLOTS)]
        cleared = s.sem("cleared")
        gmm, copied = s.sem("gate_products"), s.sem("gates_copied")
        hid, lod = s.sem("hi_done"), s.sem("lo_done")
        read = s.flag("region_read", per=4, credit=2)
        zl = s.sem("z_loaded")
        gated = s.flag("o_gated", per=2, credit=2)
        ktt = s.flag("kt_turned", per=3)
        ktc = s.flag("kt_copied", per=3, credit=3)
        stored = [s.flag(f"stored_{n}", per=16, credit=16) for n in ("q", "k", "o0", "o1", "kt")]
        wog = a["w_ogate"].rearrange("(h k p) n -> h p k n", p=P, k=KC)
        wqv = [a[n].rearrange("h (c p) n -> h p c n", p=P) for n in ("w_q", "w_k")]
        N = NT - 1
        parts = [(0, 4, 0), (4, 8, 1), (8, 9, 0)]
        with nc.Block() as block:
            @block.sync
            def _(sp):
                with sp.Fori(0, MH) as i:
                    for u in range(6):
                        if u < 2:
                            weights.load(sp, i, u, wqv[u][i])
                        else:
                            weights.load(sp, i, u, wog[u % 2, :, :, bass.ds(i * 256 + (u // 2 - 1) * P, P)])
                        if u == 3:
                            gated.wait(sp, i, 0)
                            sp.dma_start(zt[:, :, :], d["z"][bass.ds(i * 2, 2), :, :]
                                         .rearrange("b p t -> p b t")).then_inc(zl, 16)

            @block.gpsimd
            def _(gp):
                weights.split_all(gp, MH, c["ones"])

            @block.tensor
            def _(pe):
                weights.used.start(pe)
                pe.wait_ge(gates["loaded"], 16 * 8)
                for k in range(2 * KC):
                    pe.wait_ge(xl[k % SLOTS], 16 * (k // SLOTS + 1))
                    for off, n in PIECES:
                        last = nc.tensor.matmul(reg[0][0:104, PO + off:PO + off + n], wg[:, k, :],
                                                buf[:, k % SLOTS, off:off + n],
                                                start=(k == 0), stop=(k == 2 * KC - 1))
                    last.then_inc(gmm, 1)
                pe.wait_ge(lod, 2 * KC)
                pe.wait_ge(copied, 4)
                with pe.Fori(0, MH) as i:
                    for u in range(2):
                        def rows(k):
                            return tuple(z[:, bass.ds(i * 2 + k, 1), :].rearrange("p k t -> p (k t)") for z in x)
                        read.wait(pe, i, u - 1)
                        weights.product(pe, i, u, reg[u], rows)
                    for u in range(2, 6):
                        def rows(k, u=u):
                            k += KC * (u % 2)
                            return x[0][:, k, :], x[1][:, k, :]

                        def between(k, u=u):
                            if u != 3 or k not in (0, 2, 4):
                                return
                            n = k // 2
                            t0, t1, b = parts[n]
                            if n == 0:
                                read.wait(pe, i, 2)
                            ktc.wait(pe, i, (0, 0, 1)[n])
                            for t in range(t0, t1):
                                off, m = TILES[t]
                                last = nc.tensor.transpose(bank[b][0:m, (t - t0) * P:(t - t0 + 1) * P],
                                                           buf[:, 1, off:off + m], c["ident"][:, :])
                            last.then_inc(ktt.sem, 1)
                        if u % 2 == 0:
                            read.wait(pe, i, u // 2)
                        weights.product(pe, i, u, reg[u // 2 - 1], rows, first=(u % 2 == 0), last=(u % 2 == 1),
                                        between=between)

            @block.scalar
            def _(act):
                for x_ in stored:
                    x_.start(act)
                for k in range(2 * KC + SLOTS - 1):
                    if k < 2 * KC:
                        if k >= SLOTS:
                            act.wait_ge(lod, k - SLOTS + 1)
                            act.wait_ge(gmm, k - SLOTS + 1)
                        act.dma_start(buf[:, k % SLOTS, :], d["xc"][k]).then_inc(xl[k % SLOTS], 16)
                    t = k - SLOTS + 1
                    if t >= 0:
                        act.wait_ge(xl[t % SLOTS], 16 * (t // SLOTS + 1))
                        nc.scalar.activation(x[0][:, t, :], buf[:, t % SLOTS, :], ACT.Copy).then_inc(hid, 1)
                act.wait_ge(gmm, 2 * KC)
                act.wait_ge(cleared, 1)
                act.wait_ge(lod, 2 * KC)
                g = rows_of(reg[0])
                for dst, at in ((raw[0], 0), (raw[1], 64)):
                    nc.scalar.activation(dst[F, :], g[at:at + MH], ACT.Identity,
                                         bias=bias[at:at + MH, :]).then_inc(copied, 1)
                    nc.scalar.activation(dst[B, :], g[at + 32:at + 32 + MH, ::-1], ACT.Identity,
                                         bias=bias[at + 32:at + 32 + MH, :]).then_inc(copied, 1)
                read.start(act)
                with act.Fori(0, MH) as i:
                    weights.used.wait(act, i, 1)
                    stored[0].wait(act, i, 0)
                    nc.scalar.activation(buf[:, 0, :], rows_of(reg[0]), ACT.Copy,
                                         scale=MK ** -0.5).then_inc(read.sem, 1)
                    weights.used.wait(act, i, 2)
                    stored[1].wait(act, i, 0)
                    nc.scalar.activation(buf[:, 1, :], rows_of(reg[1]), ACT.Copy).then_inc(read.sem, 1)
                    for n in range(2):
                        read.wait(act, i, n + 1)
                        act.dma_start(d["qk"][i][n], buf[:, n, :]).then_inc(stored[n].sem, 16)
                    for b in range(2):
                        weights.used.wait(act, i, 2 * b + 4)
                        stored[2 + b].wait(act, i, 0)
                        nc.scalar.activation(buf[:, 2 + b, :], rows_of(reg[b]), ACT.Sigmoid,
                                             bias=c["cols_a"][:, bass.ds(i * 2 + (c["b_ogate"] + b), 1)]
                                             ).then_inc(read.sem, 1)
                        gated.wait(act, i, b + 1)
                        act.dma_start(d["o"][i * 2 + b], buf[:, 2 + b, :]).then_inc(stored[2 + b].sem, 16)
                    ktc.wait(act, i, 3)
                    act.dma_start(d["kt"][i], kt[:, :, :]).then_inc(stored[4].sem, 16)
                for x_ in stored:
                    x_.wait(act, MH, 0)

            @block.vector
            def _(dve):
                v = nc.vector
                v.memset(raw[0][:, :], 0.0)
                v.memset(kt[:, N, :], 0.0)
                v.memset(raw[1][:, :], 0.0).then_inc(cleared, 1)
                ktc.start(dve)
                gated.start(dve)
                for k in range(2 * KC):
                    dve.wait_ge(hid, k + 1)
                    v.tensor_tensor(x[1][:, k, :], buf[:, k % SLOTS, :], x[0][:, k, :].bitcast(F32),
                                    ALU.subtract).then_inc(lod, 1)
                with dve.Fori(0, MH) as i:
                    for n, (t0, t1, b) in enumerate(parts):
                        ktt.wait(dve, i, n + 1)
                        if n == 0:
                            stored[4].wait(dve, i, 0)
                        m = TILES[t1 - 1][1]
                        v.tensor_copy(kt[0:m, t0:t1, :],
                                      bank[b][0:m, 0:(t1 - t0) * P].rearrange("p (t k) -> p t k", k=MK)
                                      ).then_inc(ktc.sem, 1)
                    dve.wait_ge(zl, i * 16 + 16)
                    for f in range(2):
                        read.wait(dve, i, f + 3)
                        v.tensor_tensor(buf[:, 2 + f, :], buf[:, 2 + f, :], zt[:, f, :],
                                        ALU.mult).then_inc(gated.sem, 1)


def gate_rows(nc, a, c, d, raw, cols):
    R = 40
    F, B = slice(0, MH), slice(32, 40)
    with stage(nc) as s:
        keep = s.sb("keep", [R, L])
        li, fx = raw
        lf, e1, mn = (s.sb(n, [R, L]) for n in ("lf", "e1", "mn"))
        b_, m_ = s.sb("b", [R, L]), s.sb("m", [R, L])
        bn, m_n, ln = s.sb("bn", [R, L]), s.sb("mn2", [R, L]), s.sb("ln", [R, L])
        row = s.sb("row", [R, 3, L])
        bm = s.sb("bm", [R, L])
        end = s.sb("end", [R, 6, NT])
        ends = s.sb("ends", [R, 2, NT])
        tp = [s.ps(f"tp{q}", 512) for q in range(3)]
        load = s.sem("loaded")
        logged = s.sem("log_done")
        asked, answered = s.sem("function_asked"), s.sem("function_done")
        rows, turned, stored = s.sem("rows_ready"), s.sem("turned"), s.sem("stored")
        steps, asteps = s.sem("dve_steps"), s.sem("act_steps")
        with nc.Block() as block:
            @block.sync
            def _(sp):
                sp.dma_start(keep[:, :], a["starts"]).then_inc(load, 16)
                sp.wait_ge(rows, 1)
                for r, part in enumerate((F, B)):
                    sp.dma_start(d["bm"][r], bm[part, :]).then_inc(stored, 16)
                    sp.dma_start(d["ends"][r], ends[part, :, :]).then_inc(stored, 16)
                sp.wait_ge(stored, 64)

            @block.tensor
            def _(pe):
                pe.wait_ge(rows, 1)
                for q in range(3):
                    for t, (off, m) in enumerate(TILES):
                        last = nc.tensor.transpose(tp[q][0:m, R * t:R * t + R], row[:, q, off:off + m],
                                                   c["ident"][0:R, 0:R])
                    last.then_inc(turned, 1)

            @block.scalar
            def _(act):
                do = Steps(act, asteps)
                do(nc.scalar.activation(e1[:, :], fx[:, :], ACT.Abs))
                do(nc.scalar.activation(e1[:, :], e1[:, :], ACT.Exp, scale=-1.0))
                nc.scalar.activation(lf[:, :], e1[:, :], ACT.Ln, bias=1.0).then_inc(logged, 1)
                act.wait_ge(asked, 1)
                nc.scalar.activation(row[:, 1, :], row[:, 1, :], ACT.Exp)
                nc.scalar.activation(row[:, 2, :], m_n[:, :], ACT.Exp, scale=-1.0)
                nc.scalar.activation(ends[:, 1, :], end[:, 4, :], ACT.Exp).then_inc(answered, 1)

            @block.vector
            def _(dve):
                v = nc.vector
                do = Steps(dve, steps)
                for x in (bn, m_n, ln):
                    do.free(v.memset(x[:, :], 0.0))
                do.free(v.memset(end[:, :, :], 0.0))
                do(v.memset(cols[:, NT - 1, :, :], 0.0))
                dve.wait_ge(load, 16)
                dve.wait_ge(logged, 1)
                do(v.tensor_scalar(mn[:, :], fx[:, :], 0.0, None, ALU.min))
                do(v.tensor_tensor(lf[:, :], mn[:, :], lf[:, :], ALU.subtract))
                do.free(v.tensor_tensor_scan(b_[:, :], keep[:, :], lf[:, :], 0.0, ALU.mult, ALU.add))
                do(v.tensor_tensor_scan(m_[:, :], lf[:, :], li[:, :], 0.0, ALU.add, ALU.max))
                for dst, src in ((bn, b_), (m_n, m_), (ln, li)):
                    do.free(v.tensor_copy(dst[F, :], src[F, :]))
                    do(v.tensor_copy(dst[B, :], src[B, ::-1]))
                N = NT - 1
                for q, src in ((0, bn), (1, m_n)):
                    do.free(v.tensor_copy(end[F, q, 0:N], src[F, P - 1:N * P:P]))
                    do.free(v.tensor_copy(end[F, q, N:NT], src[F, L - 1:L]))
                    do(v.tensor_copy(end[B, q, 0:NT], src[B, 0:L:P]))
                do.free(v.tensor_copy(end[F, 2, 1:NT], end[F, 1, 0:N]))
                do(v.tensor_copy(end[B, 2, 0:N], end[B, 1, 1:NT]))
                do(v.tensor_copy(ends[:, 0, :], end[:, 2, :]))
                do(v.tensor_tensor(end[:, 3, :], end[:, 0, :], end[:, 1, :], ALU.subtract))
                do(v.tensor_tensor(end[:, 4, :], end[:, 3, :], end[:, 2, :], ALU.add))
                do(v.tensor_tensor(row[:, 0, :], ln[:, :], bn[:, :], ALU.subtract))
                do(v.tensor_tensor(bm[:, :], bn[:, :], m_n[:, :], ALU.subtract))
                for t, (off, m) in enumerate(TILES):
                    do(v.tensor_scalar(row[:, 1, off:off + m], row[:, 0, off:off + m], end[:, 3, t:t + 1], None, ALU.add))
                dve.sem_inc(asked, 1)
                dve.wait_ge(answered, 1)
                dve.sem_inc(rows, 1)
                for q in range(3):
                    dve.wait_ge(turned, q + 1)
                    view = tp[q][:, 0:R * NT].rearrange("p (t r) -> p t r", r=R)
                    v.tensor_copy(cols[:, 0:N, q, 0:R], view[:, 0:N, :])
                    v.tensor_copy(cols[0:TILES[N][1], N, q, 0:R], view[0:TILES[N][1], N, :])


def mlstm(nc, a, c, d, cols):
    LS, WS, FLOOR = 0, 1, 2
    N = NT - 1
    VW = MV + 1
    LANES = range(2)
    with stage(nc) as s:
        def lanes(make, name, *args, **kw):
            return [make(f"{name}{l}", *args, **kw) for l in LANES]
        masks = s.sb("masks", [P, 2, P])
        endb = s.sb("ends_b", [P, 2, MH, 2, NT])
        v1 = [lanes(s.sb, f"v{b}_", [P, NT, VW]) for b in range(2)]
        qk = [lanes(s.sb, f"qk{b}_", [P, 2, L]) for b in range(2)]
        kt = [lanes(s.sb, f"kt{b}_", [P, NT, MK]) for b in range(2)]
        bmb = lanes(s.sb, "bm_b", [P, 2, L])
        xz, og = lanes(s.sb, "xz", [P, 2, L]), lanes(s.sb, "og", [P, 2, L])
        kw = lanes(s.sb, "kw", [P, 2, MK])
        cb, cf = lanes(s.sb, "state_b", [P, N, VW]), lanes(s.sb, "state_f", [P, 2, VW])
        D_, qe = lanes(s.sb, "D", [P, 2, P]), lanes(s.sb, "qe", [P, 2, P])
        sw, qs = lanes(s.sb, "sw", [P, 2, P]), lanes(s.sb, "qs", [P, 2, P])
        dn, rd = lanes(s.sb, "dn", [P, 2]), lanes(s.sb, "rd", [P, 2])
        hf, hs = lanes(s.sb, "hf", [P, MV]), lanes(s.sb, "hs", [P, NT, MV])
        ssq, rstd = lanes(s.sb, "ssq", [P, NT]), lanes(s.sb, "rstd", [P, NT])
        psum = s.ps("psum", 4096)
        R = [psum[:, 2048 * l:2048 * l + 2048] for l in LANES]
        kq = [R[l][:, 0:512] for l in LANES]
        hbank = [(R[l][:, 512:1024], R[l][:, 1024:1536]) for l in LANES]
        ub = [R[l][:, 1536:2048] for l in LANES]
        turned_at = [(R[l][:, 0:L], R[l][:, 7 * P:7 * P + L]) for l in LANES]
        once, ones_set = s.sem("once_loaded"), s.sem("ones_set")
        kvl = [lanes(s.sem, f"kv{b}_loaded") for b in range(2)]
        qkl = [lanes(s.sem, f"qk{b}_loaded") for b in range(2)]
        bml, xol = lanes(s.sem, "bm_loaded"), lanes(s.sem, "xz_o_loaded")
        kwd = lanes(s.flag, "kw_ready", per=2 * N)
        um = lanes(s.flag, "update_made", per=2 * N, credit=1)
        us = lanes(s.flag, "update_added", per=2 * N, credit=1)
        dd = lanes(s.flag, "D_ready", per=NT)
        de = lanes(s.flag, "D_exp_done", per=NT)
        qed = lanes(s.flag, "qe_done", per=NT)
        kqd = lanes(s.flag, "kq_done", per=NT)
        swd = lanes(s.flag, "sw_ready", per=NT, credit=1)
        qsd = lanes(s.flag, "qs_ready", per=NT, credit=1)
        hd = lanes(s.flag, "h_made", per=NT, credit=NT + 1)
        rdd = lanes(s.flag, "den_ready", per=NT)
        hfd = lanes(s.flag, "hf_done", per=NT)
        hsd = lanes(s.flag, "hs_done", per=NT, credit=1)
        sqd = lanes(s.flag, "squares_done", per=NT)
        root = lanes(s.flag, "root_done")
        hscaled = lanes(s.flag, "h_scaled")
        turned = lanes(s.flag, "h_turned", per=2)
        gated = lanes(s.flag, "gated", per=2, credit=1)
        stored = lanes(s.flag, "stored", per=16, credit=16)
        steps = s.sem("dve_steps")
        with nc.Block() as block:
            @block.sync
            def _(sp):
                sp.dma_start(masks[:, :, :], a["masks"]).then_inc(once, 16)
                for r in range(2):
                    sp.dma_start(endb[:, r, :, :, :].rearrange("p h e t -> p (h e t)"),
                                 d["ends"][r].rearrange("h e t -> (h e t)").unsqueeze(0)
                                 .broadcast_to([P, MH * 2 * NT])).then_inc(once, 16)
                sp.wait_ge(ones_set, 1)
                with sp.Fori(0, MH // 4) as i:
                    for b in range(2):
                        j = i * 2 + b
                        for l in LANES:
                            hd[l].wait(sp, j, -NT)
                            sp.dma_start(v1[b][l][:, :, 0:MV], d["v"][j * 2 + l]).then_inc(kvl[b][l], 16)
                            sp.dma_start(kt[b][l][:, :, :], d["kt"][j * 2 + l]).then_inc(kvl[b][l], 16)
                        for l in LANES:
                            sp.dma_start(qk[b][l][:, :, :],
                                         d["qk"][j * 2 + l].rearrange("n p t -> p n t")).then_inc(qkl[b][l], 16)
                        for l in LANES:
                            qsd[l].wait(sp, j, 0)
                            sp.dma_start(bmb[l][:, :, :], d["bm"][:, bass.ds(j * 2 + l, 1), :]
                                         .rearrange("r h t -> h r t").broadcast_to([P, 2, L])).then_inc(bml[l], 16)
                        for l in LANES:
                            stored[l].wait(sp, j, 0)
                            heads = bass.ds((j * 2 + l) * 2, 2)
                            sp.dma_start(xz[l][:, :, :],
                                         d["xz"][heads, :, :].rearrange("b p t -> p b t")).then_inc(xol[l], 16)
                            sp.dma_start(og[l][:, :, :],
                                         d["o"][heads, :, :].rearrange("b p t -> p b t")).then_inc(xol[l], 16)

            @block.tensor
            def _(pe):
                for l in LANES:
                    hd[l].start(pe)
                    um[l].start(pe)
                with pe.Fori(0, MH // 4) as i:
                    for b in range(2):
                        j = i * 2 + b

                        def update(l, n, t):
                            off, m = TILES[t]
                            kwd[l].wait(pe, j, n + 1)
                            us[l].wait(pe, j, n)
                            nc.tensor.matmul(ub[l][:, 0:VW], kw[l][0:m, n % 2, :], v1[b][l][0:m, t, :],
                                             start=True, stop=True).then_inc(um[l].sem, 1)

                        def scores(l, t):
                            off, m = TILES[t]
                            swd[l].wait(pe, j, t)
                            nc.tensor.matmul(kq[l][0:m, 0:m], qk[b][l][:, 1, off:off + m],
                                             qk[b][l][:, 0, off:off + m],
                                             start=True, stop=True).then_inc(kqd[l].sem, 1)

                        for n, t in enumerate(range(N, 0, -1)):
                            for l in LANES:
                                if n == 0:
                                    pe.wait_ge(kvl[b][l], i * 32 + 32)
                                    gated[l].wait(pe, j, 0)
                                update(l, n, t)
                        for l in LANES:
                            pe.wait_ge(qkl[b][l], i * 16 + 16)
                            scores(l, 0)
                        for t, (off, m) in enumerate(TILES):
                            for l in LANES:
                                if t < N:
                                    update(l, N + t, t)
                                    scores(l, t + 1)
                                swd[l].wait(pe, j, t + 1)
                                qsd[l].wait(pe, j, t + 1)
                                hsd[l].wait(pe, j, t)
                                if t:
                                    us[l].wait(pe, j, N + t)
                                for r, bank in enumerate(hbank[l]):
                                    state = cf[l][:, t % 2, :] if r == 0 else cb[l][:, min(t, N - 1), :]
                                    has = t > 0 if r == 0 else t < N
                                    if has:
                                        nc.tensor.matmul(bank[0:m, 0:VW], qs[l][:, r, 0:m], state,
                                                         start=True, stop=False)
                                    last = nc.tensor.matmul(bank[0:m, 0:VW], sw[l][0:m, r, 0:m],
                                                            v1[b][l][0:m, t, :], start=not has, stop=True)
                                last.then_inc(hd[l].sem, 1)
                        for f in range(2):
                            for l in LANES:
                                if f == 0:
                                    hscaled[l].wait(pe, j, 1)
                                else:
                                    gated[l].wait(pe, j, 1)
                                for t, (off, m) in enumerate(TILES):
                                    last = nc.tensor.transpose(turned_at[l][f][:, off:off + m],
                                                               hs[l][0:m, t, f * P:(f + 1) * P],
                                                               c["ident"][0:m, 0:m])
                                last.then_inc(turned[l].sem, 1)

            @block.scalar
            def _(act):
                for l in LANES:
                    stored[l].start(act)
                act.wait_ge(once, 48)
                with act.Fori(0, MH // 4) as i:
                    for b in range(2):
                        j = i * 2 + b

                        def weights_of(l, t):
                            off, m = TILES[t]
                            qsd[l].wait(act, j, t)
                            for r in range(2):
                                last = nc.scalar.activation(
                                    qe[l][:, r, 0:m], bmb[l][:, r, off:off + m], ACT.Exp,
                                    bias=endb[:, r, bass.ds(j * 2 + l, 1), 0, t:t + 1].rearrange("p h t -> p (h t)"))
                            last.then_inc(qed[l].sem, 1)

                        def exp(l, t):
                            m = TILES[t][1]
                            dd[l].wait(act, j, t + 1)
                            nc.scalar.activation(D_[l][0:m, :, 0:m], D_[l][0:m, :, 0:m], ACT.Exp).then_inc(de[l].sem, 1)

                        def weigh(l, n, t, r):
                            m = TILES[t][1]
                            um[l].wait(act, j, max(n - 1, 0))
                            nc.scalar.activation(kw[l][0:m, n % 2, :], kt[b][l][0:m, t, :], ACT.Copy,
                                                 scale=cols[0:m, t, WS, bass.ds(j * 2 + (l + 32 * r), 1)]
                                                 ).then_inc(kwd[l].sem, 1)
                        for l in LANES:
                            act.wait_ge(kvl[b][l], i * 32 + 32)
                        for n, t in enumerate(range(N, 0, -1)):
                            for l in LANES:
                                weigh(l, n, t, 1)
                        for l in LANES:
                            weigh(l, N, 0, 0)
                            act.wait_ge(bml[l], j * 16 + 16)
                            weights_of(l, 0)
                            exp(l, 0)
                        for t in range(NT + 1):
                            for l in LANES:
                                if t:
                                    m = TILES[t - 1][1]
                                    rdd[l].wait(act, j, t)
                                    nc.scalar.activation(hf[l][0:m, :], hbank[l][0][0:m, 0:MV], ACT.Copy,
                                                         scale=rd[l][0:m, 0:1]).then_inc(hfd[l].sem, 1)
                                if t < N:
                                    weights_of(l, t + 1)
                                    if t + 1 < N:
                                        weigh(l, N + t + 1, t + 1, 0)
                                if t:
                                    hsd[l].wait(act, j, t)
                                    nc.scalar.activation(hf[l][0:m, :], hs[l][0:m, t - 1, :], ACT.Square,
                                                         accum_out=ssq[l][0:m, t - 1:t]).then_inc(sqd[l].sem, 1)
                                if t < N:
                                    exp(l, t + 1)
                        for l in LANES:
                            sqd[l].wait(act, j, NT)
                            nc.scalar.activation(rstd[l][:, :], ssq[l][:, :], ACT.Sqrt, bias=c["eps"][:, :],
                                                 scale=1.0 / MV).then_inc(root[l].sem, 1)
                        for l in LANES:
                            gated[l].wait(act, j, 2)
                            act.dma_start(d["hh"][bass.ds((j * 2 + l) * 2, 2), :, :].rearrange("b p t -> p b t"),
                                          og[l][:, :, :]).then_inc(stored[l].sem, 16)
                for l in LANES:
                    stored[l].wait(act, MH // 2, 0)

            @block.gpsimd
            def _(gp):
                for l in LANES:
                    qsd[l].start(gp)
                with gp.Fori(0, MH // 4) as i:
                    for b in range(2):
                        j = i * 2 + b
                        for l in LANES:
                            gp.wait_ge(qkl[b][l], i * 16 + 16)
                        for t, (off, m) in enumerate(TILES):
                            for l in LANES:
                                qed[l].wait(gp, j, t + 1)
                                hd[l].wait(gp, j, t)
                                nc.gpsimd.tensor_tensor(
                                    qs[l][:, :, 0:m], qe[l][:, :, 0:m],
                                    qk[b][l][:, 0, off:off + m].unsqueeze(1).broadcast_to([P, 2, m]),
                                    ALU.mult).then_inc(qsd[l].sem, 1)

            @block.vector
            def _(dve):
                v = nc.vector
                do = Steps(dve, steps)
                for l in LANES:
                    for flag in (us[l], swd[l], hsd[l], gated[l]):
                        flag.start(dve)
                    v.memset(ssq[l][:, :], 0.0)
                    for b in range(2):
                        ins = v.memset(v1[b][l][:, :, MV:VW], 1.0)
                ins.then_inc(ones_set, 1)
                dve.wait_ge(once, 48)
                with do.loop(MH // 4, 2 * 2 * LANE_STEPS) as i:
                    for b in range(2):
                        j = i * 2 + b

                        def col(l, t, q, r, m):
                            return cols[0:m, t, q, bass.ds(j * 2 + (l + 32 * r), 1)]

                        def decay(l, t, r):
                            return endb[:, r, bass.ds(j * 2 + l, 1), 1, t:t + 1].rearrange("p h t -> p (h t)")

                        def exponent(l, t):
                            off, m = TILES[t]
                            for r in range(2):
                                last = v.scalar_tensor_tensor(D_[l][0:m, r, 0:m], bmb[l][0:m, r, off:off + m],
                                                              col(l, t, LS, r, m), masks[0:m, r, 0:m],
                                                              ALU.add, ALU.add)
                            last.then_inc(dd[l].sem, 1)

                        def add(l, n, dst, src, t, r):
                            um[l].wait(dve, j, n + 1)
                            if src is None:
                                do(v.tensor_copy(dst, ub[l][:, 0:VW]))
                            else:
                                do(v.scalar_tensor_tensor(dst, src, decay(l, t, r), ub[l][:, 0:VW],
                                                          ALU.mult, ALU.add))
                            dve.sem_inc(us[l].sem, 1)

                        for n, t in enumerate(range(N, 0, -1)):
                            for l in LANES:
                                add(l, n, cb[l][:, t - 1, :], None if t == N else cb[l][:, t, :], t, 1)
                        for l in LANES:
                            dve.wait_ge(bml[l], j * 16 + 16)
                            exponent(l, 0)
                        for t in range(NT + 1):
                            for l in LANES:
                                if t:
                                    p, mp = t - 1, TILES[t - 1][1]
                                    hd[l].wait(dve, j, t)
                                    den = R[l][0:mp, 512:1536].rearrange("p (r n) -> p r n", r=2)[:, :, MV:VW]
                                    floor = cols[0:mp, p, FLOOR, :].rearrange("p (r h) -> p r h", r=2)[
                                        :, :, bass.ds(j * 2 + l, 1)]
                                    both = dn[l][0:mp, :].unsqueeze(2)
                                    do(v.scalar_tensor_tensor(both, den, -1.0, floor, ALU.mult, ALU.max))
                                    do(v.tensor_tensor(both, den, both, ALU.max))
                                    do(v.reciprocal(rd[l][0:mp, :], dn[l][0:mp, :]))
                                    dve.sem_inc(rdd[l].sem, 1)
                                if t < NT:
                                    off, m = TILES[t]
                                    de[l].wait(dve, j, t + 1)
                                    kqd[l].wait(dve, j, t + 1)
                                    do(v.tensor_tensor(sw[l][0:m, :, 0:m], D_[l][0:m, :, 0:m],
                                                       kq[l][0:m, 0:m].unsqueeze(1).broadcast_to([m, 2, m]),
                                                       ALU.mult))
                                    dve.sem_inc(swd[l].sem, 1)
                                if t < N:
                                    exponent(l, t + 1)
                                if t:
                                    hfd[l].wait(dve, j, t)
                                    v.scalar_tensor_tensor(hs[l][0:mp, p, :], hbank[l][1][0:mp, 0:MV],
                                                           rd[l][0:mp, 1:2], hf[l][0:mp, :],
                                                           ALU.mult, ALU.add).then_inc(hsd[l].sem, 1)
                                if t < N:
                                    add(l, N + t, cf[l][:, (t + 1) % 2, :], None if t == 0 else cf[l][:, t % 2, :],
                                        t, 0)
                        for l in LANES:
                            root[l].wait(dve, j, 1)
                            do(v.reciprocal(rstd[l][:, :], rstd[l][:, :]))
                            for t, (off, m) in enumerate(TILES):
                                ins = v.tensor_scalar(hs[l][0:m, t, :], hs[l][0:m, t, :], rstd[l][0:m, t:t + 1],
                                                      None, ALU.mult)
                                do(ins) if t == N else do.free(ins)
                            dve.sem_inc(hscaled[l].sem, 1)
                        for f in range(2):
                            for l in LANES:
                                if f == 0:
                                    dve.wait_ge(xol[l], j * 32 + 32)
                                turned[l].wait(dve, j, f + 1)
                                feature = (j * 2 + l) * 2 + f
                                do(v.scalar_tensor_tensor(og[l][:, f, :], turned_at[l][f],
                                                          c["cols_a"][:, bass.ds(feature + c["head_norm"], 1)],
                                                          og[l][:, f, :], ALU.mult, ALU.mult))
                                v.scalar_tensor_tensor(og[l][:, f, :], xz[l][:, f, :],
                                                       c["cols_a"][:, bass.ds(feature + c["mlstm_skip"], 1)],
                                                       og[l][:, f, :], ALU.mult, ALU.add).then_inc(gated[l].sem, 1)


LANE_STEPS = 2 * (NT - 1) + 4 * NT + 1 + NT + 2


def rope_tables():
    n = L - META
    pos = np.zeros((2, L), np.float32)
    pos[0, META:] = np.repeat(np.arange(n // GRID_W, dtype=np.float32), GRID_W)
    pos[1, META:] = np.tile(np.arange(GRID_W, dtype=np.float32), n // GRID_W)
    axis = HD // 2
    freqs = (np.float32(10000.0) ** (-np.arange(0, axis, 2, dtype=np.float32) / np.float32(axis))).astype(np.float32)
    angle = np.stack([pos[f // axis] * freqs[f % (axis // 2)] for f in range(HD)])
    return np.stack([np.cos(angle), np.sin(angle)], axis=1).astype(np.float32)


def rope_swap():
    swap = np.zeros((HD, HD), np.float32)
    half = HD // 4
    for f in range(HD):
        first = f % (2 * half) < half
        swap[f + half if first else f - half, f] = -1.0 if first else 1.0
    return swap


def before_masks():
    s, t = np.arange(P)[:, None], np.arange(P)[None, :]
    return np.stack([np.where(s <= t, 0.0, -1e30), np.where(s >= t, 0.0, -1e30)], axis=1).astype(np.float32)


def scan_starts():
    keep = np.ones((40, L), np.float32)
    keep[0:32, [o for o, _ in TILES]] = 0.0
    keep[32:40, [L - o - n for o, n in TILES]] = 0.0
    return keep


_INS = ["x", "meta_tokens", "norm_pre", "norm_post", "w_in_even", "q_norm", "k_norm", "ssm_a_re", "ssm_a_im",
        "ssm_log_dt", "ssm_b_re", "ssm_b_im", "ssm_c_re", "ssm_c_im", "ssm_d", "w_glu", "b_glu", "w_out_even",
        "w_in_odd", "conv_w", "conv_b", "w_q", "w_k", "w_v", "w_igate", "b_igate", "w_fgate", "b_fgate",
        "w_ogate", "b_ogate", "head_norm", "mlstm_skip", "w_out_odd"]
_FLAT = ("norm_pre", "norm_post")


def kernel(**inputs):
    import concourse.bacc as bacc
    from concourse.bass_utils import run_bass_kernel_spmd
    nc = bacc.Bacc("TRN2", target_bir_lowering=False, num_devices=1)
    arrays = {}
    for name in _INS:
        v = np.asarray(inputs[name])
        if name in _FLAT:
            v = v.reshape(-1)
        elif name != "meta_tokens":
            v = v[0]
        arrays[name] = np.ascontiguousarray(v)
    arrays["ident"] = np.eye(P, dtype=np.float32)
    arrays["rope"] = rope_tables()
    arrays["swap"] = rope_swap()
    arrays["masks"] = before_masks()
    arrays["starts"] = scan_starts()
    a = {n: nc.dram_tensor(f"in_{n}", v.shape, mybir.dt.from_np(v.dtype), kind="ExternalInput").ap()
         for n, v in arrays.items()}
    out = nc.dram_tensor("out", (L - META, D), F32, kind="ExternalOutput").ap()
    trunk(nc, a, out)
    result = run_bass_kernel_spmd(nc, [{f"in_{n}": v for n, v in arrays.items()}], core_ids=[0])
    return result.results[0]["out"][None]
```
